# Optimizing a Trainium2 kernel written in Bass

```python
import math
import jax
import jax.numpy as jnp
from jax import lax
import numpy as np

D_MODEL = 1024
BATCH = 1
SEQ = 256
DEPTH = 2

MEM_LEN = 256
EPS = 1e-6

N_A = DEPTH // 2
N_B = DEPTH - N_A

SSM_EXPAND = 2
D_INNER = SSM_EXPAND * D_MODEL
SSM_HEADDIM = 64
SSM_HEADS = D_INNER // SSM_HEADDIM
SSM_GROUPS = 4
SSM_HPG = SSM_HEADS // SSM_GROUPS
D_STATE = 128
D_CONV = 4
SSD_CHUNK = 256
CONV_DIM = D_INNER + 2 * SSM_GROUPS * D_STATE
IN_PROJ_DIM = D_INNER + CONV_DIM + SSM_HEADS

ATT_HEADS = 16
ATT_HEADDIM = D_MODEL // ATT_HEADS
MOBA_BLOCK = 256
MOBA_TOPK = 3
Q_CHUNK = 64

REL_BUCKETS = 32
REL_MAX_DIST = 128

MEM_HEADS = 4
MEM_HEADDIM = D_MODEL // MEM_HEADS

D_FF = -(-8 * D_MODEL // (3 * 256)) * 256

SEQ_ALIGN = 256

kernel_name = 'yoco_ssd_moba_hybrid'

def rmsnorm(x, g):
    x32 = x.astype(jnp.float32)
    y = x32 * lax.rsqrt(jnp.mean(x32 * x32, axis=-1, keepdims=True) + EPS)
    return (y * g.astype(jnp.float32)).astype(x.dtype)

def grouped_rmsnorm(y, g):
    b, l, d = y.shape
    y = y.reshape(b, l, SSM_GROUPS, d // SSM_GROUPS)
    y = y * lax.rsqrt(jnp.mean(y * y, axis=-1, keepdims=True) + EPS)
    return y.reshape(b, l, d) * g.astype(jnp.float32)

def ssd_chunked(x, dt, a, bm, cm):
    b, l = x.shape[:2]
    nc = l // SSD_CHUNK
    x = x.astype(jnp.float32).reshape(b, nc, SSD_CHUNK, SSM_GROUPS, SSM_HPG, SSM_HEADDIM)
    dt = dt.reshape(b, nc, SSD_CHUNK, SSM_GROUPS, SSM_HPG)
    bm = bm.astype(jnp.float32).reshape(b, nc, SSD_CHUNK, SSM_GROUPS, D_STATE)
    cm = cm.astype(jnp.float32).reshape(b, nc, SSD_CHUNK, SSM_GROUPS, D_STATE)
    a_dt = jnp.moveaxis(dt * a, 2, -1)
    a_cum = jnp.cumsum(a_dt, axis=-1)
    xdt = x * dt[..., None]
    idx = jnp.arange(SSD_CHUNK)
    causal = idx[:, None] >= idx[None, :]
    seg = a_cum[..., :, None] - a_cum[..., None, :]
    decay = jnp.exp(jnp.where(causal, seg, -jnp.inf))
    cb = jnp.einsum('bclgn,bcsgn->bcgls', cm, bm)
    y_diag = jnp.einsum('bcgls,bcgels,bcsgep->bclgep', cb, decay, xdt)
    decay_states = jnp.exp(a_cum[..., -1:] - a_cum)
    states = jnp.einsum('bclgn,bcgel,bclgep->bcgepn', bm, decay_states, xdt)
    chunk_decay = jnp.exp(a_cum[..., -1])

    def step(h, inp):
        s_c, d_c = inp
        return h * d_c[..., None, None] + s_c, h

    h0 = jnp.zeros((b, SSM_GROUPS, SSM_HPG, SSM_HEADDIM, D_STATE), jnp.float32)
    _, prev = lax.scan(step, h0, (jnp.moveaxis(states, 1, 0), jnp.moveaxis(chunk_decay, 1, 0)))
    prev = jnp.moveaxis(prev, 0, 1)
    y_off = jnp.einsum('bclgn,bcgepn,bcgel->bclgep', cm, prev, jnp.exp(a_cum))
    return (y_diag + y_off).reshape(b, l, SSM_GROUPS, SSM_HPG, SSM_HEADDIM)

def mamba2_mixer(u, w_in, conv_w, conv_b, dt_bias, a_log, d_skip, norm_g, w_out):
    b, l, _ = u.shape
    zxbcdt = u @ w_in
    z, xbc, dt = jnp.split(zxbcdt, [D_INNER, D_INNER + CONV_DIM], axis=-1)
    xbc = lax.conv_general_dilated(
        xbc, conv_w[:, None, :].astype(xbc.dtype), window_strides=(1,),
        padding=[(D_CONV - 1, 0)], dimension_numbers=('NWC', 'WIO', 'NWC'),
        feature_group_count=CONV_DIM)
    xbc = jax.nn.silu(xbc + conv_b)
    xs, bm, cm = jnp.split(xbc, [D_INNER, D_INNER + SSM_GROUPS * D_STATE], axis=-1)
    dt = jax.nn.softplus(dt.astype(jnp.float32) + dt_bias.astype(jnp.float32))
    a = -jnp.exp(a_log.astype(jnp.float32))
    xs = xs.reshape(b, l, SSM_GROUPS, SSM_HPG, SSM_HEADDIM)
    y = ssd_chunked(xs, dt.reshape(b, l, SSM_GROUPS, SSM_HPG), a.reshape(SSM_GROUPS, SSM_HPG),
                    bm.reshape(b, l, SSM_GROUPS, D_STATE), cm.reshape(b, l, SSM_GROUPS, D_STATE))
    y = y + d_skip.astype(jnp.float32).reshape(SSM_GROUPS, SSM_HPG, 1) * xs.astype(jnp.float32)
    y = y.reshape(b, l, D_INNER) * jax.nn.silu(z.astype(jnp.float32))
    y = grouped_rmsnorm(y, norm_g)
    return y.astype(u.dtype) @ w_out

def t5_bucket(rel):
    n = jnp.maximum(rel, 0)
    max_exact = REL_BUCKETS // 2
    n32 = jnp.maximum(n, max_exact).astype(jnp.float32)
    large = max_exact + (jnp.log(n32 / max_exact) / math.log(REL_MAX_DIST / max_exact)
                         * (REL_BUCKETS - max_exact)).astype(jnp.int32)
    large = jnp.minimum(large, REL_BUCKETS - 1)
    return jnp.where(n < max_exact, n, large)

def shared_kv(x, g, w_kv):
    b, t, _ = x.shape
    kv = rmsnorm(x, g) @ w_kv
    k, v = jnp.split(kv, 2, axis=-1)
    k = k.reshape(b, t, ATT_HEADS, ATT_HEADDIM).transpose(0, 2, 1, 3)
    v = v.reshape(b, t, ATT_HEADS, ATT_HEADDIM).transpose(0, 2, 1, 3)
    kmean = k.astype(jnp.float32).reshape(b, ATT_HEADS, t // MOBA_BLOCK, MOBA_BLOCK, ATT_HEADDIM).mean(axis=3)
    return k, v, kmean

def moba_attention(q, k, v, kmean, rel_bias):
    b, h, t, d = q.shape
    nb = t // MOBA_BLOCK
    topk = min(MOBA_TOPK, nb)
    scale = d ** -0.5
    kb = k.reshape(b, h, nb, MOBA_BLOCK, d)
    vb = v.reshape(b, h, nb, MOBA_BLOCK, d)
    bi = jnp.arange(b)[:, None, None, None]
    hi = jnp.arange(h)[None, :, None, None]
    bias_t = rel_bias.astype(jnp.float32).T
    offs = jnp.arange(MOBA_BLOCK)

    def chunk_fn(ci):
        start = ci * Q_CHUNK
        blk = start // MOBA_BLOCK
        qc = lax.dynamic_slice_in_dim(q, start, Q_CHUNK, axis=2)
        q_pos = start + jnp.arange(Q_CHUNK)
        gate = jnp.einsum('bhqd,bhjd->bhqj', qc.astype(jnp.float32), kmean)
        gate = jnp.where(jnp.arange(nb) < blk, gate, -jnp.inf)
        _, sel = lax.top_k(gate, topk)
        valid = sel < blk
        k_sel = kb[bi, hi, sel]
        v_sel = vb[bi, hi, sel]
        s_sel = jnp.einsum('bhqd,bhqksd->bhqks', qc, k_sel).astype(jnp.float32) * scale
        rel_sel = q_pos[None, None, :, None, None] - (sel[..., None] * MOBA_BLOCK + offs)
        s_sel = jnp.where(valid[..., None], s_sel + bias_t[hi[..., None], t5_bucket(rel_sel)], -jnp.inf)
        k_own = lax.dynamic_slice_in_dim(k, blk * MOBA_BLOCK, MOBA_BLOCK, axis=2)
        v_own = lax.dynamic_slice_in_dim(v, blk * MOBA_BLOCK, MOBA_BLOCK, axis=2)
        rel_own = q_pos[:, None] - (blk * MOBA_BLOCK + offs)[None, :]
        s_own = jnp.einsum('bhqd,bhsd->bhqs', qc, k_own).astype(jnp.float32) * scale
        s_own = jnp.where(rel_own >= 0, s_own + bias_t[:, t5_bucket(rel_own)], -jnp.inf)
        logits = jnp.concatenate([s_sel.reshape(b, h, Q_CHUNK, topk * MOBA_BLOCK), s_own], axis=-1)
        p = jax.nn.softmax(logits, axis=-1).astype(v.dtype)
        p_sel = p[..., :topk * MOBA_BLOCK].reshape(b, h, Q_CHUNK, topk, MOBA_BLOCK)
        p_own = p[..., topk * MOBA_BLOCK:]
        return (jnp.einsum('bhqks,bhqksd->bhqd', p_sel, v_sel)
                + jnp.einsum('bhqs,bhsd->bhqd', p_own, v_own))

    out = lax.map(chunk_fn, jnp.arange(t // Q_CHUNK))
    return out.transpose(1, 2, 0, 3, 4).reshape(b, h, t, d)

def memory_cross_attention(u, mem_n, w_q, w_kv, w_o):
    b, t, _ = u.shape
    m = mem_n.shape[1]
    q = (u @ w_q).reshape(b, t, MEM_HEADS, MEM_HEADDIM)
    k, v = jnp.split(mem_n @ w_kv, 2, axis=-1)
    k = k.reshape(b, m, MEM_HEADS, MEM_HEADDIM)
    v = v.reshape(b, m, MEM_HEADS, MEM_HEADDIM)
    logits = jnp.einsum('bthd,bmhd->bhtm', q, k).astype(jnp.float32) * (MEM_HEADDIM ** -0.5)
    p = jax.nn.softmax(logits, axis=-1).astype(v.dtype)
    o = jnp.einsum('bhtm,bmhd->bthd', p, v).reshape(b, t, D_MODEL)
    return o @ w_o

def swiglu(u, w_gu, w_down):
    gate, up = jnp.split(u @ w_gu, 2, axis=-1)
    return (jax.nn.silu(gate) * up) @ w_down

def setup_inputs(seed: int = 0) -> dict:
    key = jax.random.key(seed)
    ks = jax.random.split(key, 32)
    f32 = jnp.float32
    D = D_MODEL

    def nrm(k, shape, fan_in):
        return jax.random.normal(k, shape, f32) * (fan_in ** -0.5)

    def gain(k, shape):
        return 1.0 + 0.05 * jax.random.normal(k, shape, f32)

    dt0 = jnp.exp(jax.random.uniform(ks[7], (N_A, SSM_HEADS), f32)
                  * (math.log(0.1) - math.log(0.001)) + math.log(0.001))
    dt0 = jnp.maximum(dt0, 1e-4)
    return {
        'x': jax.random.normal(ks[0], (BATCH, SEQ, D), f32),
        'mem': jax.random.normal(ks[1], (BATCH, MEM_LEN, D), f32),
        'mix_pre_g': gain(ks[2], (DEPTH, D)),
        'mix_post_g': gain(ks[3], (DEPTH, D)),
        'ssm_w_in': nrm(ks[4], (N_A, D, IN_PROJ_DIM), D),
        'ssm_conv_w': nrm(ks[5], (N_A, D_CONV, CONV_DIM), D_CONV),
        'ssm_conv_b': 0.01 * jax.random.normal(ks[6], (N_A, CONV_DIM), f32),
        'ssm_dt_bias': dt0 + jnp.log(-jnp.expm1(-dt0)),
        'ssm_a_log': jnp.log(jax.random.uniform(ks[8], (N_A, SSM_HEADS), f32, 1.0, 16.0)),
        'ssm_d': gain(ks[9], (N_A, SSM_HEADS)),
        'ssm_norm_g': gain(ks[10], (N_A, D_INNER)),
        'ssm_w_out': nrm(ks[11], (N_A, D_INNER, D), D_INNER),
        'kv_norm_g': gain(ks[12], (D,)),
        'w_kv': nrm(ks[13], (D, 2 * D), D),
        'moba_w_q': nrm(ks[14], (N_B, D, D), D),
        'moba_w_o': nrm(ks[15], (N_B, D, D), D),
        'rel_bias': 0.5 * jax.random.normal(ks[16], (REL_BUCKETS, ATT_HEADS), f32),
        'mem_norm_g': gain(ks[17], (D,)),
        'mem_pre_g': gain(ks[18], (DEPTH, D)),
        'mem_post_g': gain(ks[19], (DEPTH, D)),
        'mem_w_q': nrm(ks[20], (DEPTH, D, D), D),
        'mem_w_kv': nrm(ks[21], (DEPTH, D, 2 * D), D),
        'mem_w_o': nrm(ks[22], (DEPTH, D, D), D),
        'ffn_pre_g': gain(ks[23], (DEPTH, D)),
        'ffn_post_g': gain(ks[24], (DEPTH, D)),
        'ffn_w_gu': nrm(ks[25], (DEPTH, D, 2 * D_FF), D),
        'ffn_w_down': nrm(ks[26], (DEPTH, D_FF, D), D_FF),
    }

def reference(x, mem, mix_pre_g, mix_post_g, ssm_w_in, ssm_conv_w, ssm_conv_b, ssm_dt_bias,
              ssm_a_log, ssm_d, ssm_norm_g, ssm_w_out, kv_norm_g, w_kv, moba_w_q, moba_w_o,
              rel_bias, mem_norm_g, mem_pre_g, mem_post_g, mem_w_q, mem_w_kv, mem_w_o,
              ffn_pre_g, ffn_post_g, ffn_w_gu, ffn_w_down):
    b, t, _ = x.shape
    t_pad = -(-t // SEQ_ALIGN) * SEQ_ALIGN
    x = jnp.pad(x, ((0, 0), (0, t_pad - t), (0, 0)))
    mem_n = rmsnorm(mem, mem_norm_g)
    k_sh = v_sh = kmean_sh = None
    for i in range(DEPTH):
        u = rmsnorm(x, mix_pre_g[i])
        if i < N_A:
            j = i
            h = mamba2_mixer(u, ssm_w_in[j], ssm_conv_w[j], ssm_conv_b[j], ssm_dt_bias[j],
                             ssm_a_log[j], ssm_d[j], ssm_norm_g[j], ssm_w_out[j])
        else:
            j = i - N_A
            if j == 0:
                k_sh, v_sh, kmean_sh = shared_kv(x, kv_norm_g, w_kv)
            q = (u @ moba_w_q[j]).reshape(b, t_pad, ATT_HEADS, ATT_HEADDIM).transpose(0, 2, 1, 3)
            o = moba_attention(q, k_sh, v_sh, kmean_sh, rel_bias)
            h = o.transpose(0, 2, 1, 3).reshape(b, t_pad, D_MODEL) @ moba_w_o[j]
        x = x + rmsnorm(h, mix_post_g[i])
        u = rmsnorm(x, mem_pre_g[i])
        x = x + rmsnorm(memory_cross_attention(u, mem_n, mem_w_q[i], mem_w_kv[i], mem_w_o[i]), mem_post_g[i])
        u = rmsnorm(x, ffn_pre_g[i])
        x = x + rmsnorm(swiglu(u, ffn_w_gu[i], ffn_w_down[i]), ffn_post_g[i])
    return x[:, :t]


_drawn_inputs = setup_inputs


def setup_inputs(seed=0):
    import zlib

    import numpy as np

    out = dict(_drawn_inputs(seed))
    spreads = {}
    factors = {'ssm_conv_b': 4.614}
    for name, (base, spread) in spreads.items():
        noise = np.random.default_rng([zlib.crc32(name.encode()), seed]).standard_normal(out[name].shape)
        drawn = base * np.exp(spread * noise) if base else spread * noise
        out[name] = jnp.asarray(drawn.astype(out[name].dtype))
    for name, factor in factors.items():
        out[name] = (out[name] * factor).astype(out[name].dtype)
    return out
```

```python
import math
from contextlib import ExitStack

import concourse.bass as bass
from concourse import mybir

F32, F32R, BF16 = mybir.dt.float32, mybir.dt.float32r, mybir.dt.bfloat16
ALU = mybir.AluOpType
ACT = mybir.ActivationFunctionType
AX = mybir.AxisListType

P = 128
D = 1024
S = 256
ST = S // P
KD = D // P
EPS = 1e-6
DI = 2 * D
SSM_HEADS, SSM_GROUPS, NSTATE, HD = 32, 4, 128, 64
XT = DI // P
CONV = DI + 2 * SSM_GROUPS * NSTATE
CT = CONV // P
GT = XT // SSM_GROUPS
TAPS = 4
DFF = 2816
FT = DFF // P
AH = 16
MH = 4
BUCKETS, MAX_DIST = 32, 128
SLOTS = 4
UNIT = 2048
TC = UNIT // KD
MR = UNIT // D
NEG = -1e30
G_ROW, D_ROW = 32, 64
CAUS = P + S

C_ID, C_TRI, C_CAUS, C_HOT, C_END = 0, P, P + S, 2 * P + S, 2 * P + 2 * S

ORDER = [
    ("xbc", "T", CONV // TC), ("z", "T", DI // TC),
    ("k0", "T", 4), ("v0", "V", 4),
    ("w_out", "M", DI // P // MR),
    ("q0", "T", 4), ("wo0", "M", 4),
    ("gu0", "T", 2 * DFF // TC), ("down0", "M", FT // MR),
    ("mq", "T", 4), ("mk", "T", 4), ("mv", "V", 4), ("mo", "M", 4),
    ("k1", "T", 4), ("v1", "V", 4),
    ("q1", "T", 4), ("wo1", "M", 4),
    ("gu1", "T", 2 * DFF // TC), ("down1", "M", FT // MR),
]
PIECES = [
    ("xbc", 0, 12), ("z", 0, 8), ("k0", 0, 4), ("v0", 0, 2), ("w_out", 0, 8), ("v0", 2, 2),
    ("q0", 0, 4), ("wo0", 0, 4), ("k1", 0, 2), ("gu0", 0, 22), ("down0", 0, 11), ("k1", 2, 2),
    ("mq", 0, 4), ("v1", 0, 1), ("mk", 0, 4), ("mv", 0, 4), ("v1", 1, 1), ("mo", 0, 4), ("v1", 2, 2),
    ("q1", 0, 4), ("wo1", 0, 4), ("gu1", 0, 22), ("down1", 0, 11),
]
KIND = {name: kind for name, kind, _ in ORDER}
U = {}
NAME_OF = []
for _name, _first, _count in PIECES:
    for _i in range(_first, _first + _count):
        U[(_name, _i)] = len(NAME_OF)
        NAME_OF.append((_name, _i))
NUNITS = len(NAME_OF)


def freed_by(name, i):
    if name == "params" or name == "xbc":
        return "dve"
    if name in ("gu0", "gu1"):
        return "dve" if i % 2 else "act"
    return "act"


BANKED = [("params", 0), ("dt", 0)] + [n for n in NAME_OF if KIND[n[0]] != "M"]
V_OF = {n: v for v, n in enumerate(BANKED)}
FREED = []
_n = {"act": 0, "dve": 0}
for _name, _i in BANKED:
    _e = freed_by(_name, _i)
    _n[_e] += 1
    FREED.append((_e, _n[_e]))


def reversed_last(ap):
    dims = [list(d) for d in ap.ap]
    step, n = dims[-1]
    dims[-1] = [-step, n]
    return bass.AP(ap.tensor, ap.offset + step * (n - 1), dims)


def program(nc, A, out):
    bias_rows = nc.dram_tensor("bias_rows", [AH, 3 * P], F32).ap()

    def row_tiles(w, k0, k, c0, c):
        return w[k0 * P:(k0 + k) * P, c0:c0 + c].rearrange("(k p) n -> p k n", p=P)

    w_in = A["ssm_w_in"][0]

    def unit_source(name, i):
        if name == "xbc":
            return row_tiles(w_in, 0, KD, DI + i * TC, TC)
        if name == "z":
            return row_tiles(w_in, 0, KD, i * TC, TC)
        if name in ("k0", "k1"):
            return row_tiles(A["mem_w_kv"][int(name[1])], 0, KD, i * TC, TC)
        if name in ("v0", "v1"):
            return row_tiles(A["mem_w_kv"][int(name[1])], 0, KD, D + i * TC, TC)
        if name in ("q0", "q1"):
            return row_tiles(A["mem_w_q"][int(name[1])], 0, KD, i * TC, TC)
        if name in ("gu0", "gu1"):
            return row_tiles(A["ffn_w_gu"][int(name[2])], 0, KD, (i % 2) * DFF + (i // 2) * TC, TC)
        if name == "mq":
            return row_tiles(A["moba_w_q"][0], 0, KD, i * TC, TC)
        if name == "mk":
            return row_tiles(A["w_kv"], 0, KD, i * TC, TC)
        if name == "mv":
            return row_tiles(A["w_kv"], 0, KD, D + i * TC, TC)
        w = {"w_out": A["ssm_w_out"][0], "wo0": A["mem_w_o"][0], "wo1": A["mem_w_o"][1], "mo": A["moba_w_o"][0],
             "down0": A["ffn_w_down"][0], "down1": A["ffn_w_down"][1]}[name]
        return row_tiles(w, i * MR, MR, 0, D)

    with ExitStack() as ctx:
        at = [16512]

        def place(name, shape, dtype, offset=None):
            size = math.prod(shape[1:]) * (2 if dtype == BF16 else 4)
            where = at[0] if offset is None else offset
            if offset is None:
                at[0] += -(-size // 32) * 32
            return nc.alloc_sbuf_tensor_at(name, shape, dtype, offset=where)

        def sem(name):
            return ctx.enter_context(nc.semaphore(name))

        hi = place("w_hi", [P, SLOTS, UNIT], F32R)
        raw_at = at[0]
        raw = place("w_raw", [P, SLOTS, UNIT], F32)
        lo = place("w_lo", [P, SLOTS, UNIT], F32R, raw_at)
        x = place("x", [P, ST, D], F32)
        actT_hi = place("actT_hi", [P, KD, S], F32R)
        actT_lo = place("actT_lo", [P, KD, S], F32R)
        memT_hi = place("memT_hi", [P, KD, S], F32R)
        memT_lo = place("memT_lo", [P, KD, S], F32R)
        at_memK = at[0]
        memK = place("memK", [P, KD, S], F32)
        memV = place("memV", [P, ST, D], F32)
        post_row = place("post_row", [P, D], F32)
        pre_row = place("pre_row", [P, D], F32)
        ntmp = place("ntmp", [P, ST, D], F32)
        const = place("const", [P, C_HOT], F32)
        hot = place("hot", [BUCKETS, S], F32, at_memK + 2048)
        brows = place("brows", [AH, 3 * P], F32, at_memK)
        stats = place("stats", [P, 6, 32], F32)
        gT = place("gT", [P, XT], F32)
        dT = place("dT", [P, XT], F32)
        small = place("small", [P, 8], F32)
        eps_col, one_col = small[:, 0:1], small[:, 1:2]
        phase = at[0]
        PHASE = 49152
        at[0] += PHASE
        scratch = at[0]

        z = place("z", [P, XT, S], F32, phase)
        xbc = place("xbc", [P, CT, S], F32, phase + 16384)
        y_lo = place("y_lo", [P, XT, S], F32R, phase)
        y_hi = place("y_hi", [P, XT, S], F32R, phase + 16384)
        cw = place("cw", [P, TAPS * CT + CT], F32, phase + 40960)
        dtw = place("dtw", [P, KD, SSM_HEADS], F32, phase + 41472)
        dtw_hi = place("dtw_hi", [P, KD, SSM_HEADS], F32R, phase + 42496)
        dtw_lo = place("dtw_lo", [P, KD, SSM_HEADS], F32R, phase + 43520)
        par_rows = place("par_rows", [P, 2, P], F32, phase + 44544)
        d_pair = place("d_pair", [P, 2], F32, phase + 46080)
        dt_row = place("dt_row", [P, 2, SSM_HEADS], F32, phase + 46112)
        dtc = place("dtc", [P, 8, ST, SSM_HEADS], F32, phase + 46368)
        relb = place("relb", [BUCKETS, AH], F32, phase + 48416)
        mbias = place("mbias", [P, AH, CAUS], F32, phase)
        mqT = place("mqT", [P, KD, S], F32, phase + 24576)
        mkT = place("mkT", [P, KD, S], F32, phase + 32768)
        mV = place("mV", [P, ST, D], F32, phase + 40960)
        qT = place("qT", [P, KD, S], F32, phase)
        hT_hi = place("hT_hi", [P, FT, S], F32R, phase)
        hT_lo = place("hT_lo", [P, FT, S], F32R, phase + FT * S * 4)

        def shared(name, shape, dtype, offset):
            t = place(name, shape, dtype, scratch + offset)
            return t, offset + math.prod(shape[1:]) * (2 if dtype == BF16 else 4)

        conv_acc, o = shared("conv_acc", [P, 2, 2, S], F32, 0)
        xtok, o = shared("xtok", [P, 2, ST, P], F32, 0)
        decay, o = shared("decay", [P, 2, CAUS], F32, o)
        mt, o = shared("mt", [P, 4, CAUS], F32, o)
        cbT, o = shared("cbT", [P, 2, CAUS], F32, o)
        mask_bf, o = shared("mask_bf", [P, P], BF16, max(o, 4096))
        id_bf, o = shared("id_bf", [P, P], BF16, o)
        id_r, o = shared("id_r", [P, SSM_HEADS], F32R, o)
        cumT_hi, o = shared("cumT_hi", [P, S], F32R, o)
        cumT_lo, o = shared("cumT_lo", [P, S], F32R, o)
        ycum, o = shared("ycum", [P, 2, S], F32, o)
        rs, o = shared("rs", [P, 2, S], F32, o)
        end_ssd = o
        prob, o = shared("prob", [P, 2, ST, S], F32, 0)
        probT, o = shared("probT", [P, 2, ST, S], F32, o)
        mstat, o = shared("mstat", [P, 4, ST * MH], F32, o)
        sc, o2 = shared("sc", [P, 2, 2, CAUS], F32, 0)
        scT, o2 = shared("scT", [P, 2, 2, CAUS], F32, o2)
        bstat, o2 = shared("bstat", [P, 4, 4 * AH // 2], F32, o2)
        gate, o3 = shared("gate", [P, 2, 2, S], F32, 0)
        hval, o3 = shared("hval", [P, 2, 2, S], F32, o3)
        top = scratch + max(end_ssd, o, o2, o3)
        assert top <= 229368, top

        bank = ctx.enter_context(nc.psum_tensor("bank", [P, 8, 512], F32))
        msum = [bank[:, 4 + 2 * t:6 + 2 * t, :].rearrange("p b n -> p (b n)") for t in range(ST)]

        w_loaded = [sem(f"w_loaded{s}") for s in range(SLOTS)]
        w_hi_done = sem("w_hi_done")
        w_lo_done = sem("w_lo_done")
        w_used = sem("w_used")
        t_out = {"act": sem("t_out_act"), "dve": sem("t_out_dve")}
        act_step = sem("act_step")
        dve_step = sem("dve_step")
        x_loaded, mem_loaded = sem("x_loaded"), sem("mem_loaded")
        par_loaded, const_loaded, rows_loaded = sem("par_loaded"), sem("const_loaded"), sem("rows_loaded")
        pre_loaded, post_loaded = sem("pre_loaded"), sem("post_loaded")
        consts_made = sem("consts_made")
        eps_made = sem("eps_made")
        stat_ready = sem("stat_ready")
        x_ready = sem("x_ready")
        u_ready = sem("u_ready")
        turned = sem("turned")
        turn_hi, turn_lo = sem("turn_hi"), sem("turn_lo")
        par_cleared = sem("par_cleared")
        par_turned = sem("par_turned")
        dtw_hi_done, dtw_lo_done, dt_mm = sem("dtw_hi_done"), sem("dtw_lo_done"), sem("dt_mm")
        dt_biased, dt_logged = sem("dt_biased"), sem("dt_logged")
        dt_ready, cum_mm, cum_hi, cum_ready = sem("dt_ready"), sem("cum_mm"), sem("cum_hi"), sem("cum_ready")
        brow_mm, brow_ready, brow_stored = sem("brow_mm"), sem("brow_ready"), sem("brow_stored")
        conv_first, conv_silu = sem("conv_first"), sem("conv_silu")
        cb_mm, cb_ready = sem("cb_mm"), sem("cb_ready")
        xtok_mm, xtok_ready = sem("xtok_mm"), sem("xtok_ready")
        row_mm, decay_ready, mt_ready = sem("row_mm"), sem("decay_ready"), sem("mt_ready")
        y_mm, y_ready, ysq_ready, ssq_mm, rs_ready = sem("y_mm"), sem("y_ready"), sem("ysq_ready"), sem("ssq_mm"), sem("rs_ready")
        yn_ready, y_hi_done, y_lo_done = sem("yn_ready"), sem("y_hi_done"), sem("y_lo_done")
        a_mm, a_neg, a_exp, a_norm = sem("a_mm"), sem("a_neg"), sem("a_exp"), sem("a_norm")
        a_turned, a_probT, a_out, a_hi, a_lo = sem("a_turned"), sem("a_probT"), sem("a_out"), sem("a_hi"), sem("a_lo")
        b_mm, b_neg, b_exp, b_norm = sem("b_mm"), sem("b_neg"), sem("b_exp"), sem("b_norm")
        b_turned, b_probT, b_out, b_hi, b_lo = sem("b_turned"), sem("b_probT"), sem("b_out"), sem("b_hi"), sem("b_lo")
        bias_loaded = sem("bias_loaded")
        h_hi, h_lo = sem("h_hi"), sem("h_lo")
        stored = sem("stored")

        class Own:

            def __init__(self, eng, s):
                self.eng, self.sem, self.n = eng, s, 0

            def mark(self, ins):
                ins.then_inc(self.sem, 1)
                self.n += 1

            def wait(self, i=0, per=0):
                self.eng.wait_ge(self.sem, self.n + i * per if per else self.n)

        TURN_GAIN = [A["mix_pre_g"][0], A["mem_norm_g"], A["mem_pre_g"][0], A["ffn_pre_g"][0],
                     A["mix_pre_g"][1], A["kv_norm_g"], A["mem_pre_g"][1], A["ffn_pre_g"][1]]
        POST_GAIN = [A["mix_post_g"][0], A["mem_post_g"][0], A["ffn_post_g"][0],
                     A["mix_post_g"][1], A["mem_post_g"][1], A["ffn_post_g"][1]]
        POST_TURN = [2, 3, 4, 6, 7, None]
        M_OF_POST = ["w_out", "wo0", "down0", "mo", "wo1", "down1"]

        def last_unit(name):
            return max(u for (n, _), u in U.items() if n == name)

        def every_row(row):
            return bass.AP(row.tensor, row.offset, [[0, P]] + [list(d) for d in row.ap])

        block = ctx.enter_context(nc.Block())

        @block.sync
        def _(sp):
            def load(u, slot_out=None):
                name, i = NAME_OF[u]
                if u >= SLOTS:
                    sp.wait_ge(w_used, u - SLOTS + 1)
                src = unit_source(name, i)
                dst = raw[:, u % SLOTS, :].rearrange("p (k n) -> p k n", n=src.shape[-1])
                sp.dma_start(dst, src).then_inc(w_loaded[u % SLOTS], 16)

            sp.dma_start(x[:], A["x"][0].rearrange("(t p) n -> p t n", p=P)).then_inc(x_loaded, 16)
            sp.dma_start(const[:], A["consts"][:, 0:C_HOT]).then_inc(const_loaded, 16)
            sp.wait_ge(par_cleared, 1)
            sp.dma_start(par_rows[0:TAPS * CT, 0, :], A["ssm_conv_w"][0].rearrange("k (c p) -> (k c) p", p=P)).then_inc(par_loaded, 16)
            sp.dma_start(par_rows[0:CT, 1, :], A["ssm_conv_b"][0].rearrange("(c p) -> c p", p=P)).then_inc(par_loaded, 16)
            sp.dma_start(par_rows[G_ROW:G_ROW + XT, 1, :], A["ssm_norm_g"][0].rearrange("(c p) -> c p", p=P)).then_inc(par_loaded, 16)
            sp.dma_start(d_pair[D_ROW:D_ROW + XT, :], A["ssm_d"][0].rearrange("(c e) -> c e", e=2)).then_inc(par_loaded, 16)
            sp.dma_start(dtw[:], row_tiles(w_in, 0, KD, DI + CONV, SSM_HEADS)).then_inc(par_loaded, 16)
            for u in range(NUNITS):
                load(u)

        @block.gpsimd
        def _(pool):
            mem_t = A["mem"][0].rearrange("(t p) n -> p t n", p=P)
            pool.dma_start(pre_row[:], every_row(TURN_GAIN[0])).then_inc(pre_loaded, 16)
            pool.wait_ge(u_ready, 2)
            pool.dma_start(pre_row[:], every_row(TURN_GAIN[1])).then_inc(pre_loaded, 16)
            pool.dma_start(dt_row[:, 0, :], every_row(A["ssm_dt_bias"][0])).then_inc(rows_loaded, 16)
            pool.dma_start(dt_row[:, 1, :], every_row(A["ssm_a_log"][0])).then_inc(rows_loaded, 16)
            pool.dma_start(memV[:], mem_t).then_inc(mem_loaded, 16)
            pool.dma_start(hot[:], A["consts"][0:BUCKETS, C_HOT:C_END]).then_inc(rows_loaded, 16)
            pool.dma_start(relb[:], A["rel_bias"]).then_inc(rows_loaded, 16)
            pool.dma_start(post_row[:], every_row(POST_GAIN[0])).then_inc(post_loaded, 16)
            pool.wait_ge(brow_ready, 1)
            pool.dma_start(bias_rows, brows[:]).then_inc(brow_stored, 16)
            for n in range(6):
                turn = POST_TURN[n]
                if turn is not None:
                    pool.wait_ge(u_ready, 2 * turn)
                    pool.dma_start(pre_row[:], every_row(TURN_GAIN[turn])).then_inc(pre_loaded, 16)
                if n < 5:
                    pool.wait_ge(x_ready, 2 * n + 2)
                    pool.dma_start(post_row[:], every_row(POST_GAIN[n + 1])).then_inc(post_loaded, 16)
                if n == 2:
                    pool.wait_ge(w_used, last_unit("down0") + 1)
                    pool.wait_ge(brow_stored, 16)
                    for c0, c, base in ((0, S, 0), (S, P, P)):
                        src = bass.AP(bias_rows.tensor, base, [[1, P], [3 * P, AH], [1, c]])
                        pool.dma_start(mbias[:, :, c0:c0 + c], src).then_inc(bias_loaded, 16)
                    pool.wait_ge(u_ready, 10)
                    pool.dma_start(pre_row[:], every_row(TURN_GAIN[5])).then_inc(pre_loaded, 16)
            for t in range(ST):
                pool.wait_ge(x_ready, 11 + t)
                pool.dma_start(out[0, t * P:(t + 1) * P, :], x[:, t, :]).then_inc(stored, 16)
            pool.wait_ge(stored, 16 * ST)

        @block.tensor
        def _(pe):
            ident = const[:, C_ID:C_ID + P]
            tri_ones = const[:, C_TRI:C_TRI + S]

            def product(dst, passes, first, last):
                for n, (a, b) in enumerate(passes):
                    ins = pe.matmul(dst, a, b, start=first and n == 0, stop=last and n == len(passes) - 1,
                                    skip_group_check=True)
                return ins

            def t_unit(slot, b, act_hi, act_lo):
                for c in range(TC // P):
                    for k in range(KD):
                        cols = slice(k * TC + c * P, k * TC + (c + 1) * P)
                        wh, wl = hi[:, slot, cols], lo[:, slot, cols]
                        ins = product(bank[:, b, c * S:(c + 1) * S],
                                      [(wh, act_hi[:, k, :]), (wh, act_lo[:, k, :]), (wl, act_hi[:, k, :])],
                                      k == 0, k == KD - 1)
                return ins

            def v_unit(slot, b, act_hi, act_lo):
                for t in range(ST):
                    for k in range(KD):
                        cols = slice(k * TC, (k + 1) * TC)
                        ah, al = act_hi[:, k, t * P:(t + 1) * P], act_lo[:, k, t * P:(t + 1) * P]
                        ins = product(bank[:, b, t * TC:(t + 1) * TC],
                                      [(ah, hi[:, slot, cols]), (ah, lo[:, slot, cols]), (al, hi[:, slot, cols])],
                                      k == 0, k == KD - 1)
                return ins

            def banked(name, i, act_hi, act_lo):
                u, v = U[(name, i)], V_OF[(name, i)]
                e, n = FREED[v - 2]
                pe.wait_ge(t_out[e], n)
                pe.wait_ge(w_lo_done, u + 1)
                f = t_unit if KIND[name] == "T" else v_unit
                f(u % SLOTS, v % 2, act_hi, act_lo).then_inc(w_used, 1)

            def fill(name, *units):
                for i in units:
                    banked(name, i, memT_hi, memT_lo)

            def loop_t(name, iters, free_of_slot):
                u0, v0 = U[(name, 0)], V_OF[(name, 0)]
                for v in (v0 - 2, v0 - 1):
                    e, n = FREED[v]
                    pe.wait_ge(t_out[e], n)
                with pe.Fori(0, iters) as i:
                    for j in range(5):
                        if j:
                            e, n = free_of_slot(j, i)
                            pe.wait_ge(t_out[e], n)
                        if j < 4:
                            pe.wait_ge(w_lo_done, i * 4 + (u0 + j + 1))
                            t_unit((u0 + j) % SLOTS, (v0 + j) % 2, actT_hi, actT_lo).then_inc(w_used, 1)

            def m_part(name, act_hi, act_lo, ready):
                n = last_unit(name) - U[(name, 0)] + 1
                for i in range(n):
                    u = U[(name, i)]
                    ready(i)
                    pe.wait_ge(w_lo_done, u + 1)
                    for t in range(ST):
                        for r in range(MR):
                            k = i * MR + r
                            ah, al = act_hi[:, k, t * P:(t + 1) * P], act_lo[:, k, t * P:(t + 1) * P]
                            for half in range(2):
                                cols = slice(r * D + half * 512, r * D + half * 512 + 512)
                                wh, wl = hi[:, u % SLOTS, cols], lo[:, u % SLOTS, cols]
                                ins = product(bank[:, 4 + 2 * t + half, :], [(ah, wh), (ah, wl), (al, wh)],
                                              k == 0, k == n * MR - 1)
                    ins.then_inc(w_used, 1)

            def turn(k):
                for t in range(ST):
                    pe.wait_ge(u_ready, 2 * k + t + 1)
                    for half in range(2):
                        for q in range(4):
                            c = (half * 4 + q) * P
                            ins = pe.transpose(bank[:, 4 + 2 * t + half, q * P:(q + 1) * P], ntmp[:, t, c:c + P], ident)
                        ins.then_inc(turned, 1)

            def turn_done(k):
                pe.wait_ge(turn_lo, 4 * k + 4)

            pe.wait_ge(const_loaded, 16)
            pe.wait_ge(par_loaded, 80)
            pe.wait_ge(consts_made, 1)
            for r in range(2):
                ins = pe.transpose(bank[:, 0, r * P:(r + 1) * P], par_rows[:, r, :], ident)
            ins.then_inc(par_turned, 1)
            turn(0)
            turn_done(0)
            pe.wait_ge(dtw_lo_done, 1)
            for t in range(ST):
                for k in range(KD):
                    ah, al = actT_hi[:, k, t * P:(t + 1) * P], actT_lo[:, k, t * P:(t + 1) * P]
                    ins = product(bank[:, 1, t * SSM_HEADS:(t + 1) * SSM_HEADS],
                                  [(ah, dtw_hi[:, k, :]), (ah, dtw_lo[:, k, :]), (al, dtw_hi[:, k, :])],
                                  k == 0, k == KD - 1)
            ins.then_inc(dt_mm, 1)

            loop_t("xbc", 3, lambda j, i: ("dve", i * 4 + j))
            pe.wait_ge(dt_ready, 1)
            adt = dtc[:, 6]
            product(bank[:, 2, 0:32], [(tri_ones[:, 0:P], adt[:, 0, :])], True, True)
            product(bank[:, 2, 32:64], [(tri_ones[:, P:S], adt[:, 0, :]), (tri_ones[:, 0:P], adt[:, 1, :])], True, True)
            product(bank[0:SSM_HEADS, 3, 0:S], [(adt[:, 0, :], tri_ones)], True, False)
            product(bank[0:SSM_HEADS, 3, P:S], [(adt[:, 1, :], tri_ones[:, 0:P])], False, True).then_inc(cum_mm, 1)
            turn(1)
            loop_t("z", 2, lambda j, i: ("act", i * 4 + j))
            pe.wait_ge(rows_loaded, 64)
            pe.wait_ge(cum_ready, 1)
            product(bank[0:AH, 2, 0:S], [(relb[:], hot[:])], True, True).then_inc(brow_mm, 1)
            turn_done(1)

            pe.wait_ge(conv_silu, CT // 2)
            fills = {1: ("k0", 0), 4: ("k0", 1), 7: ("k0", 2), 10: ("k0", 3), 13: ("v0", 0)}

            def ssd_y(j):
                g = j // GT
                for e in range(2):
                    h = 2 * j + e
                    pe.wait_ge(mt_ready, h + 1)
                    if e == 0:
                        if j >= 2:
                            pe.wait_ge(y_ready, j - 1)
                    rows = slice(e * HD, (e + 1) * HD)
                    pe.matmul(bank[rows, 3 + j % 2 * 3, 0:S], xtok[:, j % 2, 0, rows], mt[:, h % 4, 0:S],
                              start=True, stop=False, skip_group_check=True)
                    ins = pe.matmul(bank[rows, 3 + j % 2 * 3, P:S], xtok[:, j % 2, 1, rows], mt[:, h % 4, S:CAUS],
                                    start=False, stop=True, skip_group_check=True)
                ins.then_inc(y_mm, 1)

            def ssd_ssq(j):
                pe.wait_ge(ysq_ready, j + 1)
                if j % GT == 0 and j:
                    pe.wait_ge(rs_ready, j // GT)
                product(bank[:, 7, 0:S], [(tri_ones[:, P:S], ycum[:, j % 2, :])], j % GT == 0, j % GT == GT - 1).then_inc(ssq_mm, 1)

            for j in range(XT + 2):
                if j < XT:
                    g = j // GT
                    if j % GT == 0:
                        if g:
                            pe.wait_ge(xtok_ready, j)
                        else:
                            pe.wait_ge(brow_ready, 1)
                        Bt, Ct = xbc[:, XT + g, :], xbc[:, XT + SSM_GROUPS + g, :]
                        product(bank[:, 2, 0:S], [(Bt[:, 0:P], Ct)], True, True)
                        product(bank[:, 2, S:CAUS], [(Bt[:, P:S], Ct[:, P:S])], True, True).then_inc(cb_mm, 1)
                    if j % GT == 0:
                        pe.wait_ge(cb_ready, g + 1)
                    else:
                        pe.wait_ge(xtok_ready, j)
                    for t in range(ST):
                        ins = pe.transpose(bank[:, 2, t * P:(t + 1) * P], xbc[:, j, t * P:(t + 1) * P], ident)
                    ins.then_inc(xtok_mm, 1)
                    for e in range(2):
                        h = 2 * j + e
                        if h >= 2:
                            pe.wait_ge(decay_ready, h - 1)
                        one = id_r[:, h:h + 1].broadcast_to([P, P])
                        row = bank[:, 4 + h % 2, :]
                        for dst, l0, l1 in ((row[:, 0:S], 0, S), (row[:, S:CAUS], P, S)):
                            pe.matmul(dst, one, cumT_hi[:, l0:l1], start=True, stop=False, skip_group_check=True)
                            pe.matmul(dst, one, cumT_lo[:, l0:l1], start=False, stop=False, skip_group_check=True)
                            ins = pe.matmul(dst[:, 0:P], id_bf[:], mask_bf[:], start=False, stop=True, skip_group_check=True)
                        ins.then_inc(row_mm, 1)
                if 1 <= j <= XT:
                    ssd_y(j - 1)
                if j >= 2:
                    ssd_ssq(j - 2)
                if j in fills:
                    fill(*fills[j])
            fill("v0", 1)

            pe.wait_ge(rs_ready, SSM_GROUPS)
            m_part("w_out", y_hi, y_lo, lambda i: pe.wait_ge(y_lo_done, i * MR // GT + 1))
            fill("v0", 2, 3)
            turn(2)

            def memory_attention(layer):
                h0 = layer * MH
                for name in ("q", "k", "v"):
                    e, n = FREED[V_OF[(f"{name}{layer}", 3)]]
                    pe.wait_ge(t_out[e], n)
                for s in range(MH + 2):
                    if s < MH:
                        b = 4 + s % 2
                        if s >= 2:
                            pe.wait_ge(a_exp, h0 + s - 1)
                        for t in range(ST):
                            for kk in range(2):
                                ins = pe.matmul(bank[:, b, t * S:(t + 1) * S], qT[:, 2 * s + kk, t * P:(t + 1) * P],
                                                memK[:, 2 * s + kk, :], start=kk == 0, stop=kk == 1, skip_group_check=True)
                        ins.then_inc(a_mm, 1)
                    if 1 <= s <= MH:
                        h = s - 1
                        pe.wait_ge(a_norm, h0 + h + 1)
                        if h >= 2:
                            pe.wait_ge(a_probT, h0 + h - 1)
                        for m in range(ST):
                            for t in range(ST):
                                ins = pe.transpose(bank[:, 6 + h % 2, m * S + t * P:m * S + (t + 1) * P],
                                                   prob[:, h % 2, t, m * P:(m + 1) * P], ident)
                        ins.then_inc(a_turned, 1)
                    if s >= 2:
                        h = s - 2
                        pe.wait_ge(a_probT, h0 + h + 1)
                        if h >= 2:
                            pe.wait_ge(a_lo, h0 + h - 1)
                        for d in range(2):
                            for m in range(ST):
                                c = (2 * h + d) * P
                                ins = pe.matmul(bank[:, 2 + h % 2, d * S:(d + 1) * S], memV[:, m, c:c + P],
                                                probT[:, h % 2, m, :], start=m == 0, stop=m == 1, skip_group_check=True)
                        ins.then_inc(a_out, 1)

            def qkv(name):
                for i in range(4):
                    banked(name, i, actT_hi, actT_lo)

            def feed_forward(layer):
                name = f"gu{layer}"
                a0, d0 = FREED[V_OF[(name, 0)]][1] - 1, FREED[V_OF[(name, 1)]][1] - 1
                loop_t(name, 5, lambda j, i: (("act", "dve")[j % 2], i * 2 + ((a0, d0)[j % 2] + j // 2)))
                for i in (20, 21):
                    banked(name, i, actT_hi, actT_lo)
                m_part(f"down{layer}", hT_hi, hT_lo, lambda i: pe.wait_ge(h_lo, 11 * layer + i + 1))

            turn_done(2)
            qkv("q0")
            memory_attention(0)
            m_part("wo0", actT_hi, actT_lo, lambda i: pe.wait_ge(a_lo, i + 1))
            fill("k1", 0, 1)
            turn(3)
            turn_done(3)
            feed_forward(0)
            fill("k1", 2, 3)
            turn(4)
            turn_done(4)
            qkv("mq")
            turn(5)
            fill("v1", 0)
            turn_done(5)
            qkv("mk")
            qkv("mv")

            pairs = AH // 2
            e, n = FREED[V_OF[("mv", 3)]]
            pe.wait_ge(t_out[e], n)
            for s in range(pairs + 2):
                if s < pairs:
                    if s:
                        pe.wait_ge(b_neg, s)
                    for a in range(2):
                        rows = slice(a * HD, (a + 1) * HD)
                        pe.matmul(bank[:, 4 + a, 0:S], mqT[rows, s, P:S], mkT[rows, s, :], start=True, stop=True, skip_group_check=True)
                        ins = pe.matmul(bank[:, 4 + a, S:CAUS], mqT[rows, s, 0:P], mkT[rows, s, 0:P], start=True, stop=True, skip_group_check=True)
                    ins.then_inc(b_mm, 1)
                if 1 <= s <= pairs:
                    p = s - 1
                    pe.wait_ge(b_norm, p + 1)
                    if p:
                        pe.wait_ge(b_probT, p)
                    for a in range(2):
                        for n, c in enumerate((S, 0, P)):
                            ins = pe.transpose(bank[:, 6 + a, n * P:(n + 1) * P], sc[:, p % 2, a, c:c + P], ident)
                    ins.then_inc(b_turned, 1)
                if s >= 2:
                    p = s - 2
                    pe.wait_ge(b_probT, p + 1)
                    if p >= 2:
                        pe.wait_ge(b_lo, p - 1)
                    for a in range(2):
                        rows = slice(a * HD, (a + 1) * HD)
                        cols = slice((2 * p + a) * HD, (2 * p + a + 1) * HD)
                        pe.matmul(bank[rows, 2 + p % 2, 0:S], mV[:, 0, cols], scT[:, p % 2, a, 0:S], start=True, stop=False, skip_group_check=True)
                        ins = pe.matmul(bank[rows, 2 + p % 2, P:S], mV[:, 1, cols], scT[:, p % 2, a, S:CAUS], start=False, stop=True, skip_group_check=True)
                    ins.then_inc(b_out, 1)
            fill("v1", 1)
            m_part("mo", actT_hi, actT_lo, lambda i: pe.wait_ge(b_lo, 2 * i + 2))
            fill("v1", 2, 3)
            turn(6)
            turn_done(6)
            qkv("q1")
            memory_attention(1)
            m_part("wo1", actT_hi, actT_lo, lambda i: pe.wait_ge(a_lo, MH + i + 1))
            turn(7)
            turn_done(7)
            feed_forward(1)

        @block.scalar
        def _(act):
            own = Own(act, act_step)
            done = [0]

            def hi_unit(u, i=0, per=0):
                count = 16 * (u // SLOTS + 1)
                act.wait_ge(w_loaded[u % SLOTS], i * 16 + count if per else count)
                act.activation(hi[:, u % SLOTS, :], raw[:, u % SLOTS, :], ACT.Copy).then_inc(w_hi_done, 1)

            def hi_upto(u):
                while done[0] <= min(u, NUNITS - 1):
                    hi_unit(done[0])
                    done[0] += 1

            def statistic(c, src):
                own.mark(act.activation(ntmp[:, c % 2, :], src, ACT.Square, accum_out=stats[:, 0, c:c + 1]))
                own.wait()
                own.mark(act.activation(stats[:, 1, c:c + 1], stats[:, 0, c:c + 1], ACT.Ln, bias=eps_col, scale=1.0 / D))
                own.wait()
                act.activation(stats[:, 2, c:c + 1], stats[:, 1, c:c + 1], ACT.Exp, scale=-0.5).then_inc(stat_ready, 1)

            def turn(k, dst):
                for t in range(ST):
                    for half in range(2):
                        act.wait_ge(turned, 4 * k + 2 * t + half + 1)
                        act.activation(dst[:, half * 4:half * 4 + 4, t * P:(t + 1) * P],
                                       bank[:, 4 + 2 * t + half, :].rearrange("p (q n) -> p q n", n=P),
                                       ACT.Copy).then_inc(turn_hi, 1)

            def tiles(b):
                return bank[:, b, :].rearrange("p (c n) -> p c n", n=S)

            def copy_out(name, i):
                u, v = U[(name, i)], V_OF[(name, i)]
                act.wait_ge(w_used, u + 1)
                src = tiles(v % 2)
                dst = {"mq": mqT, "mk": mkT, "mv": mV, "k0": memK, "k1": memK, "v0": memV, "v1": memV, "q0": qT, "q1": qT}[name]
                if name == "mq":
                    src = bank[:, v % 2, :].rearrange("p (c n) -> p c n", n=P)
                    dst = reversed_last(mqT[:].rearrange("p k (t n) -> p (k t) n", n=P)[:, 4 * i:4 * i + 4, :])
                elif KIND[name] == "V":
                    dst = dst[:, :, i * TC:(i + 1) * TC]
                else:
                    dst = dst[:, 2 * i:2 * i + 2, :]
                act.activation(dst, src, ACT.Copy).then_inc(t_out["act"], 1)

            def copies(name, *units):
                for i in units:
                    hi_upto(U[(name, i)] + 2)
                    copy_out(name, i)

            def m_part(name):
                hi_upto(last_unit(name) + 2)

            def norms(n):
                act.preload_act_table_set("natural_log_exp_and_others")
                act.wait_ge(w_used, last_unit(M_OF_POST[n]) + 1)
                for t in range(ST):
                    statistic(4 + 4 * n + t, msum[t])
                if POST_TURN[n] is not None:
                    for t in range(ST):
                        act.wait_ge(x_ready, 2 * n + t + 1)
                        statistic(6 + 4 * n + t, x[:, t, :])

            act.preload_act_table_set("natural_log_exp_and_others")
            act.wait_ge(eps_made, 1)
            act.wait_ge(x_loaded, 16)
            for t in range(ST):
                statistic(t, x[:, t, :])
            act.wait_ge(par_loaded, 80)
            act.activation(dtw_hi[:], dtw[:], ACT.Copy).then_inc(dtw_hi_done, 1)
            turn(0, actT_hi)
            hi_upto(1)
            act.wait_ge(dt_mm, 1)
            act.activation(dtc[:, 0], bank[:, 1, 0:ST * SSM_HEADS].rearrange("p (t h) -> p t h", t=ST), ACT.Copy).then_inc(t_out["act"], 1)
            act.wait_ge(dt_biased, 1)
            own.mark(act.activation(dtc[:, 2], dtc[:, 1], ACT.Abs))
            own.wait()
            own.mark(act.activation(dtc[:, 3], dtc[:, 2], ACT.Exp, scale=-1.0))
            own.wait()
            act.activation(dtc[:, 4], dtc[:, 3], ACT.Ln, bias=one_col)
            act.activation(dt_row[:, 1, :], dt_row[:, 1, :], ACT.Exp).then_inc(dt_logged, 1)
            act.wait_ge(mem_loaded, 16)
            for t in range(ST):
                statistic(2 + t, memV[:, t, :])
            act.preload_act_table_set("silu_and_others")

            def silu_conv(i, j):
                act.wait_ge(t_out["dve"], i * 4 + (j + 2))
                act.activation(xbc[:, bass.ds(i * 8 + 2 * j, 2), :], conv_acc[:, j % 2], ACT.Silu).then_inc(conv_silu, 1)

            with act.Fori(0, 3) as i:
                for j in range(4):
                    hi_unit(2 + j, i, 4)
                    if j:
                        silu_conv(i, j - 1)
                    act.wait_ge(w_used, i * 4 + (j + 1))
                    for c in range(2):
                        ins = act.activation(conv_acc[:, j % 2, c, :], tiles(j % 2)[:, c, :], ACT.Identity,
                                             scale=cw[:, bass.ds(i * 8 + (3 * CT + 2 * j + c), 1)],
                                             bias=cw[:, bass.ds(i * 8 + (4 * CT + 2 * j + c), 1)])
                    ins.then_inc(conv_first, 1)
                silu_conv(i, 3)
            act.wait_ge(cum_mm, 1)
            act.activation(cumT_hi[0:SSM_HEADS, :], bank[0:SSM_HEADS, 3, 0:S], ACT.Copy).then_inc(cum_hi, 1)
            turn(1, memT_hi)
            with act.Fori(0, 2) as i:
                for j in range(4):
                    hi_unit(14 + j, i, 4)
                    act.wait_ge(w_used, i * 4 + (12 + j + 1))
                    act.activation(z[:, bass.ds(i * 8 + 2 * j, 2), :], tiles(j % 2), ACT.Silu).then_inc(t_out["act"], 1)
            done[0] = 22

            act.preload_act_table_set("natural_log_exp_and_others")
            fills = {1: ("k0", 0), 4: ("k0", 1), 7: ("k0", 2), 10: ("k0", 3), 13: ("v0", 0)}
            for j in range(XT + 3):
                if j < XT:
                    g = j // GT
                    if j % GT == 0:
                        act.wait_ge(cb_mm, g + 1)
                        act.activation(cbT[:, g % 2, :], bank[:, 2, 0:CAUS], ACT.Copy).then_inc(cb_ready, 1)
                    act.wait_ge(xtok_mm, j + 1)
                    act.activation(xtok[:, j % 2], bank[:, 2, 0:S].rearrange("p (t n) -> p t n", n=P), ACT.Copy).then_inc(xtok_ready, 1)
                    for h in (2 * j, 2 * j + 1):
                        act.wait_ge(row_mm, h + 1)
                        if h >= 2:
                            act.wait_ge(mt_ready, h - 1)
                        row = bank[:, 4 + h % 2, :]
                        act.activation(decay[:, h % 2, 0:S], row[:, 0:S], ACT.Exp, bias=dtc[:, 7, 0, h:h + 1])
                        act.activation(decay[:, h % 2, S:CAUS], row[:, S:CAUS], ACT.Exp, bias=dtc[:, 7, 1, h:h + 1]).then_inc(decay_ready, 1)
                if 1 <= j <= XT:
                    act.wait_ge(y_ready, j)
                    if j >= 3:
                        act.wait_ge(ssq_mm, j - 2)
                    act.activation(ycum[:, (j - 1) % 2, :], z[:, j - 1, :], ACT.Square).then_inc(ysq_ready, 1)
                if j >= 2 and (j - 2) % GT == GT - 1 and j - 2 < XT:
                    act.wait_ge(ssq_mm, j - 1)
                    own.mark(act.activation(rs[:, 0, :], bank[:, 7, 0:S], ACT.Ln, bias=eps_col, scale=1.0 / (GT * P)))
                    own.wait()
                    act.activation(rs[:, 1, :], rs[:, 0, :], ACT.Exp, scale=-0.5).then_inc(rs_ready, 1)
                if j >= 3 and (j - 3) % GT == GT - 1:
                    g = (j - 3) // GT
                    act.wait_ge(yn_ready, g + 1)
                    act.activation(y_hi[:, g * GT:(g + 1) * GT, :], z[:, g * GT:(g + 1) * GT, :], ACT.Copy).then_inc(y_hi_done, 1)
                if j in fills:
                    if j == 1:
                        act.wait_ge(brow_stored, 16)
                    copies(fills[j][0], fills[j][1])
            copies("v0", 1)

            m_part("w_out")
            norms(0)
            copies("v0", 2, 3)
            turn(2, actT_hi)

            def memory_attention(layer):
                for s in range(MH + 2):
                    if s < MH:
                        n, b = layer * MH + s, 4 + s % 2
                        act.wait_ge(a_neg, n + 1)
                        for t in range(ST):
                            col = 2 * s + t
                            ins = act.activation(prob[:, s % 2, t, :], bank[:, b, t * S:(t + 1) * S], ACT.Exp,
                                                 bias=mstat[:, 1, col:col + 1], scale=(D // MH) ** -0.5,
                                                 accum_out=mstat[:, 2, col:col + 1])
                        ins.then_inc(a_exp, 1)
                    if 1 <= s <= MH:
                        act.wait_ge(a_turned, layer * MH + s)
                        act.activation(probT[:, (s - 1) % 2], tiles(6 + (s - 1) % 2), ACT.Copy).then_inc(a_probT, 1)
                    if s >= 2:
                        h = s - 2
                        act.wait_ge(a_out, layer * MH + h + 1)
                        act.activation(actT_hi[:, 2 * h:2 * h + 2, :], tiles(2 + h % 2), ACT.Copy).then_inc(a_hi, 1)

            def feed_forward(layer):
                name = f"gu{layer}"
                u0, v0 = U[(name, 0)], V_OF[(name, 0)]
                a0, d0 = FREED[v0][1] - 1, FREED[v0 + 1][1] - 1
                act.preload_act_table_set("silu_and_others")

                def unit(j, i, per, tile):
                    hi_unit(u0 + 2 + j, i, per)
                    act.wait_ge(w_used, i * 4 + (u0 + j + 1) if per else u0 + j + 1)
                    if j % 2 == 0:
                        act.activation(gate[:, j // 2 % 2], tiles((v0 + j) % 2), ACT.Silu).then_inc(t_out["act"], 1)
                    else:
                        act.wait_ge(t_out["dve"], i * 2 + (d0 + j // 2 + 1) if per else d0 + j // 2 + 1)
                        act.activation(hT_hi[:, tile, :], hval[:, j // 2 % 2], ACT.Copy).then_inc(h_hi, 1)

                with act.Fori(0, 5) as i:
                    for j in range(4):
                        unit(j, i, 4, bass.ds(i * 4 + j // 2 * 2, 2))
                for j in (20, 21):
                    unit(j, 0, 0, slice(FT - 2, FT))
                done[0] = u0 + 24
                m_part(f"down{layer}")

            copies("q0", 0, 1, 2, 3)
            memory_attention(0)
            m_part("wo0")
            norms(1)
            copies("k1", 0, 1)
            turn(3, actT_hi)
            hi_upto(U[("gu0", 0)] + 1)
            feed_forward(0)
            norms(2)
            copies("k1", 2, 3)
            turn(4, actT_hi)
            copies("mq", 0, 1, 2, 3)
            turn(5, actT_hi)
            copies("v1", 0)
            copies("mk", 0, 1, 2, 3)
            copies("mv", 0, 1, 2, 3)
            pairs = AH // 2
            for s in range(pairs + 2):
                if s < pairs:
                    act.wait_ge(b_neg, s + 1)
                    for seg, c0, c1 in ((0, 0, S), (2, S, CAUS)):
                        for a in range(2):
                            col = 4 * s + seg + a
                            ins = act.activation(sc[:, s % 2, a, c0:c1], sc[:, s % 2, a, c0:c1], ACT.Exp,
                                                 bias=bstat[:, 1, col:col + 1], accum_out=bstat[:, 2, col:col + 1])
                    ins.then_inc(b_exp, 1)
                if 1 <= s <= pairs:
                    act.wait_ge(b_turned, s)
                    act.activation(scT[:, (s - 1) % 2], bank[:, 6:8, 0:CAUS], ACT.Copy).then_inc(b_probT, 1)
                if s >= 2:
                    p = s - 2
                    act.wait_ge(b_out, p + 1)
                    src = reversed_last(bank[:, 2 + p % 2, 0:S].rearrange("p (t n) -> p t n", n=P))
                    act.activation(actT_hi[:, p, :].rearrange("p (t n) -> p t n", n=P), src, ACT.Copy).then_inc(b_hi, 1)
            copies("v1", 1)
            m_part("mo")
            norms(3)
            copies("v1", 2, 3)
            turn(6, actT_hi)
            copies("q1", 0, 1, 2, 3)
            memory_attention(1)
            m_part("wo1")
            norms(4)
            turn(7, actT_hi)
            hi_upto(U[("gu1", 0)] + 1)
            feed_forward(1)
            norms(5)

        @block.vector
        def _(dve):
            own = Own(dve, dve_step)
            done = [0]

            def lo_unit(u, i=0, per=0):
                dve.wait_ge(w_hi_done, i * 4 + (u + 1) if per else u + 1)
                s = u % SLOTS
                dve.tensor_tensor(lo[:, s, :], raw[:, s, :], hi[:, s, :].bitcast(F32), ALU.subtract).then_inc(w_lo_done, 1)

            def lo_upto(u):
                while done[0] <= min(u, NUNITS - 1):
                    lo_unit(done[0])
                    done[0] += 1

            def tiles(b):
                return bank[:, b, :].rearrange("p (c n) -> p c n", n=S)

            def inverse_rms(c):
                col = [stats[:, n, c:c + 1] for n in range(6)]
                dve.wait_ge(stat_ready, c + 1)
                own.mark(dve.tensor_scalar(col[3], col[0], 1.0 / D, EPS, ALU.mult, ALU.add))
                own.wait()
                own.mark(dve.scalar_tensor_tensor(out=col[4], in0=col[2], scalar=col[3], in1=col[2], op0=ALU.mult, op1=ALU.mult))
                own.wait()
                own.mark(dve.tensor_scalar(col[4], col[4], -0.5, 1.5, ALU.mult, ALU.add))
                own.wait()
                own.mark(dve.tensor_tensor(col[5], col[2], col[4], ALU.mult))
                own.wait()

            def normalise(k, c, src, fresh=True):
                for t in range(ST):
                    if fresh:
                        inverse_rms(c + t)
                    if t == 0:
                        dve.wait_ge(pre_loaded, 16 * (k + 1))
                    dve.scalar_tensor_tensor(out=ntmp[:, t, :], in0=src[:, t, :], scalar=stats[:, 5, c + t:c + t + 1],
                                             in1=pre_row[:], op0=ALU.mult, op1=ALU.mult).then_inc(u_ready, 1)

            def turn(k, dst_hi, dst_lo):
                for t in range(ST):
                    for half in range(2):
                        dve.wait_ge(turn_hi, 4 * k + 2 * t + half + 1)
                        part = (slice(None), slice(half * 4, half * 4 + 4), slice(t * P, (t + 1) * P))
                        dve.tensor_tensor(dst_lo[part], bank[:, 4 + 2 * t + half, :].rearrange("p (q n) -> p q n", n=P),
                                          dst_hi[part].bitcast(F32), ALU.subtract).then_inc(turn_lo, 1)

            def m_part(name):
                lo_upto(last_unit(name) + 2)

            def update(n):
                for t in range(ST):
                    inverse_rms(4 + 4 * n + t)
                    if t == 0:
                        dve.wait_ge(post_loaded, 16 * (n + 1))
                    c = 4 + 4 * n + t
                    own.mark(dve.scalar_tensor_tensor(out=ntmp[:, t, :], in0=msum[t], scalar=stats[:, 5, c:c + 1],
                                                      in1=post_row[:], op0=ALU.mult, op1=ALU.mult))
                    own.wait()
                    dve.tensor_tensor(x[:, t, :], x[:, t, :], ntmp[:, t, :], ALU.add).then_inc(x_ready, 1)
                if POST_TURN[n] is not None:
                    normalise(POST_TURN[n], 6 + 4 * n, x)

            def fills(name, *units):
                for i in units:
                    lo_upto(U[(name, i)] + 2)

            dve.memset(par_rows[:], 0.0).then_inc(par_cleared, 1)
            dve.memset(one_col, 1.0)
            dve.memset(eps_col, EPS).then_inc(eps_made, 1)
            own.mark(dve.memset(cumT_hi[:].bitcast(F32), 0.0))
            own.mark(dve.memset(cumT_lo[:].bitcast(F32), 0.0))
            dve.wait_ge(par_loaded, 80)
            dve.wait_ge(const_loaded, 16)
            dve.tensor_copy(id_bf[:], const[:, C_ID:C_ID + P])
            dve.tensor_copy(mask_bf[:], const[:, C_CAUS:C_CAUS + P])
            dve.tensor_copy(id_r[:], const[:, C_ID:C_ID + SSM_HEADS])
            d_rows = slice(D_ROW, D_ROW + XT)
            dve.tensor_copy(par_rows[d_rows, 1, :].rearrange("c (e n) -> c e n", e=2), d_pair[d_rows, :].unsqueeze(2).broadcast_to([XT, 2, HD])).then_inc(consts_made, 1)
            normalise(0, 0, x)
            dve.wait_ge(dtw_hi_done, 1)
            dve.tensor_tensor(dtw_lo[:], dtw[:], dtw_hi[:].bitcast(F32), ALU.subtract).then_inc(dtw_lo_done, 1)
            turn(0, actT_hi, actT_lo)
            dve.wait_ge(par_turned, 1)
            dve.tensor_copy(cw[:, 0:TAPS * CT], bank[:, 0, 0:TAPS * CT])
            dve.tensor_copy(cw[:, TAPS * CT:TAPS * CT + CT], bank[:, 0, P:P + CT])
            dve.tensor_copy(gT[:], bank[:, 0, P + G_ROW:P + G_ROW + XT])
            dve.tensor_copy(dT[:], bank[:, 0, P + D_ROW:P + D_ROW + XT]).then_inc(t_out["dve"], 1)
            lo_upto(1)
            dve.wait_ge(t_out["act"], 1)
            dve.wait_ge(rows_loaded, 64)
            own.mark(dve.memset(brows[:, S:3 * P], NEG))
            bias_row = dt_row[:, 0:1, :].broadcast_to([P, ST, SSM_HEADS])
            dve.tensor_tensor(dtc[:, 1], dtc[:, 0], bias_row, ALU.add).then_inc(dt_biased, 1)
            dve.wait_ge(dt_logged, 1)
            own.mark(dve.tensor_scalar(dtc[:, 5], dtc[:, 3], 1.0, None, ALU.add))
            own.wait()
            own.mark(dve.tensor_scalar(dtc[:, 6], dtc[:, 5], 1.0, None, ALU.subtract))
            own.wait()
            own.mark(dve.tensor_tensor(dtc[:, 6], dtc[:, 3], dtc[:, 6], ALU.subtract))
            own.mark(dve.reciprocal(dtc[:, 2], dtc[:, 5]))
            own.wait()
            own.mark(dve.tensor_tensor(dtc[:, 6], dtc[:, 6], dtc[:, 2], ALU.mult))
            own.wait()
            own.mark(dve.tensor_tensor(dtc[:, 6], dtc[:, 6], dtc[:, 4], ALU.add))
            own.wait()
            own.mark(dve.scalar_tensor_tensor(out=dtc[:, 5], in0=dtc[:, 1], scalar=0.0, in1=dtc[:, 6], op0=ALU.max, op1=ALU.add))
            own.wait()
            exp_a = dt_row[:, 1:2, :].broadcast_to([P, ST, SSM_HEADS])
            dve.scalar_tensor_tensor(out=dtc[:, 6], in0=dtc[:, 5], scalar=-1.0, in1=exp_a, op0=ALU.mult, op1=ALU.mult).then_inc(dt_ready, 1)
            normalise(1, 2, memV)

            with dve.Fori(0, 3) as i:
                n0 = own.n
                per = 8
                for j in range(4):
                    lo_unit(2 + j, i, 4)
                    dve.wait_ge(conv_first, i * 4 + (j + 1))
                    for tap in (2, 1, 0):
                        back = TAPS - 1 - tap
                        if tap < 2:
                            own.wait(i, per)
                        for c in range(2):
                            acc = conv_acc[:, j % 2, c, back:S]
                            ins = dve.scalar_tensor_tensor(out=acc, in0=tiles(j % 2)[:, c, 0:S - back],
                                                           scalar=cw[:, bass.ds(i * 8 + (tap * CT + 2 * j + c), 1)],
                                                           in1=acc, op0=ALU.mult, op1=ALU.add)
                        if tap:
                            own.mark(ins)
                        else:
                            ins.then_inc(t_out["dve"], 1)
                assert own.n - n0 == per
            own.n += 2 * per
            done[0] = 14
            dve.wait_ge(cum_mm, 1)
            own.mark(dve.tensor_scalar(dtc[:, 7], bank[:, 2, 0:ST * SSM_HEADS].rearrange("p (t h) -> p t h", t=ST), -1.0, None, ALU.mult))
            dve.wait_ge(cum_hi, 1)
            dve.tensor_tensor(cumT_lo[0:SSM_HEADS, :], bank[0:SSM_HEADS, 3, 0:S], cumT_hi[0:SSM_HEADS, :].bitcast(F32), ALU.subtract).then_inc(cum_ready, 1)
            turn(1, memT_hi, memT_lo)
            with dve.Fori(0, 2) as i:
                for j in range(4):
                    lo_unit(14 + j, i, 4)
            done[0] = 22
            dve.wait_ge(brow_mm, 1)
            dve.tensor_copy(brows[:, 0:S], bank[0:AH, 2, 0:S]).then_inc(brow_ready, 1)

            ssd_fills = {1: ("k0", 0), 4: ("k0", 1), 7: ("k0", 2), 10: ("k0", 3), 13: ("v0", 0)}
            dve.wait_ge(t_out["act"], FREED[V_OF[("z", 7)]][1])
            for j in range(XT + 3):
                if j < XT:
                    g = j // GT
                    if j % GT == 0:
                        dve.wait_ge(cb_ready, g + 1)
                    if j >= 2:
                        dve.wait_ge(y_mm, j - 1)
                    for h in (2 * j, 2 * j + 1):
                        dve.wait_ge(decay_ready, h + 1)
                        for t, c0, c1 in ((0, 0, S), (1, S, CAUS)):
                            ins = dve.scalar_tensor_tensor(out=mt[:, h % 4, c0:c1], in0=decay[:, h % 2, c0:c1],
                                                           scalar=dtc[:, 5, t, h:h + 1], in1=cbT[:, g % 2, c0:c1],
                                                           op0=ALU.mult, op1=ALU.mult)
                        ins.then_inc(mt_ready, 1)
                if 1 <= j <= XT:
                    c = j - 1
                    dve.wait_ge(y_mm, j)
                    own.mark(dve.scalar_tensor_tensor(out=xbc[:, c, :], in0=xbc[:, c, :], scalar=dT[:, c:c + 1],
                                                      in1=bank[:, 3 + c % 2 * 3, 0:S], op0=ALU.mult, op1=ALU.add))
                    own.wait()
                    dve.tensor_tensor(z[:, c, :], z[:, c, :], xbc[:, c, :], ALU.mult).then_inc(y_ready, 1)
                if j >= 2 and (j - 2) % GT == GT - 1 and j - 2 < XT:
                    g = (j - 2) // GT
                    dve.wait_ge(rs_ready, g + 1)
                    dve.wait_ge(y_ready, GT * (g + 1))
                    for c in range(g * GT, (g + 1) * GT):
                        ins = dve.scalar_tensor_tensor(out=z[:, c, :], in0=z[:, c, :], scalar=gT[:, c:c + 1],
                                                       in1=rs[:, 1, :], op0=ALU.mult, op1=ALU.mult)
                    ins.then_inc(yn_ready, 1)
                if j >= 3 and (j - 3) % GT == GT - 1:
                    g = (j - 3) // GT
                    group = slice(g * GT, (g + 1) * GT)
                    dve.wait_ge(y_hi_done, g + 1)
                    dve.tensor_tensor(y_lo[:, group, :], z[:, group, :], y_hi[:, group, :].bitcast(F32), ALU.subtract).then_inc(y_lo_done, 1)
                if j in ssd_fills:
                    fills(ssd_fills[j][0], ssd_fills[j][1])
            fills("v0", 1)
            m_part("w_out")
            update(0)
            fills("v0", 2, 3)
            turn(2, actT_hi, actT_lo)

            def memory_attention(layer):
                scale = (D // MH) ** -0.5
                for s in range(MH + 2):
                    n = layer * MH + s
                    cols = slice(2 * s, 2 * s + 2)
                    if s < MH:
                        dve.wait_ge(a_mm, n + 1)
                        own.mark(dve.tensor_reduce(mstat[:, 0, cols], tiles(4 + s % 2), AX.X, ALU.max))
                        own.wait()
                        dve.tensor_scalar(mstat[:, 1, cols], mstat[:, 0, cols], -scale, None, ALU.mult).then_inc(a_neg, 1)
                    if s >= 2:
                        h = s - 2
                        dve.wait_ge(a_hi, layer * MH + h + 1)
                        dve.tensor_tensor(actT_lo[:, 2 * h:2 * h + 2, :], tiles(2 + h % 2),
                                          actT_hi[:, 2 * h:2 * h + 2, :].bitcast(F32), ALU.subtract).then_inc(a_lo, 1)
                    if s < MH:
                        dve.wait_ge(a_exp, n + 1)
                        own.mark(dve.reciprocal(mstat[:, 3, cols], mstat[:, 2, cols]))
                        own.wait()
                        for t in range(ST):
                            ins = dve.tensor_scalar(prob[:, s % 2, t, :], prob[:, s % 2, t, :], mstat[:, 3, 2 * s + t:2 * s + t + 1], None, ALU.mult)
                        ins.then_inc(a_norm, 1)

            def feed_forward(layer):
                name = f"gu{layer}"
                u0, v0 = U[(name, 0)], V_OF[(name, 0)]
                a0 = FREED[v0][1] - 1
                h0 = (FT // 2) * layer

                def unit(j, i, per, tile):
                    lo_unit(u0 + 2 + j, i, per)
                    if j % 2:
                        b = j // 2 % 2
                        dve.wait_ge(w_used, i * 4 + (u0 + j + 1) if per else u0 + j + 1)
                        dve.wait_ge(t_out["act"], i * 2 + (a0 + j // 2 + 1) if per else a0 + j // 2 + 1)
                        dve.tensor_tensor(hval[:, b], tiles((v0 + j) % 2), gate[:, b], ALU.mult).then_inc(t_out["dve"], 1)
                        dve.wait_ge(h_hi, i * 2 + (h0 + j // 2 + 1) if per else h0 + j // 2 + 1)
                        dve.tensor_tensor(hT_lo[:, tile, :], hval[:, b], hT_hi[:, tile, :].bitcast(F32), ALU.subtract).then_inc(h_lo, 1)

                with dve.Fori(0, 5) as i:
                    for j in range(4):
                        unit(j, i, 4, bass.ds(i * 4 + j // 2 * 2, 2))
                for j in (20, 21):
                    unit(j, 0, 0, slice(FT - 2, FT))
                done[0] = u0 + 24
                m_part(f"down{layer}")

            fills("q0", 0, 1, 2, 3)
            memory_attention(0)
            m_part("wo0")
            update(1)
            fills("k1", 0, 1)
            turn(3, actT_hi, actT_lo)
            lo_upto(U[("gu0", 0)] + 1)
            feed_forward(0)
            update(2)
            fills("k1", 2, 3)
            turn(4, actT_hi, actT_lo)
            normalise(5, 14, x, fresh=False)
            fills("mq", 0, 1, 2, 3)
            turn(5, actT_hi, actT_lo)
            fills("v1", 0)
            fills("mk", 0, 1, 2, 3)
            fills("mv", 0, 1, 2, 3)

            pairs = AH // 2
            for s in range(pairs + 2):
                cols = slice(4 * s, 4 * s + 4)
                if s < pairs:
                    dve.wait_ge(b_mm, s + 1)
                    if s == 0:
                        dve.wait_ge(bias_loaded, 32)
                    own.mark(dve.scalar_tensor_tensor(out=sc[:, s % 2], in0=bank[:, 4:6, 0:CAUS], scalar=HD ** -0.5,
                                                      in1=mbias[:, 2 * s:2 * s + 2, :], op0=ALU.mult, op1=ALU.add))
                    own.wait()
                    dve.tensor_reduce(bstat[:, 0, 4 * s:4 * s + 2], sc[:, s % 2, :, 0:S], AX.X, ALU.max)
                    own.mark(dve.tensor_reduce(bstat[:, 0, 4 * s + 2:4 * s + 4], sc[:, s % 2, :, S:CAUS], AX.X, ALU.max))
                    own.wait()
                    dve.tensor_scalar(bstat[:, 1, cols], bstat[:, 0, cols], -1.0, None, ALU.mult).then_inc(b_neg, 1)
                if s >= 2:
                    p = s - 2
                    dve.wait_ge(b_hi, p + 1)
                    src = reversed_last(bank[:, 2 + p % 2, 0:S].rearrange("p (t n) -> p t n", n=P))
                    dve.tensor_tensor(actT_lo[:, p, :].rearrange("p (t n) -> p t n", n=P), src,
                                      actT_hi[:, p, :].bitcast(F32).rearrange("p (t n) -> p t n", n=P), ALU.subtract).then_inc(b_lo, 1)
                if s < pairs:
                    dve.wait_ge(b_exp, s + 1)
                    own.mark(dve.reciprocal(bstat[:, 3, cols], bstat[:, 2, cols]))
                    own.wait()
                    for seg, c0, c1 in ((0, 0, S), (2, S, CAUS)):
                        for a in range(2):
                            col = 4 * s + seg + a
                            ins = dve.tensor_scalar(sc[:, s % 2, a, c0:c1], sc[:, s % 2, a, c0:c1], bstat[:, 3, col:col + 1], None, ALU.mult)
                    ins.then_inc(b_norm, 1)
            fills("v1", 1)
            m_part("mo")
            update(3)
            fills("v1", 2, 3)
            turn(6, actT_hi, actT_lo)
            fills("q1", 0, 1, 2, 3)
            memory_attention(1)
            m_part("wo1")
            update(4)
            turn(7, actT_hi, actT_lo)
            lo_upto(U[("gu1", 0)] + 1)
            feed_forward(1)
            update(5)


def shape_constants():
    import numpy as np

    consts = np.zeros((P, C_END), np.float32)
    consts[:, C_ID:C_ID + P] = np.eye(P)
    consts[:, C_TRI:C_TRI + P] = np.triu(np.ones((P, P)))
    consts[:, C_TRI + P:C_TRI + S] = 1.0
    consts[:, C_CAUS:C_CAUS + P] = np.tril(np.full((P, P), NEG), -1)
    exact = BUCKETS // 2
    for i in range(S):
        n = S - 1 - i
        large = exact + int(math.log(max(n, exact) / exact) / math.log(MAX_DIST / exact) * (BUCKETS - exact) + 1e-9)
        consts[n if n < exact else min(large, BUCKETS - 1), C_HOT + i] = 1.0
    return consts


_INS = ["x", "mem", "mix_pre_g", "mix_post_g", "ssm_w_in", "ssm_conv_w", "ssm_conv_b", "ssm_dt_bias", "ssm_a_log",
        "ssm_d", "ssm_norm_g", "ssm_w_out", "kv_norm_g", "w_kv", "moba_w_q", "moba_w_o", "rel_bias", "mem_norm_g",
        "mem_pre_g", "mem_post_g", "mem_w_q", "mem_w_kv", "mem_w_o", "ffn_pre_g", "ffn_post_g", "ffn_w_gu", "ffn_w_down"]


def kernel(**inputs):
    import numpy as _np
    import concourse.bacc as _bacc
    from concourse import mybir as _mybir
    from concourse.bass_utils import run_bass_kernel_spmd as _run

    nc = _bacc.Bacc("TRN2", target_bir_lowering=False, num_devices=1)
    arrays = {f"in_{name}_dram": _np.ascontiguousarray(inputs[name]) for name in _INS}
    arrays["in_consts_dram"] = shape_constants()
    A = {}
    for name in _INS + ["consts"]:
        a = arrays[f"in_{name}_dram"]
        A[name] = nc.dram_tensor(f"in_{name}_dram", a.shape, _mybir.dt.from_np(a.dtype), kind="ExternalInput").ap()
    out = nc.dram_tensor("out_0_dram", (1, S, D), F32, kind="ExternalOutput").ap()
    program(nc, A, out)
    r = _run(nc, [arrays], core_ids=[0])
    return r.results[0]["out_0_dram"]
```

```python
import math
from contextlib import ExitStack

import concourse.bass as bass
from concourse import mybir

F32, F32R, BF16 = mybir.dt.float32, mybir.dt.float32r, mybir.dt.bfloat16
ALU = mybir.AluOpType
ACT = mybir.ActivationFunctionType
AX = mybir.AxisListType

P = 128
D = 1024
S = 256
ST = S // P
KD = D // P
EPS = 1e-6
DI = 2 * D
SSM_HEADS, SSM_GROUPS, NSTATE, HD = 32, 4, 128, 64
XT = DI // P
CONV = DI + 2 * SSM_GROUPS * NSTATE
CT = CONV // P
GT = XT // SSM_GROUPS
TAPS = 4
DFF = 2816
FT = DFF // P
AH = 16
MH = 4
BUCKETS, MAX_DIST = 32, 128
SLOTS = 4
UNIT = 2048
TC = UNIT // KD
MR = UNIT // D
NEG = -1e30
G_ROW, D_ROW = 32, 64
CAUS = P + S

C_ID, C_TRI, C_CAUS, C_HOT, C_END = 0, P, P + S, 2 * P + S, 2 * P + 2 * S

ORDER = [
    ("xbc", "T", CONV // TC), ("z", "T", DI // TC),
    ("k0", "T", 4), ("v0", "V", 4),
    ("w_out", "M", DI // P // MR),
    ("q0", "T", 4), ("wo0", "M", 4),
    ("gu0", "T", 2 * DFF // TC), ("down0", "M", FT // MR),
    ("mq", "T", 4), ("mk", "T", 4), ("mv", "V", 4), ("mo", "M", 4),
    ("k1", "T", 4), ("v1", "V", 4),
    ("q1", "T", 4), ("wo1", "M", 4),
    ("gu1", "T", 2 * DFF // TC), ("down1", "M", FT // MR),
]
PIECES = [
    ("xbc", 0, 12), ("z", 0, 8), ("k0", 0, 4), ("v0", 0, 2), ("w_out", 0, 8), ("v0", 2, 2),
    ("q0", 0, 4), ("wo0", 0, 4), ("k1", 0, 2), ("gu0", 0, 22), ("down0", 0, 11), ("k1", 2, 2),
    ("mq", 0, 4), ("v1", 0, 1), ("mk", 0, 4), ("mv", 0, 4), ("v1", 1, 1), ("mo", 0, 4), ("v1", 2, 2),
    ("q1", 0, 4), ("wo1", 0, 4), ("gu1", 0, 22), ("down1", 0, 11),
]
LAG = 2
CB_STEP = 1
SSD_FILLS = {1: ("k0", 0, 0), 3: ("k0", 0, 1), 4: ("k0", 1, 0), 6: ("k0", 1, 1), 7: ("k0", 2, 0), 9: ("k0", 2, 1),
             10: ("k0", 3, 0), 12: ("k0", 3, 1), 13: ("v0", 0, 0), 15: ("v0", 0, 1), 16: ("v0", 1, 0), 17: ("v0", 1, 1)}
KIND = {name: kind for name, kind, _ in ORDER}
U = {}
NAME_OF = []
for _name, _first, _count in PIECES:
    for _i in range(_first, _first + _count):
        U[(_name, _i)] = len(NAME_OF)
        NAME_OF.append((_name, _i))
NUNITS = len(NAME_OF)


def freed_by(name, i):
    if name == "params" or name == "xbc":
        return "dve"
    if name in ("gu0", "gu1"):
        return "dve" if i % 2 else "act"
    return "act"


BANKED = [("params", 0), ("dt", 0)] + [n for n in NAME_OF if KIND[n[0]] != "M"]
V_OF = {n: v for v, n in enumerate(BANKED)}
FREED = []
_n = {"act": 0, "dve": 0}
for _name, _i in BANKED:
    _e = freed_by(_name, _i)
    _n[_e] += 1
    FREED.append((_e, _n[_e]))


def reversed_last(ap):
    dims = [list(d) for d in ap.ap]
    step, n = dims[-1]
    dims[-1] = [-step, n]
    return bass.AP(ap.tensor, ap.offset + step * (n - 1), dims)


def program(nc, A, out):
    bias_rows = nc.dram_tensor("bias_rows", [AH, 3 * P], F32).ap()

    def row_tiles(w, k0, k, c0, c):
        return w[k0 * P:(k0 + k) * P, c0:c0 + c].rearrange("(k p) n -> p k n", p=P)

    w_in = A["ssm_w_in"][0]

    def unit_source(name, i):
        if name == "xbc":
            return row_tiles(w_in, 0, KD, DI + i * TC, TC)
        if name == "z":
            return row_tiles(w_in, 0, KD, i * TC, TC)
        if name in ("k0", "k1"):
            return row_tiles(A["mem_w_kv"][int(name[1])], 0, KD, i * TC, TC)
        if name in ("v0", "v1"):
            return row_tiles(A["mem_w_kv"][int(name[1])], 0, KD, D + i * TC, TC)
        if name in ("q0", "q1"):
            return row_tiles(A["mem_w_q"][int(name[1])], 0, KD, i * TC, TC)
        if name in ("gu0", "gu1"):
            return row_tiles(A["ffn_w_gu"][int(name[2])], 0, KD, (i % 2) * DFF + (i // 2) * TC, TC)
        if name == "mq":
            return row_tiles(A["moba_w_q"][0], 0, KD, i * TC, TC)
        if name == "mk":
            return row_tiles(A["w_kv"], 0, KD, i * TC, TC)
        if name == "mv":
            return row_tiles(A["w_kv"], 0, KD, D + i * TC, TC)
        w = {"w_out": A["ssm_w_out"][0], "wo0": A["mem_w_o"][0], "wo1": A["mem_w_o"][1], "mo": A["moba_w_o"][0],
             "down0": A["ffn_w_down"][0], "down1": A["ffn_w_down"][1]}[name]
        return row_tiles(w, i * MR, MR, 0, D)

    with ExitStack() as ctx:
        at = [16512]

        def place(name, shape, dtype, offset=None):
            size = math.prod(shape[1:]) * (2 if dtype == BF16 else 4)
            where = at[0] if offset is None else offset
            if offset is None:
                at[0] += -(-size // 32) * 32
            return nc.alloc_sbuf_tensor_at(name, shape, dtype, offset=where)

        def sem(name):
            return ctx.enter_context(nc.semaphore(name))

        hi = place("w_hi", [P, SLOTS, UNIT], F32R)
        raw_at = at[0]
        raw = place("w_raw", [P, SLOTS, UNIT], F32)
        lo = place("w_lo", [P, SLOTS, UNIT], F32R, raw_at)
        x = place("x", [P, ST, D], F32)
        actT_hi = place("actT_hi", [P, KD, S], F32R)
        actT_lo = place("actT_lo", [P, KD, S], F32R)
        memT_hi = place("memT_hi", [P, KD, S], F32R)
        memT_lo = place("memT_lo", [P, KD, S], F32R)
        at_memK = at[0]
        memK = place("memK", [P, KD, S], F32)
        memV = place("memV", [P, ST, D], F32)
        post_row = place("post_row", [P, D], F32)
        pre_row = place("pre_row", [P, D], F32)
        ntmp = place("ntmp", [P, ST, D], F32)
        const = place("const", [P, C_HOT], F32)
        hot = place("hot", [BUCKETS, S], F32, at_memK + 2048)
        brows = place("brows", [AH, 3 * P], F32, at_memK)
        stats = place("stats", [P, 6, 32], F32)
        gT = place("gT", [P, XT], F32)
        dT = place("dT", [P, XT], F32)
        small = place("small", [P, 8], F32)
        eps_col, one_col = small[:, 0:1], small[:, 1:2]
        phase = at[0]
        PHASE = 49152
        at[0] += PHASE
        scratch = at[0]

        z = place("z", [P, XT, S], F32, phase)
        xbc = place("xbc", [P, CT, S], F32, phase + 16384)
        y_lo = place("y_lo", [P, XT, S], F32R, phase)
        y_hi = place("y_hi", [P, XT, S], F32R, phase + 16384)
        cw = place("cw", [P, TAPS * CT + CT], F32, phase + 40960)
        dtw = place("dtw", [P, KD, SSM_HEADS], F32, phase + 41472)
        dtw_hi = place("dtw_hi", [P, KD, SSM_HEADS], F32R, phase + 42496)
        dtw_lo = place("dtw_lo", [P, KD, SSM_HEADS], F32R, phase + 43520)
        par_rows = place("par_rows", [P, 2, P], F32, phase + 44544)
        d_pair = place("d_pair", [P, 2], F32, phase + 46080)
        dt_row = place("dt_row", [P, 2, SSM_HEADS], F32, phase + 46112)
        dtc = place("dtc", [P, 8, ST, SSM_HEADS], F32, phase + 46368)
        cbT = place("cbT", [P, 2, CAUS], F32, phase + 40960)
        ycum = place("ycum", [P, 2, S], F32, phase + 44032)
        relb = place("relb", [BUCKETS, AH], F32, phase + 48416)
        mbias = place("mbias", [P, AH, CAUS], F32, phase)
        mqT = place("mqT", [P, KD, S], F32, phase + 24576)
        mkT = place("mkT", [P, KD, S], F32, phase + 32768)
        mV = place("mV", [P, ST, D], F32, phase + 40960)
        qT = place("qT", [P, KD, S], F32, phase)
        hT_hi = place("hT_hi", [P, FT, S], F32R, phase)
        hT_lo = place("hT_lo", [P, FT, S], F32R, phase + FT * S * 4)

        def shared(name, shape, dtype, offset):
            t = place(name, shape, dtype, scratch + offset)
            return t, offset + math.prod(shape[1:]) * (2 if dtype == BF16 else 4)

        conv_acc, o = shared("conv_acc", [P, 2, 2, S], F32, 0)
        xtok, o = shared("xtok", [P, 3, ST, P], F32, 0)
        decay, o = shared("decay", [P, 2, CAUS], F32, o)
        mt, o = shared("mt", [P, 6, CAUS], F32, o)
        mask_bf, o = shared("mask_bf", [P, P], BF16, max(o, 4096))
        id_bf, o = shared("id_bf", [P, P], BF16, o)
        id_r, o = shared("id_r", [P, SSM_HEADS], F32R, o)
        cumT_hi, o = shared("cumT_hi", [P, S], F32R, o)
        cumT_lo, o = shared("cumT_lo", [P, S], F32R, o)
        rs, o = shared("rs", [P, 2, S], F32, o)
        end_ssd = o
        prob, o = shared("prob", [P, 2, ST, S], F32, 0)
        probT, o = shared("probT", [P, 2, ST, S], F32, o)
        mstat, o = shared("mstat", [P, 4, ST * MH], F32, o)
        sc, o2 = shared("sc", [P, 2, 2, CAUS], F32, 0)
        scT, o2 = shared("scT", [P, 2, 2, CAUS], F32, o2)
        bstat, o2 = shared("bstat", [P, 4, 4 * AH // 2], F32, o2)
        gate, o3 = shared("gate", [P, 2, 2, S], F32, 0)
        hval, o3 = shared("hval", [P, 2, 2, S], F32, o3)
        top = scratch + max(end_ssd, o, o2, o3)
        assert top <= 229368, top

        bank = ctx.enter_context(nc.psum_tensor("bank", [P, 8, 512], F32))
        msum = [bank[:, 4 + 2 * t:6 + 2 * t, :].rearrange("p b n -> p (b n)") for t in range(ST)]

        w_loaded = [sem(f"w_loaded{s}") for s in range(SLOTS)]
        w_hi_done = sem("w_hi_done")
        w_lo_done = sem("w_lo_done")
        w_used = sem("w_used")
        m_half = sem("m_half")
        t_out = {"act": sem("t_out_act"), "dve": sem("t_out_dve")}
        act_step = sem("act_step")
        dve_step = sem("dve_step")
        x_loaded, mem_loaded = [sem(f"x_loaded{t}") for t in range(ST)], sem("mem_loaded")
        par_loaded, const_loaded, rows_loaded = sem("par_loaded"), sem("const_loaded"), sem("rows_loaded")
        pre_loaded, post_loaded = sem("pre_loaded"), sem("post_loaded")
        consts_made = sem("consts_made")
        eps_made = sem("eps_made")
        sum_ready = sem("sum_ready")
        stat_ready = sem("stat_ready")
        x_ready = sem("x_ready")
        u_ready = sem("u_ready")
        turned = sem("turned")
        turn_hi, turn_lo = sem("turn_hi"), sem("turn_lo")
        par_cleared = sem("par_cleared")
        par_turned = sem("par_turned")
        dtw_hi_done, dtw_lo_done, dt_mm = sem("dtw_hi_done"), sem("dtw_lo_done"), sem("dt_mm")
        dt_biased, dt_logged = sem("dt_biased"), sem("dt_logged")
        dt_ready, cum_mm, cum_hi, cum_ready = sem("dt_ready"), sem("cum_mm"), sem("cum_hi"), sem("cum_ready")
        brow_mm, brow_ready, brow_stored = sem("brow_mm"), sem("brow_ready"), sem("brow_stored")
        conv_first, conv_silu = sem("conv_first"), sem("conv_silu")
        cb_mm, cb_ready = sem("cb_mm"), sem("cb_ready")
        xtok_mm, xtok_ready = sem("xtok_mm"), sem("xtok_ready")
        row_mm, decay_ready, mt_ready = sem("row_mm"), sem("decay_ready"), sem("mt_ready")
        y_mm, y_ready, ysq_ready, ssq_mm, rs_ready = sem("y_mm"), sem("y_ready"), sem("ysq_ready"), sem("ssq_mm"), sem("rs_ready")
        yn_ready, y_hi_done, y_lo_done = sem("yn_ready"), sem("y_hi_done"), sem("y_lo_done")
        a_mm, a_neg, a_exp, a_norm = sem("a_mm"), sem("a_neg"), sem("a_exp"), sem("a_norm")
        a_turned, a_probT, a_out, a_hi, a_lo = sem("a_turned"), sem("a_probT"), sem("a_out"), sem("a_hi"), sem("a_lo")
        b_mm, b_neg, b_exp, b_norm = sem("b_mm"), sem("b_neg"), sem("b_exp"), sem("b_norm")
        b_turned, b_probT, b_out, b_hi, b_lo = sem("b_turned"), sem("b_probT"), sem("b_out"), sem("b_hi"), sem("b_lo")
        bias_loaded = sem("bias_loaded")
        h_hi, h_lo = sem("h_hi"), sem("h_lo")
        stored = sem("stored")

        class Own:

            def __init__(self, eng, s):
                self.eng, self.sem, self.n = eng, s, 0

            def mark(self, ins):
                ins.then_inc(self.sem, 1)
                self.n += 1

            def wait(self, i=0, per=0):
                self.eng.wait_ge(self.sem, self.n + i * per if per else self.n)

        TURN_GAIN = [A["mix_pre_g"][0], A["mem_norm_g"], A["mem_pre_g"][0], A["ffn_pre_g"][0],
                     A["mix_pre_g"][1], A["kv_norm_g"], A["mem_pre_g"][1], A["ffn_pre_g"][1]]
        POST_GAIN = [A["mix_post_g"][0], A["mem_post_g"][0], A["ffn_post_g"][0],
                     A["mix_post_g"][1], A["mem_post_g"][1], A["ffn_post_g"][1]]
        POST_TURN = [2, 3, 4, 6, 7, None]
        M_OF_POST = ["w_out", "wo0", "down0", "mo", "wo1", "down1"]

        def stat_col(n, t, after):
            return 4 + 4 * n + (2 * t + after if POST_TURN[n] is not None else t)

        def last_unit(name):
            return max(u for (n, _), u in U.items() if n == name)

        def units_ahead(n):
            last = last_unit(M_OF_POST[n])
            return last + (2 if last + 1 < NUNITS and NAME_OF[last + 1][0] == "gu1" else 3)

        def every_row(row):
            return bass.AP(row.tensor, row.offset, [[0, P]] + [list(d) for d in row.ap])

        block = ctx.enter_context(nc.Block())

        @block.sync
        def _(sp):
            def load(u, slot_out=None):
                name, i = NAME_OF[u]
                if u >= SLOTS:
                    sp.wait_ge(w_used, u - SLOTS + 1)
                src = unit_source(name, i)
                dst = raw[:, u % SLOTS, :].rearrange("p (k n) -> p k n", n=src.shape[-1])
                sp.dma_start(dst, src).then_inc(w_loaded[u % SLOTS], 16)

            for t in range(ST):
                sp.dma_start(x[:, t, :], A["x"][0, t * P:(t + 1) * P, :]).then_inc(x_loaded[t], 16)
            sp.dma_start(const[:], A["consts"][:, 0:C_HOT]).then_inc(const_loaded, 16)
            sp.wait_ge(par_cleared, 1)
            sp.dma_start(par_rows[0:TAPS * CT, 0, :], A["ssm_conv_w"][0].rearrange("k (c p) -> (k c) p", p=P)).then_inc(par_loaded, 16)
            sp.dma_start(par_rows[0:CT, 1, :], A["ssm_conv_b"][0].rearrange("(c p) -> c p", p=P)).then_inc(par_loaded, 16)
            sp.dma_start(par_rows[G_ROW:G_ROW + XT, 1, :], A["ssm_norm_g"][0].rearrange("(c p) -> c p", p=P)).then_inc(par_loaded, 16)
            sp.dma_start(d_pair[D_ROW:D_ROW + XT, :], A["ssm_d"][0].rearrange("(c e) -> c e", e=2)).then_inc(par_loaded, 16)
            sp.dma_start(dtw[:], row_tiles(w_in, 0, KD, DI + CONV, SSM_HEADS)).then_inc(par_loaded, 16)
            for u in range(NUNITS):
                load(u)
            for t in range(ST):
                sp.wait_ge(x_ready, 2 * len(POST_GAIN) - 1 + t)
                sp.dma_start(out[0, t * P:(t + 1) * P, :], x[:, t, :]).then_inc(stored, 16)
            sp.wait_ge(stored, 16 * ST)

        @block.gpsimd
        def _(pool):
            mem_t = A["mem"][0].rearrange("(t p) n -> p t n", p=P)
            pool.dma_start(pre_row[:], every_row(TURN_GAIN[0])).then_inc(pre_loaded, 16)
            pool.wait_ge(u_ready, 2)
            pool.dma_start(pre_row[:], every_row(TURN_GAIN[1])).then_inc(pre_loaded, 16)
            pool.dma_start(dt_row[:, 0, :], every_row(A["ssm_dt_bias"][0])).then_inc(rows_loaded, 16)
            pool.dma_start(dt_row[:, 1, :], every_row(A["ssm_a_log"][0])).then_inc(rows_loaded, 16)
            pool.dma_start(memV[:], mem_t).then_inc(mem_loaded, 16)
            pool.dma_start(hot[:], A["consts"][0:BUCKETS, C_HOT:C_END]).then_inc(rows_loaded, 16)
            pool.dma_start(relb[:], A["rel_bias"]).then_inc(rows_loaded, 16)
            pool.dma_start(post_row[:], every_row(POST_GAIN[0])).then_inc(post_loaded, 16)
            pool.wait_ge(brow_ready, 1)
            pool.dma_start(bias_rows, brows[:]).then_inc(brow_stored, 16)
            for n in range(6):
                turn = POST_TURN[n]
                if turn is not None:
                    pool.wait_ge(u_ready, 2 * turn)
                    pool.dma_start(pre_row[:], every_row(TURN_GAIN[turn])).then_inc(pre_loaded, 16)
                if n < 5:
                    pool.wait_ge(x_ready, 2 * n + 2)
                    pool.dma_start(post_row[:], every_row(POST_GAIN[n + 1])).then_inc(post_loaded, 16)
                if n == 2:
                    pool.wait_ge(u_ready, 10)
                    pool.dma_start(pre_row[:], every_row(TURN_GAIN[5])).then_inc(pre_loaded, 16)
                    pool.wait_ge(brow_stored, 16)
                    for pair in range(AH // 2):
                        pool.wait_ge(w_used, last_unit("down0") + 3 + pair)
                        heads = slice(2 * pair, 2 * pair + 2)
                        for c0, c, base in ((0, S, 0), (S, P, P)):
                            src = bass.AP(bias_rows.tensor, base + pair * 6 * P, [[1, P], [3 * P, 2], [1, c]])
                            pool.dma_start(mbias[:, heads, c0:c0 + c], src).then_inc(bias_loaded, 16)

        @block.tensor
        def _(pe):
            ident = const[:, C_ID:C_ID + P]
            tri_ones = const[:, C_TRI:C_TRI + S]

            def product(dst, passes, first, last):
                for n, (a, b) in enumerate(passes):
                    ins = pe.matmul(dst, a, b, start=first and n == 0, stop=last and n == len(passes) - 1,
                                    skip_group_check=True)
                return ins

            def t_unit(slot, b, act_hi, act_lo, halves=range(2)):
                for c in halves:
                    for k in range(KD):
                        cols = slice(k * TC + c * P, k * TC + (c + 1) * P)
                        wh, wl = hi[:, slot, cols], lo[:, slot, cols]
                        ins = product(bank[:, b, c * S:(c + 1) * S],
                                      [(wh, act_hi[:, k, :]), (wh, act_lo[:, k, :]), (wl, act_hi[:, k, :])],
                                      k == 0, k == KD - 1)
                return ins

            def v_unit(slot, b, act_hi, act_lo, halves=range(2)):
                for t in halves:
                    for k in range(KD):
                        cols = slice(k * TC, (k + 1) * TC)
                        ah, al = act_hi[:, k, t * P:(t + 1) * P], act_lo[:, k, t * P:(t + 1) * P]
                        ins = product(bank[:, b, t * TC:(t + 1) * TC],
                                      [(ah, hi[:, slot, cols]), (ah, lo[:, slot, cols]), (al, hi[:, slot, cols])],
                                      k == 0, k == KD - 1)
                return ins

            def banked(name, i, act_hi, act_lo):
                u, v = U[(name, i)], V_OF[(name, i)]
                e, n = FREED[v - 2]
                pe.wait_ge(t_out[e], n)
                pe.wait_ge(w_lo_done, u + 1)
                f = t_unit if KIND[name] == "T" else v_unit
                f(u % SLOTS, v % 2, act_hi, act_lo).then_inc(w_used, 1)

            def fill(name, *units):
                for i in units:
                    banked(name, i, memT_hi, memT_lo)

            def fill_half(name, i, half):
                u, v = U[(name, i)], V_OF[(name, i)]
                if half == 0:
                    e, n = FREED[v - 2]
                    pe.wait_ge(t_out[e], n)
                    pe.wait_ge(w_lo_done, u + 1)
                f = t_unit if KIND[name] == "T" else v_unit
                ins = f(u % SLOTS, v % 2, memT_hi, memT_lo, [half])
                if half:
                    ins.then_inc(w_used, 1)

            def loop_t(name, iters, free_of_slot):
                u0, v0 = U[(name, 0)], V_OF[(name, 0)]
                for v in (v0 - 2, v0 - 1):
                    e, n = FREED[v]
                    pe.wait_ge(t_out[e], n)
                with pe.Fori(0, iters) as i:
                    for j in range(5):
                        if j:
                            e, n = free_of_slot(j, i)
                            pe.wait_ge(t_out[e], n)
                        if j < 4:
                            pe.wait_ge(w_lo_done, i * 4 + (u0 + j + 1))
                            t_unit((u0 + j) % SLOTS, (v0 + j) % 2, actT_hi, actT_lo).then_inc(w_used, 1)

            def m_part(name, act_hi, act_lo, ready):
                n = last_unit(name) - U[(name, 0)] + 1
                steps = [(i, t) for i in range(n - 2) for t in range(ST)] + [(i, t) for t in range(ST) for i in (n - 2, n - 1)]
                for i, t in steps:
                    u = U[(name, i)]
                    if t == 0:
                        ready(i)
                        pe.wait_ge(w_lo_done, u + 1)
                    for r in range(MR):
                        k = i * MR + r
                        ah, al = act_hi[:, k, t * P:(t + 1) * P], act_lo[:, k, t * P:(t + 1) * P]
                        for half in range(2):
                            cols = slice(r * D + half * 512, r * D + half * 512 + 512)
                            wh, wl = hi[:, u % SLOTS, cols], lo[:, u % SLOTS, cols]
                            ins = product(bank[:, 4 + 2 * t + half, :], [(ah, wh), (ah, wl), (al, wh)],
                                          k == 0, k == n * MR - 1)
                    if t == ST - 1:
                        ins.then_inc(w_used, 1)
                    elif i == n - 1:
                        ins.then_inc(m_half, 1)

            def turn(k, name=None, i=0):
                if name:
                    fill(name, i)
                for t in range(ST):
                    if name and t:
                        fill_half(name, i + 1, 0)
                    pe.wait_ge(u_ready, 2 * k + t + 1)
                    for half in range(2):
                        for q in range(4):
                            c = (half * 4 + q) * P
                            ins = pe.transpose(bank[:, 4 + 2 * t + half, q * P:(q + 1) * P], ntmp[:, t, c:c + P], ident)
                        ins.then_inc(turned, 1)
                if name:
                    fill_half(name, i + 1, 1)

            def turn_done(k):
                pe.wait_ge(turn_lo, 4 * k + 4)

            pe.wait_ge(const_loaded, 16)
            pe.wait_ge(par_loaded, 80)
            pe.wait_ge(consts_made, 1)
            for r in range(2):
                ins = pe.transpose(bank[:, 0, r * P:(r + 1) * P], par_rows[:, r, :], ident)
            ins.then_inc(par_turned, 1)
            turn(0)
            turn_done(0)
            pe.wait_ge(dtw_lo_done, 1)
            for t in range(ST):
                for k in range(KD):
                    ah, al = actT_hi[:, k, t * P:(t + 1) * P], actT_lo[:, k, t * P:(t + 1) * P]
                    ins = product(bank[:, 1, t * SSM_HEADS:(t + 1) * SSM_HEADS],
                                  [(ah, dtw_hi[:, k, :]), (ah, dtw_lo[:, k, :]), (al, dtw_hi[:, k, :])],
                                  k == 0, k == KD - 1)
            ins.then_inc(dt_mm, 1)

            loop_t("xbc", 3, lambda j, i: ("dve", i * 4 + j))
            pe.wait_ge(dt_ready, 1)
            adt = dtc[:, 6]
            product(bank[:, 2, 0:32], [(tri_ones[:, 0:P], adt[:, 0, :])], True, True)
            product(bank[:, 2, 32:64], [(tri_ones[:, P:S], adt[:, 0, :]), (tri_ones[:, 0:P], adt[:, 1, :])], True, True)
            product(bank[0:SSM_HEADS, 3, 0:S], [(adt[:, 0, :], tri_ones)], True, False)
            product(bank[0:SSM_HEADS, 3, P:S], [(adt[:, 1, :], tri_ones[:, 0:P])], False, True).then_inc(cum_mm, 1)
            turn(1)
            loop_t("z", 2, lambda j, i: ("act", i * 4 + j))
            pe.wait_ge(rows_loaded, 64)
            pe.wait_ge(cum_ready, 1)
            product(bank[0:AH, 2, 0:S], [(relb[:], hot[:])], True, True).then_inc(brow_mm, 1)
            turn_done(1)

            pe.wait_ge(conv_silu, CT // 2)
            def ssd_y(j):
                g = j // GT
                for e in range(2):
                    h = 2 * j + e
                    pe.wait_ge(mt_ready, h + 1)
                    if e == 0:
                        if j >= 2:
                            pe.wait_ge(y_ready, j - 1)
                    rows = slice(e * HD, (e + 1) * HD)
                    pe.matmul(bank[rows, 3 + j % 2 * 3, 0:S], xtok[:, j % 3, 0, rows], mt[:, h % 6, 0:S],
                              start=True, stop=False, skip_group_check=True)
                    ins = pe.matmul(bank[rows, 3 + j % 2 * 3, P:S], xtok[:, j % 3, 1, rows], mt[:, h % 6, S:CAUS],
                                    start=False, stop=True, skip_group_check=True)
                ins.then_inc(y_mm, 1)

            def ssd_ssq(j):
                pe.wait_ge(ysq_ready, j + 1)
                if j % GT == 0 and j:
                    pe.wait_ge(rs_ready, j // GT)
                product(bank[:, 7, 0:S], [(tri_ones[:, P:S], ycum[:, j % 2, :])], j % GT == 0, j % GT == GT - 1).then_inc(ssq_mm, 1)

            def ssd_cb(g):
                Bt, Ct = xbc[:, XT + g, :], xbc[:, XT + SSM_GROUPS + g, :]
                product(bank[:, 2, 0:S], [(Bt[:, 0:P], Ct)], True, True)
                product(bank[:, 2, S:CAUS], [(Bt[:, P:S], Ct[:, P:S])], True, True).then_inc(cb_mm, 1)

            pe.wait_ge(brow_ready, 1)
            ssd_cb(0)
            for j in range(XT + LAG + 1):
                if j < XT:
                    g = j // GT
                    if j == 0 or j % GT == CB_STEP + 1 and g + 1 < SSM_GROUPS:
                        pe.wait_ge(cb_ready, g + 2 if j else 1)
                    if j:
                        pe.wait_ge(xtok_ready, j)
                    for t in range(ST):
                        ins = pe.transpose(bank[:, 2, t * P:(t + 1) * P], xbc[:, j, t * P:(t + 1) * P], ident)
                    ins.then_inc(xtok_mm, 1)
                    for e in range(2):
                        h = 2 * j + e
                        if h >= 2:
                            pe.wait_ge(decay_ready, h - 1)
                        one = id_r[:, h:h + 1].broadcast_to([P, P])
                        row = bank[:, 4 + h % 2, :]
                        for dst, l0, l1 in ((row[:, 0:S], 0, S), (row[:, S:CAUS], P, S)):
                            pe.matmul(dst, one, cumT_hi[:, l0:l1], start=True, stop=False, skip_group_check=True)
                            pe.matmul(dst, one, cumT_lo[:, l0:l1], start=False, stop=False, skip_group_check=True)
                            ins = pe.matmul(dst[:, 0:P], id_bf[:], mask_bf[:], start=False, stop=True, skip_group_check=True)
                        ins.then_inc(row_mm, 1)
                    if j % GT == CB_STEP and g + 1 < SSM_GROUPS:
                        pe.wait_ge(xtok_ready, j + 1)
                        ssd_cb(g + 1)
                    if j in SSD_FILLS:
                        fill_half(*SSD_FILLS[j])
                if LAG <= j < XT + LAG:
                    ssd_y(j - LAG)
                if j > LAG:
                    ssd_ssq(j - LAG - 1)
                if j >= XT and j in SSD_FILLS:
                    fill_half(*SSD_FILLS[j])

            pe.wait_ge(rs_ready, SSM_GROUPS)
            m_part("w_out", y_hi, y_lo, lambda i: pe.wait_ge(y_lo_done, i * MR // GT + 1))
            turn(2, "v0", 2)

            def memory_attention(layer):
                h0 = layer * MH
                for name in ("q", "k", "v"):
                    e, n = FREED[V_OF[(f"{name}{layer}", 3)]]
                    pe.wait_ge(t_out[e], n)
                for s in range(MH + 2):
                    if s < MH:
                        b = 4 + s % 2
                        if s >= 2:
                            pe.wait_ge(a_exp, h0 + s - 1)
                        for t in range(ST):
                            for kk in range(2):
                                ins = pe.matmul(bank[:, b, t * S:(t + 1) * S], qT[:, 2 * s + kk, t * P:(t + 1) * P],
                                                memK[:, 2 * s + kk, :], start=kk == 0, stop=kk == 1, skip_group_check=True)
                        ins.then_inc(a_mm, 1)
                    if 1 <= s <= MH:
                        h = s - 1
                        pe.wait_ge(a_norm, h0 + h + 1)
                        if h >= 2:
                            pe.wait_ge(a_probT, h0 + h - 1)
                        for m in range(ST):
                            for t in range(ST):
                                ins = pe.transpose(bank[:, 6 + h % 2, m * S + t * P:m * S + (t + 1) * P],
                                                   prob[:, h % 2, t, m * P:(m + 1) * P], ident)
                        ins.then_inc(a_turned, 1)
                    if s >= 2:
                        h = s - 2
                        pe.wait_ge(a_probT, h0 + h + 1)
                        if h >= 2:
                            pe.wait_ge(a_lo, h0 + h - 1)
                        for d in range(2):
                            for m in range(ST):
                                c = (2 * h + d) * P
                                ins = pe.matmul(bank[:, 2 + h % 2, d * S:(d + 1) * S], memV[:, m, c:c + P],
                                                probT[:, h % 2, m, :], start=m == 0, stop=m == 1, skip_group_check=True)
                        ins.then_inc(a_out, 1)

            def qkv(name):
                for i in range(4):
                    banked(name, i, actT_hi, actT_lo)

            def feed_forward(layer):
                name = f"gu{layer}"
                a0, d0 = FREED[V_OF[(name, 0)]][1] - 1, FREED[V_OF[(name, 1)]][1] - 1
                loop_t(name, 5, lambda j, i: (("act", "dve")[j % 2], i * 2 + ((a0, d0)[j % 2] + j // 2)))
                for i in (20, 21):
                    banked(name, i, actT_hi, actT_lo)
                m_part(f"down{layer}", hT_hi, hT_lo, lambda i: pe.wait_ge(h_lo, 11 * layer + i + 1))

            turn_done(2)
            qkv("q0")
            memory_attention(0)
            m_part("wo0", actT_hi, actT_lo, lambda i: pe.wait_ge(a_lo, i + 1))
            turn(3, "k1", 0)
            turn_done(3)
            feed_forward(0)
            turn(4, "k1", 2)
            turn_done(4)
            qkv("mq")
            turn(5)
            fill("v1", 0)
            turn_done(5)
            qkv("mk")
            qkv("mv")

            pairs = AH // 2
            e, n = FREED[V_OF[("mv", 3)]]
            pe.wait_ge(t_out[e], n)
            for s in range(pairs + 2):
                if s < pairs:
                    if s:
                        pe.wait_ge(b_neg, s)
                    for a in range(2):
                        rows = slice(a * HD, (a + 1) * HD)
                        pe.matmul(bank[:, 4 + a, 0:S], mqT[rows, s, P:S], mkT[rows, s, :], start=True, stop=True, skip_group_check=True)
                        ins = pe.matmul(bank[:, 4 + a, S:CAUS], mqT[rows, s, 0:P], mkT[rows, s, 0:P], start=True, stop=True, skip_group_check=True)
                    ins.then_inc(b_mm, 1)
                if 1 <= s <= pairs:
                    p = s - 1
                    pe.wait_ge(b_norm, p + 1)
                    if p:
                        pe.wait_ge(b_probT, p)
                    for a in range(2):
                        for n, c in enumerate((S, 0, P)):
                            ins = pe.transpose(bank[:, 6 + a, n * P:(n + 1) * P], sc[:, p % 2, a, c:c + P], ident)
                    ins.then_inc(b_turned, 1)
                if s >= 2:
                    p = s - 2
                    pe.wait_ge(b_probT, p + 1)
                    if p >= 2:
                        pe.wait_ge(b_lo, p - 1)
                    for a in range(2):
                        rows = slice(a * HD, (a + 1) * HD)
                        cols = slice((2 * p + a) * HD, (2 * p + a + 1) * HD)
                        pe.matmul(bank[rows, 2 + p % 2, 0:S], mV[:, 0, cols], scT[:, p % 2, a, 0:S], start=True, stop=False, skip_group_check=True)
                        ins = pe.matmul(bank[rows, 2 + p % 2, P:S], mV[:, 1, cols], scT[:, p % 2, a, S:CAUS], start=False, stop=True, skip_group_check=True)
                    ins.then_inc(b_out, 1)
            fill("v1", 1)
            m_part("mo", actT_hi, actT_lo, lambda i: pe.wait_ge(b_lo, 2 * i + 2))
            turn(6, "v1", 2)
            turn_done(6)
            qkv("q1")
            memory_attention(1)
            m_part("wo1", actT_hi, actT_lo, lambda i: pe.wait_ge(a_lo, MH + i + 1))
            turn(7)
            turn_done(7)
            feed_forward(1)

        @block.scalar
        def _(act):
            own = Own(act, act_step)
            done = [0]

            def hi_unit(u, i=0, per=0):
                count = 16 * (u // SLOTS + 1)
                act.wait_ge(w_loaded[u % SLOTS], i * 16 + count if per else count)
                act.activation(hi[:, u % SLOTS, :], raw[:, u % SLOTS, :], ACT.Copy).then_inc(w_hi_done, 1)

            def hi_upto(u):
                while done[0] <= min(u, NUNITS - 1):
                    hi_unit(done[0])
                    done[0] += 1

            def statistic(c, t, src):
                act.activation(ntmp[:, t, :], src, ACT.Square, accum_out=stats[:, 0, c:c + 1]).then_inc(sum_ready, 1)
                act.wait_ge(sum_ready, c + 1)
                own.mark(act.activation(stats[:, 1, c:c + 1], stats[:, 0, c:c + 1], ACT.Ln, bias=eps_col, scale=1.0 / D))
                own.wait()
                act.activation(stats[:, 2, c:c + 1], stats[:, 1, c:c + 1], ACT.Exp, scale=-0.5).then_inc(stat_ready, 1)

            def turn(k, dst):
                for t in range(ST):
                    for half in range(2):
                        act.wait_ge(turned, 4 * k + 2 * t + half + 1)
                        act.activation(dst[:, half * 4:half * 4 + 4, t * P:(t + 1) * P],
                                       bank[:, 4 + 2 * t + half, :].rearrange("p (q n) -> p q n", n=P),
                                       ACT.Copy).then_inc(turn_hi, 1)

            def tiles(b):
                return bank[:, b, :].rearrange("p (c n) -> p c n", n=S)

            def copy_out(name, i):
                u, v = U[(name, i)], V_OF[(name, i)]
                act.wait_ge(w_used, u + 1)
                src = tiles(v % 2)
                dst = {"mq": mqT, "mk": mkT, "mv": mV, "k0": memK, "k1": memK, "v0": memV, "v1": memV, "q0": qT, "q1": qT}[name]
                if name == "mq":
                    src = bank[:, v % 2, :].rearrange("p (c n) -> p c n", n=P)
                    dst = reversed_last(mqT[:].rearrange("p k (t n) -> p (k t) n", n=P)[:, 4 * i:4 * i + 4, :])
                elif KIND[name] == "V":
                    dst = dst[:, :, i * TC:(i + 1) * TC]
                else:
                    dst = dst[:, 2 * i:2 * i + 2, :]
                act.activation(dst, src, ACT.Copy).then_inc(t_out["act"], 1)

            def copies(name, *units):
                for i in units:
                    hi_upto(U[(name, i)] + 2)
                    copy_out(name, i)

            def m_part(name):
                hi_upto(last_unit(name) + 1)

            def norms(n):
                act.preload_act_table_set("natural_log_exp_and_others")
                last = last_unit(M_OF_POST[n])
                act.wait_ge(m_half, n + 1)
                statistic(stat_col(n, 0, 0), 0, msum[0])
                hi_upto(last + 2)
                if POST_TURN[n] is not None:
                    act.wait_ge(x_ready, 2 * n + 1)
                    statistic(stat_col(n, 0, 1), 0, x[:, 0, :])
                act.wait_ge(w_used, last + 1)
                statistic(stat_col(n, 1, 0), 1, msum[1])
                hi_upto(units_ahead(n))
                if POST_TURN[n] is not None:
                    act.wait_ge(x_ready, 2 * n + 2)
                    statistic(stat_col(n, 1, 1), 1, x[:, 1, :])

            act.preload_act_table_set("natural_log_exp_and_others")
            act.wait_ge(eps_made, 1)
            for t in range(ST):
                act.wait_ge(x_loaded[t], 16)
                statistic(t, t, x[:, t, :])
            act.wait_ge(par_loaded, 80)
            act.activation(dtw_hi[:], dtw[:], ACT.Copy).then_inc(dtw_hi_done, 1)
            turn(0, actT_hi)
            hi_upto(1)
            act.wait_ge(dt_mm, 1)
            act.activation(dtc[:, 0], bank[:, 1, 0:ST * SSM_HEADS].rearrange("p (t h) -> p t h", t=ST), ACT.Copy).then_inc(t_out["act"], 1)
            act.wait_ge(dt_biased, 1)
            own.mark(act.activation(dtc[:, 2], dtc[:, 1], ACT.Abs))
            own.wait()
            own.mark(act.activation(dtc[:, 3], dtc[:, 2], ACT.Exp, scale=-1.0))
            own.wait()
            act.activation(dtc[:, 4], dtc[:, 3], ACT.Ln, bias=one_col)
            act.activation(dt_row[:, 1, :], dt_row[:, 1, :], ACT.Exp).then_inc(dt_logged, 1)
            act.wait_ge(mem_loaded, 16)
            for t in range(ST):
                statistic(2 + t, t, memV[:, t, :])
            act.preload_act_table_set("silu_and_others")

            def silu_conv(i, j):
                act.wait_ge(t_out["dve"], i * 4 + (j + 2))
                act.activation(xbc[:, bass.ds(i * 8 + 2 * j, 2), :], conv_acc[:, j % 2], ACT.Silu).then_inc(conv_silu, 1)

            with act.Fori(0, 3) as i:
                for j in range(4):
                    hi_unit(2 + j, i, 4)
                    if j:
                        silu_conv(i, j - 1)
                    act.wait_ge(w_used, i * 4 + (j + 1))
                    for c in range(2):
                        ins = act.activation(conv_acc[:, j % 2, c, :], tiles(j % 2)[:, c, :], ACT.Identity,
                                             scale=cw[:, bass.ds(i * 8 + (3 * CT + 2 * j + c), 1)],
                                             bias=cw[:, bass.ds(i * 8 + (4 * CT + 2 * j + c), 1)])
                    ins.then_inc(conv_first, 1)
                silu_conv(i, 3)
            act.wait_ge(cum_mm, 1)
            act.activation(cumT_hi[0:SSM_HEADS, :], bank[0:SSM_HEADS, 3, 0:S], ACT.Copy).then_inc(cum_hi, 1)
            turn(1, memT_hi)
            with act.Fori(0, 2) as i:
                for j in range(4):
                    hi_unit(14 + j, i, 4)
                    act.wait_ge(w_used, i * 4 + (12 + j + 1))
                    act.activation(z[:, bass.ds(i * 8 + 2 * j, 2), :], tiles(j % 2), ACT.Silu).then_inc(t_out["act"], 1)
            done[0] = 22

            act.preload_act_table_set("natural_log_exp_and_others")
            def copy_cb(g):
                act.wait_ge(cb_mm, g + 1)
                act.activation(cbT[:, g % 2, :], bank[:, 2, 0:CAUS], ACT.Copy).then_inc(cb_ready, 1)

            copy_cb(0)
            for j in range(XT + LAG + 2):
                c = j - LAG
                if j < XT:
                    g = j // GT
                    act.wait_ge(xtok_mm, j + 1)
                    act.activation(xtok[:, j % 3], bank[:, 2, 0:S].rearrange("p (t n) -> p t n", n=P), ACT.Copy).then_inc(xtok_ready, 1)
                    for h in (2 * j, 2 * j + 1):
                        act.wait_ge(row_mm, h + 1)
                        if h >= 2:
                            act.wait_ge(mt_ready, h - 1)
                        row = bank[:, 4 + h % 2, :]
                        act.activation(decay[:, h % 2, 0:S], row[:, 0:S], ACT.Exp, bias=dtc[:, 7, 0, h:h + 1])
                        act.activation(decay[:, h % 2, S:CAUS], row[:, S:CAUS], ACT.Exp, bias=dtc[:, 7, 1, h:h + 1]).then_inc(decay_ready, 1)
                    if j % GT == CB_STEP and g + 1 < SSM_GROUPS:
                        copy_cb(g + 1)
                if 0 <= c < XT:
                    act.wait_ge(y_ready, c + 1)
                    if c >= 2:
                        act.wait_ge(ssq_mm, c - 1)
                    act.activation(ycum[:, c % 2, :], z[:, c, :], ACT.Square).then_inc(ysq_ready, 1)
                if c > 0 and c % GT == 0:
                    act.wait_ge(ssq_mm, c)
                    own.mark(act.activation(rs[:, 0, :], bank[:, 7, 0:S], ACT.Ln, bias=eps_col, scale=1.0 / (GT * P)))
                    own.wait()
                    act.activation(rs[:, 1, :], rs[:, 0, :], ACT.Exp, scale=-0.5).then_inc(rs_ready, 1)
                if c > 1 and c % GT == 1:
                    g = c // GT - 1
                    act.wait_ge(yn_ready, g + 1)
                    act.activation(y_hi[:, g * GT:(g + 1) * GT, :], z[:, g * GT:(g + 1) * GT, :], ACT.Copy).then_inc(y_hi_done, 1)
                if j in SSD_FILLS:
                    name, i, half = SSD_FILLS[j]
                    if half == 0:
                        hi_upto(U[(name, i)] + 2)
                    else:
                        if name == "k0" and i == 0:
                            act.wait_ge(brow_stored, 16)
                        copy_out(name, i)

            m_part("w_out")
            norms(0)
            copy_out("v0", 2)
            turn(2, actT_hi)
            copy_out("v0", 3)

            def memory_attention(layer):
                for s in range(MH + 2):
                    if s < MH:
                        n, b = layer * MH + s, 4 + s % 2
                        act.wait_ge(a_neg, n + 1)
                        for t in range(ST):
                            col = 2 * s + t
                            ins = act.activation(prob[:, s % 2, t, :], bank[:, b, t * S:(t + 1) * S], ACT.Exp,
                                                 bias=mstat[:, 1, col:col + 1], scale=(D // MH) ** -0.5,
                                                 accum_out=mstat[:, 2, col:col + 1])
                        ins.then_inc(a_exp, 1)
                    if 1 <= s <= MH:
                        act.wait_ge(a_turned, layer * MH + s)
                        act.activation(probT[:, (s - 1) % 2], tiles(6 + (s - 1) % 2), ACT.Copy).then_inc(a_probT, 1)
                    if s >= 2:
                        h = s - 2
                        act.wait_ge(a_out, layer * MH + h + 1)
                        act.activation(actT_hi[:, 2 * h:2 * h + 2, :], tiles(2 + h % 2), ACT.Copy).then_inc(a_hi, 1)

            def feed_forward(layer):
                name = f"gu{layer}"
                u0, v0 = U[(name, 0)], V_OF[(name, 0)]
                a0, d0 = FREED[v0][1] - 1, FREED[v0 + 1][1] - 1
                act.preload_act_table_set("silu_and_others")

                def unit(j, i, per, tile):
                    hi_unit(u0 + 2 + j, i, per)
                    act.wait_ge(w_used, i * 4 + (u0 + j + 1) if per else u0 + j + 1)
                    if j % 2 == 0:
                        act.activation(gate[:, j // 2 % 2], tiles((v0 + j) % 2), ACT.Silu).then_inc(t_out["act"], 1)
                    else:
                        act.wait_ge(t_out["dve"], i * 2 + (d0 + j // 2 + 1) if per else d0 + j // 2 + 1)
                        act.activation(hT_hi[:, tile, :], hval[:, j // 2 % 2], ACT.Copy).then_inc(h_hi, 1)

                with act.Fori(0, 5) as i:
                    for j in range(4):
                        unit(j, i, 4, bass.ds(i * 4 + j // 2 * 2, 2))
                for j in (20, 21):
                    unit(j, 0, 0, slice(FT - 2, FT))
                done[0] = u0 + 24
                m_part(f"down{layer}")

            copies("q0", 0, 1, 2, 3)
            memory_attention(0)
            m_part("wo0")
            norms(1)
            copy_out("k1", 0)
            turn(3, actT_hi)
            copy_out("k1", 1)
            hi_upto(U[("gu0", 0)] + 1)
            feed_forward(0)
            norms(2)
            copy_out("k1", 2)
            turn(4, actT_hi)
            copy_out("k1", 3)
            copies("mq", 0, 1, 2, 3)
            turn(5, actT_hi)
            copies("v1", 0)
            copies("mk", 0, 1, 2, 3)
            copies("mv", 0, 1, 2, 3)
            pairs = AH // 2
            for s in range(pairs + 2):
                if s < pairs:
                    act.wait_ge(b_neg, s + 1)
                    for seg, c0, c1 in ((0, 0, S), (2, S, CAUS)):
                        for a in range(2):
                            col = 4 * s + seg + a
                            ins = act.activation(sc[:, s % 2, a, c0:c1], sc[:, s % 2, a, c0:c1], ACT.Exp,
                                                 bias=bstat[:, 1, col:col + 1], accum_out=bstat[:, 2, col:col + 1])
                    ins.then_inc(b_exp, 1)
                if 1 <= s <= pairs:
                    act.wait_ge(b_turned, s)
                    act.activation(scT[:, (s - 1) % 2], bank[:, 6:8, 0:CAUS], ACT.Copy).then_inc(b_probT, 1)
                if s >= 2:
                    p = s - 2
                    act.wait_ge(b_out, p + 1)
                    src = reversed_last(bank[:, 2 + p % 2, 0:S].rearrange("p (t n) -> p t n", n=P))
                    act.activation(actT_hi[:, p, :].rearrange("p (t n) -> p t n", n=P), src, ACT.Copy).then_inc(b_hi, 1)
            copies("v1", 1)
            m_part("mo")
            norms(3)
            copy_out("v1", 2)
            turn(6, actT_hi)
            copy_out("v1", 3)
            copies("q1", 0, 1, 2, 3)
            memory_attention(1)
            m_part("wo1")
            norms(4)
            turn(7, actT_hi)
            hi_upto(U[("gu1", 0)] + 1)
            feed_forward(1)
            norms(5)

        @block.vector
        def _(dve):
            own = Own(dve, dve_step)
            done = [0]

            def lo_unit(u, i=0, per=0):
                dve.wait_ge(w_hi_done, i * 4 + (u + 1) if per else u + 1)
                s = u % SLOTS
                dve.tensor_tensor(lo[:, s, :], raw[:, s, :], hi[:, s, :].bitcast(F32), ALU.subtract).then_inc(w_lo_done, 1)

            def lo_upto(u):
                while done[0] <= min(u, NUNITS - 1):
                    lo_unit(done[0])
                    done[0] += 1

            def tiles(b):
                return bank[:, b, :].rearrange("p (c n) -> p c n", n=S)

            def inverse_rms(c):
                total, _, r, v, step, result = [stats[:, n, c:c + 1] for n in range(6)]
                dve.wait_ge(sum_ready, c + 1)
                own.mark(dve.tensor_scalar(v, total, -0.5 / D, -0.5 * EPS, ALU.mult, ALU.add))
                own.wait()
                dve.wait_ge(stat_ready, c + 1)
                own.mark(dve.scalar_tensor_tensor(out=step, in0=r, scalar=v, in1=r, op0=ALU.mult, op1=ALU.mult))
                own.wait()
                own.mark(dve.tensor_scalar(result, step, 1.5, r, ALU.add, ALU.mult))
                own.wait()

            def normalise(k, c, t, src, fresh=True):
                if fresh:
                    inverse_rms(c)
                if t == 0:
                    dve.wait_ge(pre_loaded, 16 * (k + 1))
                dve.scalar_tensor_tensor(out=ntmp[:, t, :], in0=src[:, t, :], scalar=stats[:, 5, c:c + 1],
                                         in1=pre_row[:], op0=ALU.mult, op1=ALU.mult).then_inc(u_ready, 1)

            def turn(k, dst_hi, dst_lo):
                for t in range(ST):
                    for half in range(2):
                        dve.wait_ge(turn_hi, 4 * k + 2 * t + half + 1)
                        part = (slice(None), slice(half * 4, half * 4 + 4), slice(t * P, (t + 1) * P))
                        dve.tensor_tensor(dst_lo[part], bank[:, 4 + 2 * t + half, :].rearrange("p (q n) -> p q n", n=P),
                                          dst_hi[part].bitcast(F32), ALU.subtract).then_inc(turn_lo, 1)

            def m_part(name):
                lo_upto(last_unit(name) + 1)

            def update(n):
                for t in range(ST):
                    c = stat_col(n, t, 0)
                    inverse_rms(c)
                    if t == 0:
                        dve.wait_ge(post_loaded, 16 * (n + 1))
                    own.mark(dve.scalar_tensor_tensor(out=ntmp[:, t, :], in0=msum[t], scalar=stats[:, 5, c:c + 1],
                                                      in1=post_row[:], op0=ALU.mult, op1=ALU.mult))
                    own.wait()
                    dve.tensor_tensor(x[:, t, :], x[:, t, :], ntmp[:, t, :], ALU.add).then_inc(x_ready, 1)
                    lo_upto(units_ahead(n) if t else last_unit(M_OF_POST[n]) + 2)
                    if POST_TURN[n] is not None:
                        normalise(POST_TURN[n], stat_col(n, t, 1), t, x)

            def fills(name, *units):
                for i in units:
                    lo_upto(U[(name, i)] + 2)

            dve.memset(par_rows[:], 0.0).then_inc(par_cleared, 1)
            dve.memset(one_col, 1.0)
            dve.memset(eps_col, EPS).then_inc(eps_made, 1)
            own.mark(dve.memset(cumT_hi[:].bitcast(F32), 0.0))
            own.mark(dve.memset(cumT_lo[:].bitcast(F32), 0.0))
            dve.wait_ge(par_loaded, 80)
            dve.wait_ge(const_loaded, 16)
            dve.tensor_copy(id_bf[:], const[:, C_ID:C_ID + P])
            dve.tensor_copy(mask_bf[:], const[:, C_CAUS:C_CAUS + P])
            dve.tensor_copy(id_r[:], const[:, C_ID:C_ID + SSM_HEADS])
            d_rows = slice(D_ROW, D_ROW + XT)
            dve.tensor_copy(par_rows[d_rows, 1, :].rearrange("c (e n) -> c e n", e=2), d_pair[d_rows, :].unsqueeze(2).broadcast_to([XT, 2, HD])).then_inc(consts_made, 1)
            for t in range(ST):
                normalise(0, t, t, x)
            dve.wait_ge(dtw_hi_done, 1)
            dve.tensor_tensor(dtw_lo[:], dtw[:], dtw_hi[:].bitcast(F32), ALU.subtract).then_inc(dtw_lo_done, 1)
            turn(0, actT_hi, actT_lo)
            dve.wait_ge(par_turned, 1)
            dve.tensor_copy(cw[:, 0:TAPS * CT], bank[:, 0, 0:TAPS * CT])
            dve.tensor_copy(cw[:, TAPS * CT:TAPS * CT + CT], bank[:, 0, P:P + CT])
            dve.tensor_copy(gT[:], bank[:, 0, P + G_ROW:P + G_ROW + XT])
            dve.tensor_copy(dT[:], bank[:, 0, P + D_ROW:P + D_ROW + XT]).then_inc(t_out["dve"], 1)
            lo_upto(1)
            dve.wait_ge(t_out["act"], 1)
            dve.wait_ge(rows_loaded, 64)
            own.mark(dve.memset(brows[:, S:3 * P], NEG))
            bias_row = dt_row[:, 0:1, :].broadcast_to([P, ST, SSM_HEADS])
            dve.tensor_tensor(dtc[:, 1], dtc[:, 0], bias_row, ALU.add).then_inc(dt_biased, 1)
            dve.wait_ge(dt_logged, 1)
            own.mark(dve.tensor_scalar(dtc[:, 5], dtc[:, 3], 1.0, None, ALU.add))
            own.wait()
            own.mark(dve.tensor_scalar(dtc[:, 6], dtc[:, 5], 1.0, None, ALU.subtract))
            own.wait()
            own.mark(dve.tensor_tensor(dtc[:, 6], dtc[:, 3], dtc[:, 6], ALU.subtract))
            own.mark(dve.reciprocal(dtc[:, 2], dtc[:, 5]))
            own.wait()
            own.mark(dve.tensor_tensor(dtc[:, 6], dtc[:, 6], dtc[:, 2], ALU.mult))
            own.wait()
            own.mark(dve.tensor_tensor(dtc[:, 6], dtc[:, 6], dtc[:, 4], ALU.add))
            own.wait()
            own.mark(dve.scalar_tensor_tensor(out=dtc[:, 5], in0=dtc[:, 1], scalar=0.0, in1=dtc[:, 6], op0=ALU.max, op1=ALU.add))
            own.wait()
            exp_a = dt_row[:, 1:2, :].broadcast_to([P, ST, SSM_HEADS])
            dve.scalar_tensor_tensor(out=dtc[:, 6], in0=dtc[:, 5], scalar=-1.0, in1=exp_a, op0=ALU.mult, op1=ALU.mult).then_inc(dt_ready, 1)
            for t in range(ST):
                normalise(1, 2 + t, t, memV)

            with dve.Fori(0, 3) as i:
                n0 = own.n
                per = 8
                for j in range(4):
                    lo_unit(2 + j, i, 4)
                    dve.wait_ge(conv_first, i * 4 + (j + 1))
                    for tap in (2, 1, 0):
                        back = TAPS - 1 - tap
                        if tap < 2:
                            own.wait(i, per)
                        for c in range(2):
                            acc = conv_acc[:, j % 2, c, back:S]
                            ins = dve.scalar_tensor_tensor(out=acc, in0=tiles(j % 2)[:, c, 0:S - back],
                                                           scalar=cw[:, bass.ds(i * 8 + (tap * CT + 2 * j + c), 1)],
                                                           in1=acc, op0=ALU.mult, op1=ALU.add)
                        if tap:
                            own.mark(ins)
                        else:
                            ins.then_inc(t_out["dve"], 1)
                assert own.n - n0 == per
            own.n += 2 * per
            done[0] = 14
            dve.wait_ge(cum_mm, 1)
            own.mark(dve.tensor_scalar(dtc[:, 7], bank[:, 2, 0:ST * SSM_HEADS].rearrange("p (t h) -> p t h", t=ST), -1.0, None, ALU.mult))
            dve.wait_ge(cum_hi, 1)
            dve.tensor_tensor(cumT_lo[0:SSM_HEADS, :], bank[0:SSM_HEADS, 3, 0:S], cumT_hi[0:SSM_HEADS, :].bitcast(F32), ALU.subtract).then_inc(cum_ready, 1)
            turn(1, memT_hi, memT_lo)
            with dve.Fori(0, 2) as i:
                for j in range(4):
                    lo_unit(14 + j, i, 4)
            done[0] = 22
            dve.wait_ge(brow_mm, 1)
            dve.tensor_copy(brows[:, 0:S], bank[0:AH, 2, 0:S]).then_inc(brow_ready, 1)

            dve.wait_ge(t_out["act"], FREED[V_OF[("z", 7)]][1])
            for j in range(XT + LAG + 2):
                c = j - LAG
                if j < XT:
                    g = j // GT
                    if j % GT == 0:
                        dve.wait_ge(cb_ready, g + 1)
                    if j >= 3:
                        dve.wait_ge(y_mm, j - 2)
                    for h in (2 * j, 2 * j + 1):
                        dve.wait_ge(decay_ready, h + 1)
                        for t, c0, c1 in ((0, 0, S), (1, S, CAUS)):
                            ins = dve.scalar_tensor_tensor(out=mt[:, h % 6, c0:c1], in0=decay[:, h % 2, c0:c1],
                                                           scalar=dtc[:, 5, t, h:h + 1], in1=cbT[:, g % 2, c0:c1],
                                                           op0=ALU.mult, op1=ALU.mult)
                        ins.then_inc(mt_ready, 1)
                if 0 <= c < XT:
                    dve.wait_ge(y_mm, c + 1)
                    own.mark(dve.scalar_tensor_tensor(out=xbc[:, c, :], in0=xbc[:, c, :], scalar=dT[:, c:c + 1],
                                                      in1=bank[:, 3 + c % 2 * 3, 0:S], op0=ALU.mult, op1=ALU.add))
                    own.wait()
                    dve.tensor_tensor(z[:, c, :], z[:, c, :], xbc[:, c, :], ALU.mult).then_inc(y_ready, 1)
                if c > 0 and c % GT == 0:
                    g = c // GT - 1
                    dve.wait_ge(rs_ready, g + 1)
                    dve.wait_ge(y_ready, GT * (g + 1))
                    for k in range(g * GT, (g + 1) * GT):
                        ins = dve.scalar_tensor_tensor(out=z[:, k, :], in0=z[:, k, :], scalar=gT[:, k:k + 1],
                                                       in1=rs[:, 1, :], op0=ALU.mult, op1=ALU.mult)
                    ins.then_inc(yn_ready, 1)
                if c > 1 and c % GT == 1:
                    g = c // GT - 1
                    group = slice(g * GT, (g + 1) * GT)
                    dve.wait_ge(y_hi_done, g + 1)
                    dve.tensor_tensor(y_lo[:, group, :], z[:, group, :], y_hi[:, group, :].bitcast(F32), ALU.subtract).then_inc(y_lo_done, 1)
                if j in SSD_FILLS and SSD_FILLS[j][2] == 0:
                    fills(*SSD_FILLS[j][0:2])
            m_part("w_out")
            update(0)
            turn(2, actT_hi, actT_lo)

            def memory_attention(layer):
                scale = (D // MH) ** -0.5
                for s in range(MH + 2):
                    n = layer * MH + s
                    cols = slice(2 * s, 2 * s + 2)
                    if s < MH:
                        dve.wait_ge(a_mm, n + 1)
                        own.mark(dve.tensor_reduce(mstat[:, 0, cols], tiles(4 + s % 2), AX.X, ALU.max))
                        own.wait()
                        dve.tensor_scalar(mstat[:, 1, cols], mstat[:, 0, cols], -scale, None, ALU.mult).then_inc(a_neg, 1)
                    if s >= 2:
                        h = s - 2
                        dve.wait_ge(a_hi, layer * MH + h + 1)
                        dve.tensor_tensor(actT_lo[:, 2 * h:2 * h + 2, :], tiles(2 + h % 2),
                                          actT_hi[:, 2 * h:2 * h + 2, :].bitcast(F32), ALU.subtract).then_inc(a_lo, 1)
                    if s < MH:
                        dve.wait_ge(a_exp, n + 1)
                        own.mark(dve.reciprocal(mstat[:, 3, cols], mstat[:, 2, cols]))
                        own.wait()
                        for t in range(ST):
                            ins = dve.tensor_scalar(prob[:, s % 2, t, :], prob[:, s % 2, t, :], mstat[:, 3, 2 * s + t:2 * s + t + 1], None, ALU.mult)
                        ins.then_inc(a_norm, 1)

            def feed_forward(layer):
                name = f"gu{layer}"
                u0, v0 = U[(name, 0)], V_OF[(name, 0)]
                a0 = FREED[v0][1] - 1
                h0 = (FT // 2) * layer

                def unit(j, i, per, tile):
                    lo_unit(u0 + 2 + j, i, per)
                    if j % 2:
                        b = j // 2 % 2
                        dve.wait_ge(w_used, i * 4 + (u0 + j + 1) if per else u0 + j + 1)
                        dve.wait_ge(t_out["act"], i * 2 + (a0 + j // 2 + 1) if per else a0 + j // 2 + 1)
                        dve.tensor_tensor(hval[:, b], tiles((v0 + j) % 2), gate[:, b], ALU.mult).then_inc(t_out["dve"], 1)
                        dve.wait_ge(h_hi, i * 2 + (h0 + j // 2 + 1) if per else h0 + j // 2 + 1)
                        dve.tensor_tensor(hT_lo[:, tile, :], hval[:, b], hT_hi[:, tile, :].bitcast(F32), ALU.subtract).then_inc(h_lo, 1)

                with dve.Fori(0, 5) as i:
                    for j in range(4):
                        unit(j, i, 4, bass.ds(i * 4 + j // 2 * 2, 2))
                for j in (20, 21):
                    unit(j, 0, 0, slice(FT - 2, FT))
                done[0] = u0 + 24
                m_part(f"down{layer}")

            fills("q0", 0, 1, 2, 3)
            memory_attention(0)
            m_part("wo0")
            update(1)
            turn(3, actT_hi, actT_lo)
            lo_upto(U[("gu0", 0)] + 1)
            feed_forward(0)
            update(2)
            turn(4, actT_hi, actT_lo)
            for t in range(ST):
                normalise(5, stat_col(2, t, 1), t, x, fresh=False)
            fills("mq", 0, 1, 2, 3)
            turn(5, actT_hi, actT_lo)
            fills("v1", 0)
            fills("mk", 0, 1, 2, 3)
            fills("mv", 0, 1, 2, 3)

            pairs = AH // 2
            for s in range(pairs + 2):
                cols = slice(4 * s, 4 * s + 4)
                if s < pairs:
                    dve.wait_ge(b_mm, s + 1)
                    if s == 0:
                        dve.wait_ge(bias_loaded, 16 * AH)
                    own.mark(dve.scalar_tensor_tensor(out=sc[:, s % 2], in0=bank[:, 4:6, 0:CAUS], scalar=HD ** -0.5,
                                                      in1=mbias[:, 2 * s:2 * s + 2, :], op0=ALU.mult, op1=ALU.add))
                    own.wait()
                    dve.tensor_reduce(bstat[:, 0, 4 * s:4 * s + 2], sc[:, s % 2, :, 0:S], AX.X, ALU.max)
                    own.mark(dve.tensor_reduce(bstat[:, 0, 4 * s + 2:4 * s + 4], sc[:, s % 2, :, S:CAUS], AX.X, ALU.max))
                    own.wait()
                    dve.tensor_scalar(bstat[:, 1, cols], bstat[:, 0, cols], -1.0, None, ALU.mult).then_inc(b_neg, 1)
                if s >= 2:
                    p = s - 2
                    dve.wait_ge(b_hi, p + 1)
                    src = reversed_last(bank[:, 2 + p % 2, 0:S].rearrange("p (t n) -> p t n", n=P))
                    dve.tensor_tensor(actT_lo[:, p, :].rearrange("p (t n) -> p t n", n=P), src,
                                      actT_hi[:, p, :].bitcast(F32).rearrange("p (t n) -> p t n", n=P), ALU.subtract).then_inc(b_lo, 1)
                if s < pairs:
                    dve.wait_ge(b_exp, s + 1)
                    own.mark(dve.reciprocal(bstat[:, 3, cols], bstat[:, 2, cols]))
                    own.wait()
                    for seg, c0, c1 in ((0, 0, S), (2, S, CAUS)):
                        for a in range(2):
                            col = 4 * s + seg + a
                            ins = dve.tensor_scalar(sc[:, s % 2, a, c0:c1], sc[:, s % 2, a, c0:c1], bstat[:, 3, col:col + 1], None, ALU.mult)
                    ins.then_inc(b_norm, 1)
            fills("v1", 1)
            m_part("mo")
            update(3)
            turn(6, actT_hi, actT_lo)
            fills("q1", 0, 1, 2, 3)
            memory_attention(1)
            m_part("wo1")
            update(4)
            turn(7, actT_hi, actT_lo)
            lo_upto(U[("gu1", 0)] + 1)
            feed_forward(1)
            update(5)


def shape_constants():
    import numpy as np

    consts = np.zeros((P, C_END), np.float32)
    consts[:, C_ID:C_ID + P] = np.eye(P)
    consts[:, C_TRI:C_TRI + P] = np.triu(np.ones((P, P)))
    consts[:, C_TRI + P:C_TRI + S] = 1.0
    consts[:, C_CAUS:C_CAUS + P] = np.tril(np.full((P, P), NEG), -1)
    exact = BUCKETS // 2
    for i in range(S):
        n = S - 1 - i
        large = exact + int(math.log(max(n, exact) / exact) / math.log(MAX_DIST / exact) * (BUCKETS - exact) + 1e-9)
        consts[n if n < exact else min(large, BUCKETS - 1), C_HOT + i] = 1.0
    return consts


_INS = ["x", "mem", "mix_pre_g", "mix_post_g", "ssm_w_in", "ssm_conv_w", "ssm_conv_b", "ssm_dt_bias", "ssm_a_log",
        "ssm_d", "ssm_norm_g", "ssm_w_out", "kv_norm_g", "w_kv", "moba_w_q", "moba_w_o", "rel_bias", "mem_norm_g",
        "mem_pre_g", "mem_post_g", "mem_w_q", "mem_w_kv", "mem_w_o", "ffn_pre_g", "ffn_post_g", "ffn_w_gu", "ffn_w_down"]


def kernel(**inputs):
    import numpy as _np
    import concourse.bacc as _bacc
    from concourse import mybir as _mybir
    from concourse.bass_utils import run_bass_kernel_spmd as _run

    nc = _bacc.Bacc("TRN2", target_bir_lowering=False, num_devices=1)
    arrays = {f"in_{name}_dram": _np.ascontiguousarray(inputs[name]) for name in _INS}
    arrays["in_consts_dram"] = shape_constants()
    A = {}
    for name in _INS + ["consts"]:
        a = arrays[f"in_{name}_dram"]
        A[name] = nc.dram_tensor(f"in_{name}_dram", a.shape, _mybir.dt.from_np(a.dtype), kind="ExternalInput").ap()
    out = nc.dram_tensor("out_0_dram", (1, S, D), F32, kind="ExternalOutput").ap()
    program(nc, A, out)
    r = _run(nc, [arrays], core_ids=[0])
    return r.results[0]["out_0_dram"]
```

```python
import math
from contextlib import ExitStack

import concourse.bass as bass
from concourse import mybir

F32, F32R, BF16 = mybir.dt.float32, mybir.dt.float32r, mybir.dt.bfloat16
ALU = mybir.AluOpType
ACT = mybir.ActivationFunctionType
AX = mybir.AxisListType

P = 128
D = 1024
S = 256
ST = S // P
KD = D // P
EPS = 1e-6
DI = 2 * D
SSM_HEADS, SSM_GROUPS, NSTATE, HD = 32, 4, 128, 64
XT = DI // P
CONV = DI + 2 * SSM_GROUPS * NSTATE
CT = CONV // P
GT = XT // SSM_GROUPS
TAPS = 4
DFF = 2816
FT = DFF // P
AH = 16
MH = 4
BUCKETS, MAX_DIST = 32, 128
SLOTS = 4
UNIT = 2048
TC = UNIT // KD
MR = UNIT // D
NEG = -1e30
G_ROW, D_ROW = 32, 64
CAUS = P + S

C_ID, C_TRI, C_CAUS, C_HOT, C_END = 0, P, P + S, 2 * P + S, 2 * P + 2 * S

MOBA_UNITS = [(name, i) for i in range(D // TC) for name in ("mk", "mv")]
KIND = {"xbc": "T", "z": "T", "w_out": "M", "k0": "T", "v0": "V", "q0": "T", "wo0": "M", "gu0": "T", "down0": "M",
        "mq": "T", "mk": "T", "mv": "V", "mo": "M", "k1": "T", "v1": "V", "q1": "T", "wo1": "M", "gu1": "T", "down1": "M"}
PIECES = [
    ("xbc", 0, CONV // TC), ("z", 0, DI // TC), ("k0", 0, D // TC), ("v0", 0, 2), ("w_out", 0, XT // MR), ("v0", 2, 2),
    ("q0", 0, D // TC), ("wo0", 0, KD // MR), ("k1", 0, 2), ("gu0", 0, 2 * DFF // TC), ("down0", 0, FT // MR), ("k1", 2, 2),
    ("mq", 0, D // TC), ("v1", 0, 1), *[(name, i, 1) for name, i in MOBA_UNITS], ("v1", 1, 1), ("mo", 0, KD // MR), ("v1", 2, 2),
    ("q1", 0, D // TC), ("wo1", 0, KD // MR), ("gu1", 0, 2 * DFF // TC), ("down1", 0, FT // MR),
]
LAG = 2
BLAG = 1
CB_STEP = 2
SSD_FILLS = {1: ("k0", 0, 0), 3: ("k0", 0, 1), 4: ("k0", 1, 0), 6: ("k0", 1, 1), 7: ("k0", 2, 0), 9: ("k0", 2, 1),
             10: ("k0", 3, 0), 12: ("k0", 3, 1), 13: ("v0", 0, 0), 15: ("v0", 0, 1), 16: ("v0", 1, 0), 17: ("v0", 1, 1)}
U = {}
NAME_OF = []
for _name, _first, _count in PIECES:
    for _i in range(_first, _first + _count):
        U[(_name, _i)] = len(NAME_OF)
        NAME_OF.append((_name, _i))
NUNITS = len(NAME_OF)
SSD_SPLITS = {}
for _step, (_name, _i, _half) in SSD_FILLS.items():
    if _half == 0:
        SSD_SPLITS[_step], SSD_SPLITS[_step + 1] = (U[(_name, _i)] + 2, 0), (U[(_name, _i)] + 2, 1)


def freed_by(name, i):
    if name == "params" or name == "xbc":
        return "dve"
    if name in ("gu0", "gu1"):
        return "dve" if i % 2 else "act"
    return "act"


BANKED = [("params", 0), ("dt", 0)] + [n for n in NAME_OF if KIND[n[0]] != "M"]
V_OF = {n: v for v, n in enumerate(BANKED)}
FREED = []
_n = {"act": 0, "dve": 0}
for _name, _i in BANKED:
    _e = freed_by(_name, _i)
    _n[_e] += 1
    FREED.append((_e, _n[_e]))


def reversed_last(ap):
    dims = [list(d) for d in ap.ap]
    step, n = dims[-1]
    dims[-1] = [-step, n]
    return bass.AP(ap.tensor, ap.offset + step * (n - 1), dims)


def program(nc, A, out):
    bias_rows = nc.dram_tensor("bias_rows", [AH, 3 * P], F32).ap()

    def row_tiles(w, k0, k, c0, c):
        return w[k0 * P:(k0 + k) * P, c0:c0 + c].rearrange("(k p) n -> p k n", p=P)

    w_in = A["ssm_w_in"][0]

    def unit_source(name, i):
        if name == "xbc":
            return row_tiles(w_in, 0, KD, DI + i * TC, TC)
        if name == "z":
            return row_tiles(w_in, 0, KD, i * TC, TC)
        if name in ("k0", "k1"):
            return row_tiles(A["mem_w_kv"][int(name[1])], 0, KD, i * TC, TC)
        if name in ("v0", "v1"):
            return row_tiles(A["mem_w_kv"][int(name[1])], 0, KD, D + i * TC, TC)
        if name in ("q0", "q1"):
            return row_tiles(A["mem_w_q"][int(name[1])], 0, KD, i * TC, TC)
        if name in ("gu0", "gu1"):
            return row_tiles(A["ffn_w_gu"][int(name[2])], 0, KD, (i % 2) * DFF + (i // 2) * TC, TC)
        if name == "mq":
            return row_tiles(A["moba_w_q"][0], 0, KD, i * TC, TC)
        if name == "mk":
            return row_tiles(A["w_kv"], 0, KD, i * TC, TC)
        if name == "mv":
            return row_tiles(A["w_kv"], 0, KD, D + i * TC, TC)
        w = {"w_out": A["ssm_w_out"][0], "wo0": A["mem_w_o"][0], "wo1": A["mem_w_o"][1], "mo": A["moba_w_o"][0],
             "down0": A["ffn_w_down"][0], "down1": A["ffn_w_down"][1]}[name]
        return row_tiles(w, i * MR, MR, 0, D)

    with ExitStack() as ctx:
        at = [16512]

        def place(name, shape, dtype, offset=None):
            size = math.prod(shape[1:]) * (2 if dtype == BF16 else 4)
            where = at[0] if offset is None else offset
            if offset is None:
                at[0] += -(-size // 32) * 32
            return nc.alloc_sbuf_tensor_at(name, shape, dtype, offset=where)

        def sem(name):
            return ctx.enter_context(nc.semaphore(name))

        hi = place("w_hi", [P, SLOTS, UNIT], F32R)
        raw_at = at[0]
        raw = place("w_raw", [P, SLOTS, UNIT], F32)
        lo = place("w_lo", [P, SLOTS, UNIT], F32R, raw_at)
        x = place("x", [P, ST, D], F32)
        actT_hi = place("actT_hi", [P, KD, S], F32R)
        actT_lo = place("actT_lo", [P, KD, S], F32R)
        memT_hi = place("memT_hi", [P, KD, S], F32R)
        memT_lo = place("memT_lo", [P, KD, S], F32R)
        at_memK = at[0]
        memK = place("memK", [P, KD, S], F32)
        memV = place("memV", [P, ST, D], F32)
        post_row = place("post_row", [P, D], F32)
        pre_row = place("pre_row", [P, D], F32)
        ntmp = place("ntmp", [P, ST, D], F32)
        const = place("const", [P, C_HOT], F32)
        hot = place("hot", [BUCKETS, S], F32, at_memK + 2048)
        brows = place("brows", [AH, 3 * P], F32, at_memK)
        stats = place("stats", [P, 6, 32], F32)
        gT = place("gT", [P, XT], F32)
        dT = place("dT", [P, XT], F32)
        small = place("small", [P, 8], F32)
        eps_col, one_col = small[:, 0:1], small[:, 1:2]
        phase = at[0]
        PHASE = 49152
        at[0] += PHASE
        scratch = at[0]

        z = place("z", [P, XT, S], F32, phase)
        dt_heads = place("dt_heads", [P, S], F32, phase)
        xbc = place("xbc", [P, CT, S], F32, phase + 16384)
        y_lo = place("y_lo", [P, XT, S], F32R, phase)
        y_hi = place("y_hi", [P, XT, S], F32R, phase + 16384)
        cw = place("cw", [P, TAPS * CT + CT], F32, phase + 40960)
        dtw = place("dtw", [P, KD, SSM_HEADS], F32, phase + 41472)
        dtw_hi = place("dtw_hi", [P, KD, SSM_HEADS], F32R, phase + 42496)
        dtw_lo = place("dtw_lo", [P, KD, SSM_HEADS], F32R, phase + 43520)
        par_rows = place("par_rows", [P, 2, P], F32, phase + 44544)
        d_pair = place("d_pair", [P, 2], F32, phase + 46080)
        dt_row = place("dt_row", [P, 2, SSM_HEADS], F32, phase + 46112)
        dtc = place("dtc", [P, 8, ST, SSM_HEADS], F32, phase + 46368)
        cbT = place("cbT", [P, 2, CAUS], F32, phase + 40960)
        ycum = place("ycum", [P, 2, S], F32, phase + 44032)
        relb = place("relb", [BUCKETS, AH], F32, phase + 48416)
        mbias = place("mbias", [P, AH, CAUS], F32, phase)
        mqT = place("mqT", [P, KD, S], F32, phase + 24576)
        mkT = place("mkT", [P, KD, S], F32, phase + 32768)
        oT_hi = place("oT_hi", [P, KD, S], F32R, phase + 24576)
        oT_lo = place("oT_lo", [P, KD, S], F32R, phase + 32768)
        mV = place("mV", [P, ST, D], F32, phase + 40960)
        qT = place("qT", [P, KD, S], F32, phase)
        hT_hi = place("hT_hi", [P, FT, S], F32R, phase)
        hT_lo = place("hT_lo", [P, FT, S], F32R, phase + FT * S * 4)

        def shared(name, shape, dtype, offset):
            t = place(name, shape, dtype, scratch + offset)
            return t, offset + math.prod(shape[1:]) * (2 if dtype == BF16 else 4)

        conv_acc, o = shared("conv_acc", [P, 2, 2, S], F32, 0)
        xtok, o = shared("xtok", [P, 3, ST, P], F32, 0)
        decay, o = shared("decay", [P, 2, CAUS], F32, o)
        mt, o = shared("mt", [P, 6, CAUS], F32, o)
        mask_bf, o = shared("mask_bf", [P, P], BF16, max(o, 4096))
        id_bf, o = shared("id_bf", [P, P], BF16, o)
        id_r, o = shared("id_r", [P, SSM_HEADS], F32R, o)
        cumT_hi, o = shared("cumT_hi", [P, S], F32R, o)
        cumT_lo, o = shared("cumT_lo", [P, S], F32R, o)
        rs, o = shared("rs", [P, 2, S], F32, o)
        end_ssd = o
        prob, o = shared("prob", [P, 2, ST, S], F32, 0)
        probT, o = shared("probT", [P, 2, ST, S], F32, o)
        mstat, o = shared("mstat", [P, 4, ST * MH], F32, o)
        sc, o2 = shared("sc", [P, 3, 2, CAUS], F32, 0)
        scT, o2 = shared("scT", [P, 2, 2, CAUS], F32, o2)
        bstat, o2 = shared("bstat", [P, 4, ST, AH], F32, o2)
        gate, o3 = shared("gate", [P, 2, 2, S], F32, 0)
        hval, o3 = shared("hval", [P, 2, 2, S], F32, o3)
        top = scratch + max(end_ssd, o, o2, o3)
        assert top <= 229368, top

        bank = ctx.enter_context(nc.psum_tensor("bank", [P, 8, 512], F32))
        msum = [bank[:, 4 + 2 * t:6 + 2 * t, :].rearrange("p b n -> p (b n)") for t in range(ST)]

        w_loaded = [sem(f"w_loaded{s}") for s in range(SLOTS)]
        w_hi_done = sem("w_hi_done")
        w_lo_done = sem("w_lo_done")
        w_used = sem("w_used")
        m_half = sem("m_half")
        t_out = {"act": sem("t_out_act"), "dve": sem("t_out_dve")}
        act_step = sem("act_step")
        dve_step = sem("dve_step")
        x_loaded, mem_loaded = [sem(f"x_loaded{t}") for t in range(ST)], sem("mem_loaded")
        par_loaded, const_loaded, rows_loaded = sem("par_loaded"), sem("const_loaded"), sem("rows_loaded")
        pre_loaded, post_loaded = sem("pre_loaded"), sem("post_loaded")
        consts_made = sem("consts_made")
        eps_made = sem("eps_made")
        sum_ready = sem("sum_ready")
        stat_ready = sem("stat_ready")
        x_ready = sem("x_ready")
        u_ready = sem("u_ready")
        turned = sem("turned")
        turn_hi, turn_lo = sem("turn_hi"), sem("turn_lo")
        par_cleared = sem("par_cleared")
        par_turned = sem("par_turned")
        dtw_hi_done, dtw_lo_done = sem("dtw_hi_done"), sem("dtw_lo_done")
        dt_mm, dt_turned = sem("dt_mm"), sem("dt_turned")
        dt_biased, dt_logged = sem("dt_biased"), sem("dt_logged")
        dt_ready, cum_mm, cum_hi, cum_ready = sem("dt_ready"), sem("cum_mm"), sem("cum_hi"), sem("cum_ready")
        brow_mm, brow_ready, brow_stored = sem("brow_mm"), sem("brow_ready"), sem("brow_stored")
        conv_first, conv_silu = sem("conv_first"), sem("conv_silu")
        cb_mm, cb_ready = sem("cb_mm"), sem("cb_ready")
        xtok_mm, xtok_ready = sem("xtok_mm"), sem("xtok_ready")
        row_mm, decay_ready, mt_ready = sem("row_mm"), sem("decay_ready"), sem("mt_ready")
        y_mm, y_ready, ysq_ready, ssq_mm, rs_ready = sem("y_mm"), sem("y_ready"), sem("ysq_ready"), sem("ssq_mm"), sem("rs_ready")
        yn_ready, y_hi_done, y_lo_done = sem("yn_ready"), sem("y_hi_done"), sem("y_lo_done")
        a_mm, a_neg, a_exp, a_norm = sem("a_mm"), sem("a_neg"), sem("a_exp"), sem("a_norm")
        a_turned, a_probT, a_out, a_hi, a_lo = sem("a_turned"), sem("a_probT"), sem("a_out"), sem("a_hi"), sem("a_lo")
        b_mm, b_read, b_neg, b_exp, b_norm = sem("b_mm"), sem("b_read"), sem("b_neg"), sem("b_exp"), sem("b_norm")
        b_turned, b_probT, b_out, b_hi, b_lo = sem("b_turned"), sem("b_probT"), sem("b_out"), sem("b_hi"), sem("b_lo")
        bias_loaded = sem("bias_loaded")
        h_hi, h_lo = sem("h_hi"), sem("h_lo")
        stored = sem("stored")

        class Own:

            def __init__(self, eng, s):
                self.eng, self.sem, self.n = eng, s, 0

            def mark(self, ins):
                ins.then_inc(self.sem, 1)
                self.n += 1

            def wait(self, i=0, per=0):
                self.eng.wait_ge(self.sem, self.n + i * per if per else self.n)

        TURN_GAIN = [A["mix_pre_g"][0], A["mem_norm_g"], A["mem_pre_g"][0], A["ffn_pre_g"][0],
                     A["mix_pre_g"][1], A["kv_norm_g"], A["mem_pre_g"][1], A["ffn_pre_g"][1]]
        POST_GAIN = [A["mix_post_g"][0], A["mem_post_g"][0], A["ffn_post_g"][0],
                     A["mix_post_g"][1], A["mem_post_g"][1], A["ffn_post_g"][1]]
        POST_TURN = [2, 3, 4, 6, 7, None]
        M_OF_POST = ["w_out", "wo0", "down0", "mo", "wo1", "down1"]

        def stat_col(n, t, after):
            return 4 + 4 * n + (2 * t + after if POST_TURN[n] is not None else t)

        def last_unit(name):
            return max(u for (n, _), u in U.items() if n == name)

        def units_ahead(n):
            last = last_unit(M_OF_POST[n])
            return last + (2 if last + 1 < NUNITS and NAME_OF[last + 1][0] == "gu1" else 3)

        def every_row(row):
            return bass.AP(row.tensor, row.offset, [[0, P]] + [list(d) for d in row.ap])

        block = ctx.enter_context(nc.Block())

        @block.sync
        def _(sp):
            def load(u):
                name, i = NAME_OF[u]
                if u >= SLOTS:
                    sp.wait_ge(w_used, u - SLOTS + 1)
                src = unit_source(name, i)
                dst = raw[:, u % SLOTS, :].rearrange("p (k n) -> p k n", n=src.shape[-1])
                sp.dma_start(dst, src).then_inc(w_loaded[u % SLOTS], 16)

            for t in range(ST):
                sp.dma_start(x[:, t, :], A["x"][0, t * P:(t + 1) * P, :]).then_inc(x_loaded[t], 16)
            sp.dma_start(const[:], A["consts"][:, 0:C_HOT]).then_inc(const_loaded, 16)
            sp.wait_ge(par_cleared, 1)
            sp.dma_start(par_rows[0:TAPS * CT, 0, :], A["ssm_conv_w"][0].rearrange("k (c p) -> (k c) p", p=P)).then_inc(par_loaded, 16)
            sp.dma_start(par_rows[0:CT, 1, :], A["ssm_conv_b"][0].rearrange("(c p) -> c p", p=P)).then_inc(par_loaded, 16)
            sp.dma_start(par_rows[G_ROW:G_ROW + XT, 1, :], A["ssm_norm_g"][0].rearrange("(c p) -> c p", p=P)).then_inc(par_loaded, 16)
            sp.dma_start(d_pair[D_ROW:D_ROW + XT, :], A["ssm_d"][0].rearrange("(c e) -> c e", e=2)).then_inc(par_loaded, 16)
            sp.dma_start(dtw[:], row_tiles(w_in, 0, KD, DI + CONV, SSM_HEADS)).then_inc(par_loaded, 16)
            for u in range(NUNITS):
                load(u)
            for t in range(ST):
                sp.wait_ge(x_ready, 2 * len(POST_GAIN) - 1 + t)
                sp.dma_start(out[0, t * P:(t + 1) * P, :], x[:, t, :]).then_inc(stored, 16)
            sp.wait_ge(stored, 16 * ST)

        @block.gpsimd
        def _(pool):
            mem_t = A["mem"][0].rearrange("(t p) n -> p t n", p=P)
            pool.dma_start(pre_row[:], every_row(TURN_GAIN[0])).then_inc(pre_loaded, 16)
            pool.dma_start(dt_row[:, 0, :], every_row(A["ssm_dt_bias"][0])).then_inc(rows_loaded, 16)
            pool.dma_start(dt_row[:, 1, :], every_row(A["ssm_a_log"][0])).then_inc(rows_loaded, 16)
            pool.dma_start(relb[:], A["rel_bias"]).then_inc(rows_loaded, 16)
            pool.dma_start(hot[:], A["consts"][0:BUCKETS, C_HOT:C_END]).then_inc(rows_loaded, 16)
            pool.wait_ge(u_ready, 2)
            pool.dma_start(pre_row[:], every_row(TURN_GAIN[1])).then_inc(pre_loaded, 16)
            pool.dma_start(memV[:], mem_t).then_inc(mem_loaded, 16)
            pool.dma_start(post_row[:], every_row(POST_GAIN[0])).then_inc(post_loaded, 16)
            pool.wait_ge(brow_ready, 1)
            pool.dma_start(bias_rows, brows[:]).then_inc(brow_stored, 16)
            for n in range(6):
                turn = POST_TURN[n]
                if turn is not None:
                    pool.wait_ge(u_ready, 2 * turn)
                    pool.dma_start(pre_row[:], every_row(TURN_GAIN[turn])).then_inc(pre_loaded, 16)
                if n < 5:
                    pool.wait_ge(x_ready, 2 * n + 2)
                    pool.dma_start(post_row[:], every_row(POST_GAIN[n + 1])).then_inc(post_loaded, 16)
                if n == 2:
                    pool.wait_ge(u_ready, 10)
                    pool.dma_start(pre_row[:], every_row(TURN_GAIN[5])).then_inc(pre_loaded, 16)
                    pool.wait_ge(brow_stored, 16)
                    for pair in range(AH // 2):
                        pool.wait_ge(w_used, last_unit("down0") + 1 + pair)
                        heads = slice(2 * pair, 2 * pair + 2)
                        for c0, c, base in ((0, S, 0), (S, P, P)):
                            src = bass.AP(bias_rows.tensor, base + pair * 6 * P, [[1, P], [3 * P, 2], [1, c]])
                            pool.dma_start(mbias[:, heads, c0:c0 + c], src).then_inc(bias_loaded, 16)

        @block.tensor
        def _(pe):
            ident = const[:, C_ID:C_ID + P]
            tri_ones = const[:, C_TRI:C_TRI + S]

            def product(dst, passes, first, last):
                for n, (a, b) in enumerate(passes):
                    ins = pe.matmul(dst, a, b, start=first and n == 0, stop=last and n == len(passes) - 1,
                                    skip_group_check=True)
                return ins

            def t_unit(slot, b, act_hi, act_lo, halves=range(2)):
                for c in halves:
                    for k in range(KD):
                        cols = slice(k * TC + c * P, k * TC + (c + 1) * P)
                        wh, wl = hi[:, slot, cols], lo[:, slot, cols]
                        ins = product(bank[:, b, c * S:(c + 1) * S],
                                      [(wh, act_hi[:, k, :]), (wh, act_lo[:, k, :]), (wl, act_hi[:, k, :])],
                                      k == 0, k == KD - 1)
                return ins

            def v_unit(slot, b, act_hi, act_lo, halves=range(2)):
                for t in halves:
                    for k in range(KD):
                        cols = slice(k * TC, (k + 1) * TC)
                        ah, al = act_hi[:, k, t * P:(t + 1) * P], act_lo[:, k, t * P:(t + 1) * P]
                        ins = product(bank[:, b, t * TC:(t + 1) * TC],
                                      [(ah, hi[:, slot, cols]), (ah, lo[:, slot, cols]), (al, hi[:, slot, cols])],
                                      k == 0, k == KD - 1)
                return ins

            def banked(name, i, act_hi, act_lo, free=None):
                u, v = U[(name, i)], V_OF[(name, i)]
                e, n = free or FREED[v - 2]
                pe.wait_ge(t_out[e], n)
                pe.wait_ge(w_lo_done, u + 1)
                f = t_unit if KIND[name] == "T" else v_unit
                f(u % SLOTS, v % 2, act_hi, act_lo).then_inc(w_used, 1)

            def fill(name, *units):
                for i in units:
                    banked(name, i, memT_hi, memT_lo)

            def fill_half(name, i, half):
                u, v = U[(name, i)], V_OF[(name, i)]
                if half == 0:
                    e, n = FREED[v - 2]
                    pe.wait_ge(t_out[e], n)
                    pe.wait_ge(w_lo_done, u + 1)
                f = t_unit if KIND[name] == "T" else v_unit
                ins = f(u % SLOTS, v % 2, memT_hi, memT_lo, [half])
                if half:
                    ins.then_inc(w_used, 1)

            def loop_t(name, iters, free_of_slot):
                u0, v0 = U[(name, 0)], V_OF[(name, 0)]
                for e, n in FREED[v0 - 2:v0]:
                    pe.wait_ge(t_out[e], n)
                with pe.Fori(0, iters) as i:
                    for j in range(5):
                        if j:
                            e, n = free_of_slot(j, i)
                            pe.wait_ge(t_out[e], n)
                        if j < 4:
                            pe.wait_ge(w_lo_done, i * 4 + (u0 + j + 1))
                            t_unit((u0 + j) % SLOTS, (v0 + j) % 2, actT_hi, actT_lo).then_inc(w_used, 1)

            def m_part(name, act_hi, act_lo, ready):
                n = last_unit(name) - U[(name, 0)] + 1
                steps = [(i, t) for i in range(n - 2) for t in range(ST)] + [(i, t) for t in range(ST) for i in (n - 2, n - 1)]
                for i, t in steps:
                    u = U[(name, i)]
                    if t == 0:
                        ready(i)
                        pe.wait_ge(w_lo_done, u + 1)
                    for r in range(MR):
                        k = i * MR + r
                        ah, al = act_hi[:, k, t * P:(t + 1) * P], act_lo[:, k, t * P:(t + 1) * P]
                        for half in range(2):
                            cols = slice(r * D + half * 512, r * D + half * 512 + 512)
                            wh, wl = hi[:, u % SLOTS, cols], lo[:, u % SLOTS, cols]
                            ins = product(bank[:, 4 + 2 * t + half, :], [(ah, wh), (ah, wl), (al, wh)],
                                          k == 0, k == n * MR - 1)
                    if t == ST - 1:
                        ins.then_inc(w_used, 1)
                    elif i == n - 1:
                        ins.then_inc(m_half, 1)

            def turn(k, name=None, i=0):
                if name:
                    fill(name, i)
                for t in range(ST):
                    if name and t:
                        fill_half(name, i + 1, 0)
                    pe.wait_ge(u_ready, 2 * k + t + 1)
                    for half in range(2):
                        for q in range(4):
                            c = (half * 4 + q) * P
                            ins = pe.transpose(bank[:, 4 + 2 * t + half, q * P:(q + 1) * P], ntmp[:, t, c:c + P], ident)
                        ins.then_inc(turned, 1)
                if name:
                    fill_half(name, i + 1, 1)

            def turn_done(k):
                pe.wait_ge(turn_lo, 4 * k + 4)

            pe.wait_ge(const_loaded, 16)
            turn(0)
            pe.wait_ge(par_loaded, 80)
            pe.wait_ge(consts_made, 1)
            for r in range(2):
                ins = pe.transpose(bank[:, 0, r * P:(r + 1) * P], par_rows[:, r, :], ident)
            ins.then_inc(par_turned, 1)
            turn_done(0)
            pe.wait_ge(dtw_lo_done, 1)
            for k in range(KD):
                ins = product(bank[0:SSM_HEADS, 1, 0:S],
                              [(dtw_hi[:, k, :], actT_hi[:, k, :]), (dtw_hi[:, k, :], actT_lo[:, k, :]), (dtw_lo[:, k, :], actT_hi[:, k, :])],
                              k == 0, k == KD - 1)
            ins.then_inc(dt_mm, 1)
            e, n = FREED[V_OF[("dt", 0)]]
            pe.wait_ge(t_out[e], n)
            for t in range(ST):
                ins = pe.transpose(bank[:, 2, t * SSM_HEADS:(t + 1) * SSM_HEADS], dt_heads[0:SSM_HEADS, t * P:(t + 1) * P],
                                   ident[0:SSM_HEADS, 0:SSM_HEADS])
            ins.then_inc(dt_turned, 1)

            u0 = U[("xbc", 0)]
            pe.wait_ge(dt_biased, 1)
            pe.wait_ge(t_out["dve"], 1)
            with pe.Fori(0, 3) as i:
                for j in range(4):
                    if j == 2:
                        pe.wait_ge(t_out["dve"], i * 4 + 1)
                    pe.wait_ge(w_lo_done, i * 4 + (u0 + j + 1))
                    t_unit((u0 + j) % SLOTS, j, actT_hi, actT_lo).then_inc(w_used, 1)
                pe.wait_ge(t_out["dve"], i * 4 + 3)
            def cumulate():
                pe.wait_ge(dt_ready, 1)
                e, n = FREED[V_OF[("xbc", CONV // TC - 1)]]
                pe.wait_ge(t_out[e], n)
                adt = dtc[:, 6]
                product(bank[:, 2, 0:32], [(tri_ones[:, 0:P], adt[:, 0, :])], True, True)
                product(bank[:, 2, 32:64], [(tri_ones[:, P:S], adt[:, 0, :]), (tri_ones[:, 0:P], adt[:, 1, :])], True, True)
                product(bank[0:SSM_HEADS, 3, 0:S], [(adt[:, 0, :], tri_ones)], True, False)
                product(bank[0:SSM_HEADS, 3, P:S], [(adt[:, 1, :], tri_ones[:, 0:P])], False, True).then_inc(cum_mm, 1)

            for i in range(DI // TC):
                banked("z", i, actT_hi, actT_lo, FREED[V_OF[("z", i)] - 4] if i < 2 else None)
                if i == 3:
                    turn(1)
                if i == 4:
                    cumulate()
                if i == 6:
                    pe.wait_ge(rows_loaded, 64)
                    pe.wait_ge(cum_ready, 1)
                    product(bank[0:AH, 2, 0:S], [(relb[:], hot[:])], True, True).then_inc(brow_mm, 1)
            turn_done(1)

            pe.wait_ge(conv_silu, CT // 2)
            def ssd_y(j):
                g = j // GT
                for e in range(2):
                    h = 2 * j + e
                    pe.wait_ge(mt_ready, h + 1)
                    if e == 0:
                        if j >= 2:
                            pe.wait_ge(y_ready, j - 1)
                    rows = slice(e * HD, (e + 1) * HD)
                    pe.matmul(bank[rows, 3 + j % 2 * 3, 0:S], xtok[:, j % 3, 0, rows], mt[:, h % 6, 0:S],
                              start=True, stop=False, skip_group_check=True)
                    ins = pe.matmul(bank[rows, 3 + j % 2 * 3, P:S], xtok[:, j % 3, 1, rows], mt[:, h % 6, S:CAUS],
                                    start=False, stop=True, skip_group_check=True)
                ins.then_inc(y_mm, 1)

            def ssd_ssq(j):
                pe.wait_ge(ysq_ready, j + 1)
                if j % GT == 0 and j:
                    pe.wait_ge(rs_ready, j // GT)
                product(bank[:, 7, 0:S], [(tri_ones[:, P:S], ycum[:, j % 2, :])], j % GT == 0, j % GT == GT - 1).then_inc(ssq_mm, 1)

            def ssd_cb(g):
                Bt, Ct = xbc[:, XT + g, :], xbc[:, XT + SSM_GROUPS + g, :]
                product(bank[:, 2, 0:S], [(Bt[:, 0:P], Ct)], True, True)
                product(bank[:, 2, S:CAUS], [(Bt[:, P:S], Ct[:, P:S])], True, True).then_inc(cb_mm, 1)

            pe.wait_ge(brow_ready, 1)
            ssd_cb(0)
            for j in range(XT + LAG + 2):
                if j < XT:
                    g = j // GT
                    if j == 0 or j % GT == CB_STEP + 1 and g + 1 < SSM_GROUPS:
                        pe.wait_ge(cb_ready, g + 2 if j else 1)
                    if j:
                        pe.wait_ge(xtok_ready, j)
                    for t in range(ST):
                        ins = pe.transpose(bank[:, 2, t * P:(t + 1) * P], xbc[:, j, t * P:(t + 1) * P], ident)
                    ins.then_inc(xtok_mm, 1)
                    for e in range(2):
                        h = 2 * j + e
                        if h >= 2:
                            pe.wait_ge(decay_ready, h - 1)
                        one = id_r[:, h:h + 1].broadcast_to([P, P])
                        row = bank[:, 4 + h % 2, :]
                        for dst, l0, l1 in ((row[:, 0:S], 0, S), (row[:, S:CAUS], P, S)):
                            pe.matmul(dst, one, cumT_hi[:, l0:l1], start=True, stop=False, skip_group_check=True)
                            pe.matmul(dst, one, cumT_lo[:, l0:l1], start=False, stop=False, skip_group_check=True)
                            ins = pe.matmul(dst[:, 0:P], id_bf[:], mask_bf[:], start=False, stop=True, skip_group_check=True)
                        ins.then_inc(row_mm, 1)
                    if j % GT == CB_STEP and g + 1 < SSM_GROUPS:
                        pe.wait_ge(xtok_ready, j + 1)
                        ssd_cb(g + 1)
                if j > LAG + 1:
                    ssd_ssq(j - LAG - 2)
                if j < XT:
                    if j in SSD_FILLS:
                        fill_half(*SSD_FILLS[j])
                if LAG <= j < XT + LAG:
                    ssd_y(j - LAG)
                if j >= XT and j in SSD_FILLS:
                    fill_half(*SSD_FILLS[j])

            pe.wait_ge(rs_ready, SSM_GROUPS)
            m_part("w_out", y_hi, y_lo, lambda i: pe.wait_ge(y_lo_done, i * MR // GT + 1))
            turn(2, "v0", 2)

            def memory_attention(layer):
                h0 = layer * MH
                query = f"q{layer}"

                def scores(h):
                    for name, i in ((f"k{layer}", 3), (f"v{layer}", 3), (query, h))[0 if h == 0 else 2:]:
                        e, n = FREED[V_OF[(name, i)]]
                        pe.wait_ge(t_out[e], n)
                    b = 4 + h % 2
                    if h >= 2:
                        pe.wait_ge(a_exp, h0 + h - 1)
                    for t in range(ST):
                        for kk in range(2):
                            ins = pe.matmul(bank[:, b, t * S:(t + 1) * S], qT[:, 2 * h + kk, t * P:(t + 1) * P],
                                            memK[:, 2 * h + kk, :], start=kk == 0, stop=kk == 1, skip_group_check=True)
                    ins.then_inc(a_mm, 1)

                banked(query, 0, actT_hi, actT_lo)
                for s in range(MH + 2):
                    if s + 1 < MH:
                        banked(query, s + 1, actT_hi, actT_lo)
                        scores(s)
                    if s + 2 == MH:
                        scores(MH - 1)
                    if 1 <= s <= MH:
                        h = s - 1
                        pe.wait_ge(a_norm, h0 + h + 1)
                        if h >= 2:
                            pe.wait_ge(a_probT, h0 + h - 1)
                        for m in range(ST):
                            for t in range(ST):
                                ins = pe.transpose(bank[:, 6 + h % 2, m * S + t * P:m * S + (t + 1) * P],
                                                   prob[:, h % 2, t, m * P:(m + 1) * P], ident)
                        ins.then_inc(a_turned, 1)
                    if s >= 2:
                        h = s - 2
                        pe.wait_ge(a_probT, h0 + h + 1)
                        if h >= 2:
                            pe.wait_ge(a_lo, h0 + h - 1)
                        for d in range(2):
                            for m in range(ST):
                                c = (2 * h + d) * P
                                ins = pe.matmul(bank[:, 2 + h % 2, d * S:(d + 1) * S], memV[:, m, c:c + P],
                                                probT[:, h % 2, m, :], start=m == 0, stop=m == 1, skip_group_check=True)
                        ins.then_inc(a_out, 1)

            def qkv(name):
                for i in range(4):
                    banked(name, i, actT_hi, actT_lo)

            def feed_forward(layer):
                name = f"gu{layer}"
                a0, d0 = FREED[V_OF[(name, 0)]][1] - 1, FREED[V_OF[(name, 1)]][1] - 1
                loop_t(name, 5, lambda j, i: (("act", "dve")[j % 2], i * 2 + ((a0, d0)[j % 2] + j // 2)))
                for i in (20, 21):
                    banked(name, i, actT_hi, actT_lo)
                m_part(f"down{layer}", hT_hi, hT_lo, lambda i: pe.wait_ge(h_lo, 11 * layer + i + 1))

            turn_done(2)
            memory_attention(0)
            m_part("wo0", actT_hi, actT_lo, lambda i: pe.wait_ge(a_lo, i + 1))
            turn(3, "k1", 0)
            turn_done(3)
            feed_forward(0)
            turn(4, "k1", 2)
            turn_done(4)
            qkv("mq")
            turn(5)
            fill("v1", 0)
            turn_done(5)

            pairs = AH // 2
            banked("mk", 0, actT_hi, actT_lo)
            for s in range(pairs + BLAG + 1):
                if s + 1 < len(MOBA_UNITS):
                    banked(*MOBA_UNITS[s + 1], actT_hi, actT_lo)
                if s >= pairs - 1 and s <= pairs:
                    fill_half("v1", 1, s - pairs + 1)
                if s < pairs:
                    for name in ("mq", "mk"):
                        e, n = FREED[V_OF[(name, s // 2)]]
                        pe.wait_ge(t_out[e], n)
                    if s:
                        pe.wait_ge(b_read, s)
                    for a in range(2):
                        rows = slice(a * HD, (a + 1) * HD)
                        pe.matmul(bank[:, 4 + a, 0:S], mqT[rows, s, P:S], mkT[rows, s, :], start=True, stop=True, skip_group_check=True)
                        ins = pe.matmul(bank[:, 4 + a, S:CAUS], mqT[rows, s, 0:P], mkT[rows, s, 0:P], start=True, stop=True, skip_group_check=True)
                    ins.then_inc(b_mm, 1)
                if BLAG <= s < pairs + BLAG:
                    p = s - BLAG
                    pe.wait_ge(b_norm, p + 1)
                    if p:
                        pe.wait_ge(b_probT, p)
                    for a in range(2):
                        for n, c in enumerate((S, 0, P)):
                            ins = pe.transpose(bank[:, 6 + a, n * P:(n + 1) * P], sc[:, p % 3, a, c:c + P], ident)
                    ins.then_inc(b_turned, 1)
                if s > BLAG:
                    p = s - BLAG - 1
                    pe.wait_ge(b_probT, p + 1)
                    e, n = FREED[V_OF[("mv", p // 2)]]
                    pe.wait_ge(t_out[e], n)
                    if p >= 2:
                        pe.wait_ge(b_lo, p - 1)
                    for a in range(2):
                        rows = slice(a * HD, (a + 1) * HD)
                        cols = slice((2 * p + a) * HD, (2 * p + a + 1) * HD)
                        pe.matmul(bank[rows, 2 + p % 2, 0:S], mV[:, 0, cols], scT[:, p % 2, a, 0:S], start=True, stop=False, skip_group_check=True)
                        ins = pe.matmul(bank[rows, 2 + p % 2, P:S], mV[:, 1, cols], scT[:, p % 2, a, S:CAUS], start=False, stop=True, skip_group_check=True)
                    ins.then_inc(b_out, 1)
            m_part("mo", oT_hi, oT_lo, lambda i: pe.wait_ge(b_lo, 2 * i + 2))
            turn(6, "v1", 2)
            turn_done(6)
            memory_attention(1)
            m_part("wo1", actT_hi, actT_lo, lambda i: pe.wait_ge(a_lo, MH + i + 1))
            turn(7)
            turn_done(7)
            feed_forward(1)

        @block.scalar
        def _(act):
            own = Own(act, act_step)
            done = [0]

            def hi_unit(u, i=0, per=0):
                count = 16 * (u // SLOTS + 1)
                act.wait_ge(w_loaded[u % SLOTS], i * 16 + count if per else count)
                act.activation(hi[:, u % SLOTS, :], raw[:, u % SLOTS, :], ACT.Copy).then_inc(w_hi_done, 1)

            def hi_part(u, part):
                assert u == done[0]
                cols = slice(part * UNIT // 2, (part + 1) * UNIT // 2)
                if part == 0:
                    act.wait_ge(w_loaded[u % SLOTS], 16 * (u // SLOTS + 1))
                ins = act.activation(hi[:, u % SLOTS, cols], raw[:, u % SLOTS, cols], ACT.Copy)
                if part:
                    ins.then_inc(w_hi_done, 1)
                    done[0] += 1

            def hi_upto(u):
                while done[0] <= min(u, NUNITS - 1):
                    hi_unit(done[0])
                    done[0] += 1

            def statistic(c, t, src):
                act.activation(ntmp[:, t, :], src, ACT.Square, accum_out=stats[:, 0, c:c + 1]).then_inc(sum_ready, 1)
                act.wait_ge(sum_ready, c + 1)
                own.mark(act.activation(stats[:, 1, c:c + 1], stats[:, 0, c:c + 1], ACT.Ln, bias=eps_col, scale=1.0 / D))
                own.wait()
                act.activation(stats[:, 2, c:c + 1], stats[:, 1, c:c + 1], ACT.Exp, scale=-0.5).then_inc(stat_ready, 1)

            def turn(k, dst):
                for t in range(ST):
                    for half in range(2):
                        act.wait_ge(turned, 4 * k + 2 * t + half + 1)
                        act.activation(dst[:, half * 4:half * 4 + 4, t * P:(t + 1) * P],
                                       bank[:, 4 + 2 * t + half, :].rearrange("p (q n) -> p q n", n=P),
                                       ACT.Copy).then_inc(turn_hi, 1)

            def tiles(b):
                return bank[:, b, :].rearrange("p (c n) -> p c n", n=S)

            def copy_out(name, i):
                u, v = U[(name, i)], V_OF[(name, i)]
                act.wait_ge(w_used, u + 1)
                src = tiles(v % 2)
                dst = {"mq": mqT, "mk": mkT, "mv": mV, "k0": memK, "k1": memK, "v0": memV, "v1": memV, "q0": qT, "q1": qT}[name]
                if name == "mq":
                    src = bank[:, v % 2, :].rearrange("p (c n) -> p c n", n=P)
                    dst = reversed_last(mqT[:].rearrange("p k (t n) -> p (k t) n", n=P)[:, 4 * i:4 * i + 4, :])
                elif KIND[name] == "V":
                    dst = dst[:, :, i * TC:(i + 1) * TC]
                else:
                    dst = dst[:, 2 * i:2 * i + 2, :]
                act.activation(dst, src, ACT.Copy).then_inc(t_out["act"], 1)

            def copies(name, *units):
                for i in units:
                    hi_upto(U[(name, i)] + 2)
                    copy_out(name, i)

            def m_part(name):
                hi_upto(last_unit(name) + 1)

            def norms(n):
                act.preload_act_table_set("natural_log_exp_and_others")
                last = last_unit(M_OF_POST[n])
                act.wait_ge(m_half, n + 1)
                statistic(stat_col(n, 0, 0), 0, msum[0])
                hi_upto(last + 2)
                if POST_TURN[n] is not None:
                    act.wait_ge(x_ready, 2 * n + 1)
                    statistic(stat_col(n, 0, 1), 0, x[:, 0, :])
                act.wait_ge(w_used, last + 1)
                statistic(stat_col(n, 1, 0), 1, msum[1])
                hi_upto(units_ahead(n))
                if POST_TURN[n] is not None:
                    act.wait_ge(x_ready, 2 * n + 2)
                    statistic(stat_col(n, 1, 1), 1, x[:, 1, :])

            act.preload_act_table_set("natural_log_exp_and_others")
            act.wait_ge(eps_made, 1)
            for t in range(ST):
                act.wait_ge(x_loaded[t], 16)
                statistic(t, t, x[:, t, :])
            act.wait_ge(par_loaded, 80)
            act.activation(dtw_hi[:], dtw[:], ACT.Copy).then_inc(dtw_hi_done, 1)
            turn(0, actT_hi)
            hi_upto(1)
            act.wait_ge(dt_mm, 1)
            act.activation(dt_heads[0:SSM_HEADS, :], bank[0:SSM_HEADS, 1, 0:S], ACT.Copy).then_inc(t_out["act"], 1)
            act.wait_ge(dt_biased, 1)
            own.mark(act.activation(dtc[:, 2], dtc[:, 1], ACT.Abs))
            own.wait()
            own.mark(act.activation(dtc[:, 3], dtc[:, 2], ACT.Exp, scale=-1.0))
            own.wait()
            act.activation(dtc[:, 4], dtc[:, 3], ACT.Ln, bias=one_col)
            act.activation(dt_row[:, 1, :], dt_row[:, 1, :], ACT.Exp).then_inc(dt_logged, 1)
            act.preload_act_table_set("silu_and_others")

            def silu_conv(i, j):
                act.wait_ge(t_out["dve"], i * 4 + (j + 2))
                act.activation(xbc[:, bass.ds(i * 8 + 2 * j, 2), :], conv_acc[:, j % 2], ACT.Silu).then_inc(conv_silu, 1)

            with act.Fori(0, 3) as i:
                for j in range(4):
                    hi_unit(2 + j, i, 4)
                    if j:
                        silu_conv(i, j - 1)
                    act.wait_ge(w_used, i * 4 + (j + 1))
                    for c in range(2):
                        ins = act.activation(conv_acc[:, j % 2, c, :], tiles(j)[:, c, :], ACT.Identity,
                                             scale=cw[:, bass.ds(i * 8 + (3 * CT + 2 * j + c), 1)],
                                             bias=cw[:, bass.ds(i * 8 + (4 * CT + 2 * j + c), 1)])
                    ins.then_inc(conv_first, 1)
                silu_conv(i, 3)
            done[0] = U[("z", 0)] + 2
            for i in range(DI // TC):
                hi_upto(U[("z", i)] + 2)
                act.wait_ge(w_used, U[("z", i)] + 1)
                act.activation(z[:, 2 * i:2 * i + 2, :], tiles(V_OF[("z", i)] % 2), ACT.Silu).then_inc(t_out["act"], 1)
                if i == 1:
                    act.preload_act_table_set("natural_log_exp_and_others")
                    act.wait_ge(mem_loaded, 16)
                    for t in range(ST):
                        statistic(2 + t, t, memV[:, t, :])
                    act.preload_act_table_set("silu_and_others")
                if i == 4:
                    turn(1, memT_hi)
                if i == 5:
                    act.wait_ge(cum_mm, 1)
                    act.activation(cumT_hi[0:SSM_HEADS, :], bank[0:SSM_HEADS, 3, 0:S], ACT.Copy).then_inc(cum_hi, 1)

            def copy_cb(g):
                act.wait_ge(cb_mm, g + 1)
                act.activation(cbT[:, g % 2, :], bank[:, 2, 0:CAUS], ACT.Copy).then_inc(cb_ready, 1)

            copy_cb(0)
            act.preload_act_table_set("natural_log_exp_and_others")
            for j in range(XT + LAG + 3):
                c = j - LAG
                if j < XT:
                    g = j // GT
                    act.wait_ge(xtok_mm, j + 1)
                    act.activation(xtok[:, j % 3], bank[:, 2, 0:S].rearrange("p (t n) -> p t n", n=P), ACT.Copy).then_inc(xtok_ready, 1)
                    for h in (2 * j, 2 * j + 1):
                        act.wait_ge(row_mm, h + 1)
                        if h >= 2:
                            act.wait_ge(mt_ready, h - 1)
                        row = bank[:, 4 + h % 2, :]
                        act.activation(decay[:, h % 2, 0:S], row[:, 0:S], ACT.Exp, bias=dtc[:, 7, 0, h:h + 1])
                        act.activation(decay[:, h % 2, S:CAUS], row[:, S:CAUS], ACT.Exp, bias=dtc[:, 7, 1, h:h + 1]).then_inc(decay_ready, 1)
                    if j % GT == CB_STEP and g + 1 < SSM_GROUPS:
                        copy_cb(g + 1)
                if 1 <= c <= XT:
                    act.wait_ge(y_ready, c)
                    if c >= 3:
                        act.wait_ge(ssq_mm, c - 2)
                    act.activation(ycum[:, (c - 1) % 2, :], z[:, c - 1, :], ACT.Square).then_inc(ysq_ready, 1)
                if c > 1 and c % GT == 1:
                    act.wait_ge(ssq_mm, c - 1)
                    own.mark(act.activation(rs[:, 0, :], bank[:, 7, 0:S], ACT.Ln, bias=eps_col, scale=1.0 / (GT * P)))
                    own.wait()
                    act.activation(rs[:, 1, :], rs[:, 0, :], ACT.Exp, scale=-0.5).then_inc(rs_ready, 1)
                if c > 2 and c % GT == 2:
                    g = c // GT - 1
                    act.wait_ge(yn_ready, g + 1)
                    act.activation(y_hi[:, g * GT:(g + 1) * GT, :], z[:, g * GT:(g + 1) * GT, :], ACT.Copy).then_inc(y_hi_done, 1)
                if j in SSD_SPLITS:
                    hi_part(*SSD_SPLITS[j])
                if j in SSD_FILLS:
                    name, i, half = SSD_FILLS[j]
                    if half:
                        if name == "k0" and i == 0:
                            act.wait_ge(brow_stored, 16)
                        copy_out(name, i)

            m_part("w_out")
            norms(0)
            copy_out("v0", 2)
            turn(2, actT_hi)
            copy_out("v0", 3)

            def memory_attention(layer):
                copies(f"q{layer}", 0)
                for s in range(MH + 3):
                    if s + 1 < MH:
                        copies(f"q{layer}", s + 1)
                    if s < MH:
                        n, b = layer * MH + s, 4 + s % 2
                        act.wait_ge(a_neg, n + 1)
                        for t in range(ST):
                            col = 2 * s + t
                            ins = act.activation(prob[:, s % 2, t, :], bank[:, b, t * S:(t + 1) * S], ACT.Exp,
                                                 bias=mstat[:, 1, col:col + 1], scale=(D // MH) ** -0.5,
                                                 accum_out=mstat[:, 2, col:col + 1])
                        ins.then_inc(a_exp, 1)
                    if s >= 3:
                        h = s - 3
                        act.wait_ge(a_out, layer * MH + h + 1)
                        act.activation(actT_hi[:, 2 * h:2 * h + 2, :], tiles(2 + h % 2), ACT.Copy).then_inc(a_hi, 1)
                    if 1 <= s <= MH:
                        act.wait_ge(a_turned, layer * MH + s)
                        act.activation(probT[:, (s - 1) % 2], tiles(6 + (s - 1) % 2), ACT.Copy).then_inc(a_probT, 1)

            def feed_forward(layer):
                name = f"gu{layer}"
                u0, v0 = U[(name, 0)], V_OF[(name, 0)]
                a0, d0 = FREED[v0][1] - 1, FREED[v0 + 1][1] - 1
                act.preload_act_table_set("silu_and_others")

                def unit(j, i, per, tile):
                    hi_unit(u0 + 2 + j, i, per)
                    act.wait_ge(w_used, i * 4 + (u0 + j + 1) if per else u0 + j + 1)
                    if j % 2 == 0:
                        act.activation(gate[:, j // 2 % 2], tiles((v0 + j) % 2), ACT.Silu).then_inc(t_out["act"], 1)
                    else:
                        act.wait_ge(t_out["dve"], i * 2 + (d0 + j // 2 + 1) if per else d0 + j // 2 + 1)
                        act.activation(hT_hi[:, tile, :], hval[:, j // 2 % 2], ACT.Copy).then_inc(h_hi, 1)

                with act.Fori(0, 5) as i:
                    for j in range(4):
                        unit(j, i, 4, bass.ds(i * 4 + j // 2 * 2, 2))
                for j in (20, 21):
                    unit(j, 0, 0, slice(FT - 2, FT))
                done[0] = u0 + 24
                m_part(f"down{layer}")

            memory_attention(0)
            m_part("wo0")
            norms(1)
            copy_out("k1", 0)
            turn(3, actT_hi)
            copy_out("k1", 1)
            hi_upto(U[("gu0", 0)] + 1)
            feed_forward(0)
            norms(2)
            copy_out("k1", 2)
            turn(4, actT_hi)
            copy_out("k1", 3)
            copies("mq", 0, 1, 2, 3)
            turn(5, actT_hi)
            copies("v1", 0)
            copies("mk", 0)
            hi_upto(U[MOBA_UNITS[1]] + 1)
            pairs = AH // 2
            for s in range(pairs + BLAG + 2):
                unit = MOBA_UNITS[s + 1] if s + 1 < len(MOBA_UNITS) else ("v1", 1) if s == pairs else None
                if unit:
                    copy_out(*unit)
                    if s < pairs:
                        hi_upto(U[unit] + 2)
                if s < pairs:
                    act.wait_ge(b_neg, s + 1)
                    for t, c0, c1 in ((1, 0, S), (0, S, CAUS)):
                        for a in range(2):
                            h = 2 * s + a
                            ins = act.activation(sc[:, s % 3, a, c0:c1], sc[:, s % 3, a, c0:c1], ACT.Exp,
                                                 bias=bstat[:, 1, t, h:h + 1], accum_out=bstat[:, 2, t, h:h + 1])
                    ins.then_inc(b_exp, 1)
                if s > BLAG + 1:
                    p = s - BLAG - 2
                    act.wait_ge(b_out, p + 1)
                    src = reversed_last(bank[:, 2 + p % 2, 0:S].rearrange("p (t n) -> p t n", n=P))
                    act.activation(oT_hi[:, p, :].rearrange("p (t n) -> p t n", n=P), src, ACT.Copy).then_inc(b_hi, 1)
                if BLAG <= s < pairs + BLAG:
                    p = s - BLAG
                    act.wait_ge(b_turned, p + 1)
                    act.activation(scT[:, p % 2], bank[:, 6:8, 0:CAUS], ACT.Copy).then_inc(b_probT, 1)
                if s == pairs:
                    hi_upto(U[unit] + 2)
            m_part("mo")
            norms(3)
            copy_out("v1", 2)
            turn(6, actT_hi)
            copy_out("v1", 3)
            memory_attention(1)
            m_part("wo1")
            norms(4)
            turn(7, actT_hi)
            hi_upto(U[("gu1", 0)] + 1)
            feed_forward(1)
            norms(5)

        @block.vector
        def _(dve):
            own = Own(dve, dve_step)
            done = [0]

            def lo_unit(u, i=0, per=0):
                dve.wait_ge(w_hi_done, i * 4 + (u + 1) if per else u + 1)
                s = u % SLOTS
                dve.tensor_tensor(lo[:, s, :], raw[:, s, :], hi[:, s, :].bitcast(F32), ALU.subtract).then_inc(w_lo_done, 1)

            def lo_part(u, part):
                assert u == done[0]
                cols = slice(part * UNIT // 2, (part + 1) * UNIT // 2)
                s = u % SLOTS
                if part == 0:
                    dve.wait_ge(w_hi_done, u + 1)
                ins = dve.tensor_tensor(lo[:, s, cols], raw[:, s, cols], hi[:, s, cols].bitcast(F32), ALU.subtract)
                if part:
                    ins.then_inc(w_lo_done, 1)
                    done[0] += 1

            def lo_upto(u):
                while done[0] <= min(u, NUNITS - 1):
                    lo_unit(done[0])
                    done[0] += 1

            def tiles(b):
                return bank[:, b, :].rearrange("p (c n) -> p c n", n=S)

            def inverse_rms(c):
                total, _, r, v, step, result = [stats[:, n, c:c + 1] for n in range(6)]
                dve.wait_ge(sum_ready, c + 1)
                own.mark(dve.tensor_scalar(v, total, -0.5 / D, -0.5 * EPS, ALU.mult, ALU.add))
                own.wait()
                dve.wait_ge(stat_ready, c + 1)
                own.mark(dve.scalar_tensor_tensor(out=step, in0=r, scalar=v, in1=r, op0=ALU.mult, op1=ALU.mult))
                own.wait()
                own.mark(dve.tensor_scalar(result, step, 1.5, r, ALU.add, ALU.mult))
                own.wait()

            def normalise(k, c, t, src, fresh=True):
                if fresh:
                    inverse_rms(c)
                if t == 0:
                    dve.wait_ge(pre_loaded, 16 * (k + 1))
                dve.scalar_tensor_tensor(out=ntmp[:, t, :], in0=src[:, t, :], scalar=stats[:, 5, c:c + 1],
                                         in1=pre_row[:], op0=ALU.mult, op1=ALU.mult).then_inc(u_ready, 1)

            def turn(k, dst_hi, dst_lo):
                for t in range(ST):
                    for half in range(2):
                        dve.wait_ge(turn_hi, 4 * k + 2 * t + half + 1)
                        part = (slice(None), slice(half * 4, half * 4 + 4), slice(t * P, (t + 1) * P))
                        dve.tensor_tensor(dst_lo[part], bank[:, 4 + 2 * t + half, :].rearrange("p (q n) -> p q n", n=P),
                                          dst_hi[part].bitcast(F32), ALU.subtract).then_inc(turn_lo, 1)

            def m_part(name):
                lo_upto(last_unit(name) + 1)

            def update(n):
                for t in range(ST):
                    c = stat_col(n, t, 0)
                    inverse_rms(c)
                    if t == 0:
                        dve.wait_ge(post_loaded, 16 * (n + 1))
                    own.mark(dve.scalar_tensor_tensor(out=ntmp[:, t, :], in0=msum[t], scalar=stats[:, 5, c:c + 1],
                                                      in1=post_row[:], op0=ALU.mult, op1=ALU.mult))
                    own.wait()
                    dve.tensor_tensor(x[:, t, :], x[:, t, :], ntmp[:, t, :], ALU.add).then_inc(x_ready, 1)
                    if units_ahead(n) > last_unit(M_OF_POST[n]) + 2:
                        lo_upto(units_ahead(n) if t else last_unit(M_OF_POST[n]) + 2)
                    if POST_TURN[n] is not None:
                        normalise(POST_TURN[n], stat_col(n, t, 1), t, x)

            def fills(name, *units):
                for i in units:
                    lo_upto(U[(name, i)] + 2)

            dve.memset(par_rows[:], 0.0).then_inc(par_cleared, 1)
            dve.memset(one_col, 1.0)
            dve.memset(eps_col, EPS).then_inc(eps_made, 1)
            own.mark(dve.memset(cumT_hi[:].bitcast(F32), 0.0))
            own.mark(dve.memset(cumT_lo[:].bitcast(F32), 0.0))
            for t in range(ST):
                normalise(0, t, t, x)
            dve.wait_ge(par_loaded, 80)
            dve.wait_ge(const_loaded, 16)
            dve.tensor_copy(id_bf[:], const[:, C_ID:C_ID + P])
            dve.tensor_copy(mask_bf[:], const[:, C_CAUS:C_CAUS + P])
            dve.tensor_copy(id_r[:], const[:, C_ID:C_ID + SSM_HEADS])
            d_rows = slice(D_ROW, D_ROW + XT)
            dve.tensor_copy(par_rows[d_rows, 1, :].rearrange("c (e n) -> c e n", e=2), d_pair[d_rows, :].unsqueeze(2).broadcast_to([XT, 2, HD])).then_inc(consts_made, 1)
            dve.wait_ge(dtw_hi_done, 1)
            dve.tensor_tensor(dtw_lo[:], dtw[:], dtw_hi[:].bitcast(F32), ALU.subtract).then_inc(dtw_lo_done, 1)
            turn(0, actT_hi, actT_lo)
            dve.wait_ge(par_turned, 1)
            dve.tensor_copy(cw[:, 0:TAPS * CT], bank[:, 0, 0:TAPS * CT])
            dve.tensor_copy(cw[:, TAPS * CT:TAPS * CT + CT], bank[:, 0, P:P + CT])
            dve.tensor_copy(gT[:], bank[:, 0, P + G_ROW:P + G_ROW + XT])
            dve.tensor_copy(dT[:], bank[:, 0, P + D_ROW:P + D_ROW + XT]).then_inc(t_out["dve"], 1)
            lo_upto(1)
            dve.wait_ge(dt_turned, 1)
            dve.wait_ge(rows_loaded, 64)
            own.mark(dve.memset(brows[:, S:3 * P], NEG))
            bias_row = dt_row[:, 0:1, :].broadcast_to([P, ST, SSM_HEADS])
            dt_raw = bank[:, 2, 0:ST * SSM_HEADS].rearrange("p (t h) -> p t h", t=ST)
            dve.tensor_tensor(dtc[:, 1], dt_raw, bias_row, ALU.add).then_inc(dt_biased, 1)
            dve.wait_ge(dt_logged, 1)
            own.mark(dve.tensor_scalar(dtc[:, 5], dtc[:, 3], 1.0, None, ALU.add))
            own.wait()
            own.mark(dve.tensor_scalar(dtc[:, 6], dtc[:, 5], 1.0, None, ALU.subtract))
            own.wait()
            own.mark(dve.tensor_tensor(dtc[:, 6], dtc[:, 3], dtc[:, 6], ALU.subtract))
            own.mark(dve.reciprocal(dtc[:, 2], dtc[:, 5]))
            own.wait()
            own.mark(dve.tensor_tensor(dtc[:, 6], dtc[:, 6], dtc[:, 2], ALU.mult))
            own.wait()
            own.mark(dve.tensor_tensor(dtc[:, 6], dtc[:, 6], dtc[:, 4], ALU.add))
            own.wait()
            own.mark(dve.scalar_tensor_tensor(out=dtc[:, 5], in0=dtc[:, 1], scalar=0.0, in1=dtc[:, 6], op0=ALU.max, op1=ALU.add))
            own.wait()
            exp_a = dt_row[:, 1:2, :].broadcast_to([P, ST, SSM_HEADS])
            dve.scalar_tensor_tensor(out=dtc[:, 6], in0=dtc[:, 5], scalar=-1.0, in1=exp_a, op0=ALU.mult, op1=ALU.mult).then_inc(dt_ready, 1)

            with dve.Fori(0, 3) as i:
                n0 = own.n
                per = 8
                for j in range(4):
                    lo_unit(2 + j, i, 4)
                    dve.wait_ge(conv_first, i * 4 + (j + 1))
                    for tap in (2, 1, 0):
                        back = TAPS - 1 - tap
                        if tap < 2:
                            own.wait(i, per)
                        for c in range(2):
                            acc = conv_acc[:, j % 2, c, back:S]
                            ins = dve.scalar_tensor_tensor(out=acc, in0=tiles(j)[:, c, 0:S - back],
                                                           scalar=cw[:, bass.ds(i * 8 + (tap * CT + 2 * j + c), 1)],
                                                           in1=acc, op0=ALU.mult, op1=ALU.add)
                        if tap:
                            own.mark(ins)
                        else:
                            ins.then_inc(t_out["dve"], 1)
                assert own.n - n0 == per
            own.n += 2 * per
            done[0] = 14
            for i in range(DI // TC):
                lo_upto(U[("z", i)] + 2)
                if i == 1:
                    for t in range(ST):
                        normalise(1, 2 + t, t, memV)
                if i == 4:
                    turn(1, memT_hi, memT_lo)
                if i == 5:
                    dve.wait_ge(cum_mm, 1)
                    own.mark(dve.tensor_scalar(dtc[:, 7], bank[:, 2, 0:ST * SSM_HEADS].rearrange("p (t h) -> p t h", t=ST), -1.0, None, ALU.mult))
                    dve.wait_ge(cum_hi, 1)
                    dve.tensor_tensor(cumT_lo[0:SSM_HEADS, :], bank[0:SSM_HEADS, 3, 0:S], cumT_hi[0:SSM_HEADS, :].bitcast(F32), ALU.subtract).then_inc(cum_ready, 1)
            dve.wait_ge(brow_mm, 1)
            dve.tensor_copy(brows[:, 0:S], bank[0:AH, 2, 0:S]).then_inc(brow_ready, 1)

            dve.wait_ge(t_out["act"], FREED[V_OF[("z", 7)]][1])
            for j in range(XT + LAG + 3):
                c = j - LAG
                if j < XT:
                    g = j // GT
                    if j % GT == 0:
                        dve.wait_ge(cb_ready, g + 1)
                    if j >= 3:
                        dve.wait_ge(y_mm, j - 2)
                    for h in (2 * j, 2 * j + 1):
                        dve.wait_ge(decay_ready, h + 1)
                        for t, c0, c1 in ((0, 0, S), (1, S, CAUS)):
                            ins = dve.scalar_tensor_tensor(out=mt[:, h % 6, c0:c1], in0=decay[:, h % 2, c0:c1],
                                                           scalar=dtc[:, 5, t, h:h + 1], in1=cbT[:, g % 2, c0:c1],
                                                           op0=ALU.mult, op1=ALU.mult)
                        ins.then_inc(mt_ready, 1)
                if 0 <= c < XT:
                    dve.wait_ge(y_mm, c + 1)
                    own.mark(dve.scalar_tensor_tensor(out=xbc[:, c, :], in0=xbc[:, c, :], scalar=dT[:, c:c + 1],
                                                      in1=bank[:, 3 + c % 2 * 3, 0:S], op0=ALU.mult, op1=ALU.add))
                    own.wait()
                    dve.tensor_tensor(z[:, c, :], z[:, c, :], xbc[:, c, :], ALU.mult).then_inc(y_ready, 1)
                if c > 1 and c % GT == 1:
                    g = c // GT - 1
                    dve.wait_ge(rs_ready, g + 1)
                    dve.wait_ge(y_ready, GT * (g + 1))
                    for k in range(g * GT, (g + 1) * GT):
                        ins = dve.scalar_tensor_tensor(out=z[:, k, :], in0=z[:, k, :], scalar=gT[:, k:k + 1],
                                                       in1=rs[:, 1, :], op0=ALU.mult, op1=ALU.mult)
                    ins.then_inc(yn_ready, 1)
                if c > 2 and c % GT == 2:
                    g = c // GT - 1
                    group = slice(g * GT, (g + 1) * GT)
                    dve.wait_ge(y_hi_done, g + 1)
                    dve.tensor_tensor(y_lo[:, group, :], z[:, group, :], y_hi[:, group, :].bitcast(F32), ALU.subtract).then_inc(y_lo_done, 1)
                if j - 1 in SSD_SPLITS:
                    lo_part(*SSD_SPLITS[j - 1])
            m_part("w_out")
            update(0)
            turn(2, actT_hi, actT_lo)

            def memory_attention(layer):
                scale = (D // MH) ** -0.5
                fills(f"q{layer}", 0)
                for s in range(MH + 3):
                    if s + 1 < MH:
                        fills(f"q{layer}", s + 1)
                    n = layer * MH + s
                    cols = slice(2 * s, 2 * s + 2)
                    if s < MH:
                        dve.wait_ge(a_mm, n + 1)
                        own.mark(dve.tensor_reduce(mstat[:, 0, cols], tiles(4 + s % 2), AX.X, ALU.max))
                        own.wait()
                        dve.tensor_scalar(mstat[:, 1, cols], mstat[:, 0, cols], -scale, None, ALU.mult).then_inc(a_neg, 1)
                    if s < MH:
                        dve.wait_ge(a_exp, n + 1)
                        own.mark(dve.reciprocal(mstat[:, 3, cols], mstat[:, 2, cols]))
                        own.wait()
                        for t in range(ST):
                            ins = dve.tensor_scalar(prob[:, s % 2, t, :], prob[:, s % 2, t, :], mstat[:, 3, 2 * s + t:2 * s + t + 1], None, ALU.mult)
                        ins.then_inc(a_norm, 1)
                    if s >= 3:
                        h = s - 3
                        dve.wait_ge(a_hi, layer * MH + h + 1)
                        dve.tensor_tensor(actT_lo[:, 2 * h:2 * h + 2, :], tiles(2 + h % 2),
                                          actT_hi[:, 2 * h:2 * h + 2, :].bitcast(F32), ALU.subtract).then_inc(a_lo, 1)

            def feed_forward(layer):
                name = f"gu{layer}"
                u0, v0 = U[(name, 0)], V_OF[(name, 0)]
                a0 = FREED[v0][1] - 1
                h0 = (FT // 2) * layer

                def unit(j, i, per, tile):
                    lo_unit(u0 + 2 + j, i, per)
                    if j % 2:
                        b = j // 2 % 2
                        dve.wait_ge(w_used, i * 4 + (u0 + j + 1) if per else u0 + j + 1)
                        dve.wait_ge(t_out["act"], i * 2 + (a0 + j // 2 + 1) if per else a0 + j // 2 + 1)
                        dve.tensor_tensor(hval[:, b], tiles((v0 + j) % 2), gate[:, b], ALU.mult).then_inc(t_out["dve"], 1)
                        dve.wait_ge(h_hi, i * 2 + (h0 + j // 2 + 1) if per else h0 + j // 2 + 1)
                        dve.tensor_tensor(hT_lo[:, tile, :], hval[:, b], hT_hi[:, tile, :].bitcast(F32), ALU.subtract).then_inc(h_lo, 1)

                with dve.Fori(0, 5) as i:
                    for j in range(4):
                        unit(j, i, 4, bass.ds(i * 4 + j // 2 * 2, 2))
                for j in (20, 21):
                    unit(j, 0, 0, slice(FT - 2, FT))
                done[0] = u0 + 24
                m_part(f"down{layer}")

            memory_attention(0)
            m_part("wo0")
            update(1)
            turn(3, actT_hi, actT_lo)
            lo_upto(U[("gu0", 0)] + 1)
            feed_forward(0)
            update(2)
            turn(4, actT_hi, actT_lo)
            for t in range(ST):
                normalise(5, stat_col(2, t, 1), t, x, fresh=False)
            fills("mq", 0, 1, 2, 3)
            turn(5, actT_hi, actT_lo)
            fills("v1", 0)
            fills("mk", 0)
            lo_upto(U[MOBA_UNITS[1]] + 1)

            pairs = AH // 2
            for s in range(pairs + BLAG + 2):
                if s == 0:
                    dve.wait_ge(bias_loaded, 16 * AH)
                if s < pairs:
                    dve.wait_ge(b_mm, s + 1)
                    if s >= 3:
                        dve.wait_ge(b_turned, s - 2)
                    dve.scalar_tensor_tensor(out=sc[:, s % 3], in0=bank[:, 4:6, 0:CAUS], scalar=HD ** -0.5,
                                             in1=mbias[:, 2 * s:2 * s + 2, :], op0=ALU.mult, op1=ALU.add).then_inc(b_read, 1)
                    dve.wait_ge(b_read, s + 1)
                    heads = slice(2 * s, 2 * s + 2)
                    dve.tensor_reduce(bstat[:, 0, 1, heads], sc[:, s % 3, :, 0:S], AX.X, ALU.max)
                    own.mark(dve.tensor_reduce(bstat[:, 0, 0, heads], sc[:, s % 3, :, S:CAUS], AX.X, ALU.max))
                    own.wait()
                    dve.tensor_scalar(bstat[:, 1, :, heads], bstat[:, 0, :, heads], -1.0, None, ALU.mult).then_inc(b_neg, 1)
                if s + 1 < len(MOBA_UNITS):
                    fills(*MOBA_UNITS[s + 1])
                if s < pairs:
                    p = s
                    heads = slice(2 * p, 2 * p + 2)
                    dve.wait_ge(b_exp, p + 1)
                    own.mark(dve.reciprocal(bstat[:, 3, :, heads], bstat[:, 2, :, heads]))
                    own.wait()
                    for t, c0, c1 in ((1, 0, S), (0, S, CAUS)):
                        for a in range(2):
                            h = 2 * p + a
                            ins = dve.tensor_scalar(sc[:, p % 3, a, c0:c1], sc[:, p % 3, a, c0:c1], bstat[:, 3, t, h:h + 1], None, ALU.mult)
                    ins.then_inc(b_norm, 1)
                if s > BLAG + 1:
                    p = s - BLAG - 2
                    dve.wait_ge(b_hi, p + 1)
                    src = reversed_last(bank[:, 2 + p % 2, 0:S].rearrange("p (t n) -> p t n", n=P))
                    dve.tensor_tensor(oT_lo[:, p, :].rearrange("p (t n) -> p t n", n=P), src,
                                      oT_hi[:, p, :].bitcast(F32).rearrange("p (t n) -> p t n", n=P), ALU.subtract).then_inc(b_lo, 1)
                if s == pairs:
                    fills("v1", 1)
            m_part("mo")
            update(3)
            turn(6, actT_hi, actT_lo)
            memory_attention(1)
            m_part("wo1")
            update(4)
            turn(7, actT_hi, actT_lo)
            lo_upto(U[("gu1", 0)] + 1)
            feed_forward(1)
            update(5)


def shape_constants():
    import numpy as np

    consts = np.zeros((P, C_END), np.float32)
    consts[:, C_ID:C_ID + P] = np.eye(P)
    consts[:, C_TRI:C_TRI + P] = np.triu(np.ones((P, P)))
    consts[:, C_TRI + P:C_TRI + S] = 1.0
    consts[:, C_CAUS:C_CAUS + P] = np.tril(np.full((P, P), NEG), -1)
    exact = BUCKETS // 2
    for i in range(S):
        n = S - 1 - i
        large = exact + int(math.log(max(n, exact) / exact) / math.log(MAX_DIST / exact) * (BUCKETS - exact) + 1e-9)
        consts[n if n < exact else min(large, BUCKETS - 1), C_HOT + i] = 1.0
    return consts


_INS = ["x", "mem", "mix_pre_g", "mix_post_g", "ssm_w_in", "ssm_conv_w", "ssm_conv_b", "ssm_dt_bias", "ssm_a_log",
        "ssm_d", "ssm_norm_g", "ssm_w_out", "kv_norm_g", "w_kv", "moba_w_q", "moba_w_o", "rel_bias", "mem_norm_g",
        "mem_pre_g", "mem_post_g", "mem_w_q", "mem_w_kv", "mem_w_o", "ffn_pre_g", "ffn_post_g", "ffn_w_gu", "ffn_w_down"]


def kernel(**inputs):
    import numpy as _np
    import concourse.bacc as _bacc
    from concourse import mybir as _mybir
    from concourse.bass_utils import run_bass_kernel_spmd as _run

    nc = _bacc.Bacc("TRN2", target_bir_lowering=False, num_devices=1)
    arrays = {f"in_{name}_dram": _np.ascontiguousarray(inputs[name]) for name in _INS}
    arrays["in_consts_dram"] = shape_constants()
    A = {}
    for name in _INS + ["consts"]:
        a = arrays[f"in_{name}_dram"]
        A[name] = nc.dram_tensor(f"in_{name}_dram", a.shape, _mybir.dt.from_np(a.dtype), kind="ExternalInput").ap()
    out = nc.dram_tensor("out_0_dram", (1, S, D), F32, kind="ExternalOutput").ap()
    program(nc, A, out)
    r = _run(nc, [arrays], core_ids=[0])
    return r.results[0]["out_0_dram"]
```
